# Optimizing a Trainium2 kernel written in Bass

```python
import numpy as np
import jax, jax.numpy as jnp
from jax import lax

D_MODEL = 1024
BATCH = 1
SEQ = 512
DEPTH = 1

HEAD_DIM = 64
NSA_HEADS = 8
NSA_KV_GROUPS = 2
NSA_HPG = NSA_HEADS // NSA_KV_GROUPS
CMP_BLOCK = 32
CMP_STRIDE = 16
CMP_HIDDEN = 256
SEL_BLOCK = 64
SEL_TOPK = 16
NSA_WINDOW = 512
Q_BLOCK = 128
FORCE_SCORE = 1e6
DIL_GROUPS = ((128, 1), (512, 4), (2048, 16))
DIL_HPG = 4
DIL_HEADS = DIL_HPG * len(DIL_GROUPS)
DIL_BLOCK = 128
D_FF = -(-8 * D_MODEL // (3 * 256)) * 256
NSA_Q = NSA_HEADS * HEAD_DIM
NSA_KV = 3 * 2 * NSA_KV_GROUPS * HEAD_DIM
NSA_GATE = NSA_HEADS * 3
DIL_QKV = 3 * DIL_HEADS * HEAD_DIM
MERGE_GATE = 2 * D_MODEL
IN_SPLITS = tuple(int(c) for c in np.cumsum([NSA_Q, NSA_KV, NSA_GATE, DIL_QKV]))
D_IN = NSA_Q + NSA_KV + NSA_GATE + DIL_QKV + MERGE_GATE
NSA_OUT = NSA_HEADS * HEAD_DIM
DIL_OUT = DIL_HPG * HEAD_DIM
N_ALIBI = NSA_HEADS + DIL_HEADS
EPS = 1e-6
NEG_INF = -1e30
TINY = 1e-30

kernel_name = "hybrid_nsa_dilated_alibi_trunk"

def rmsnorm(x, g):
    xf = x.astype(jnp.float32)
    y = xf * lax.rsqrt(jnp.mean(xf * xf, axis=-1, keepdims=True) + EPS)
    return (y * g.astype(jnp.float32)).astype(x.dtype)

def alibi_slopes():
    k = jnp.arange(1, N_ALIBI + 1, dtype=jnp.float32)
    s = jnp.exp2(-8.0 * k / N_ALIBI)
    d0 = s[:DIL_HPG]
    d1 = s[DIL_HPG:2 * DIL_HPG]
    nsa = s[2 * DIL_HPG:2 * DIL_HPG + NSA_HEADS]
    d2 = s[2 * DIL_HPG + NSA_HEADS:]
    return nsa, (d0, d1, d2)

def masked_softmax(s, mask):
    s = jnp.where(mask, s, NEG_INF)
    m = jnp.max(s, axis=-1, keepdims=True)
    e = jnp.where(mask, jnp.exp(s - m), 0.0)
    l = jnp.sum(e, axis=-1, keepdims=True)
    lt = jnp.maximum(l, TINY)
    return e / lt, (m + jnp.log(lt))[..., 0]

def compress(kv, pe, w1, w2):
    B, S, G, hd = kv.shape
    n_c = (S - CMP_BLOCK) // CMP_STRIDE + 1
    idx = jnp.arange(n_c)[:, None] * CMP_STRIDE + jnp.arange(CMP_BLOCK)[None, :]
    blk = kv[:, idx] + pe[:, None, :]
    blk = blk.transpose(0, 1, 3, 2, 4).reshape(B, n_c, G, CMP_BLOCK * hd)
    return jax.nn.silu(blk @ w1) @ w2

def nsa_attention(q, kvs, gates, pe_k, pe_v, w_ck1, w_ck2, w_cv1, w_cv2, slopes):
    B, S, H, hd = q.shape
    G, Hg = NSA_KV_GROUPS, NSA_HPG
    k_cmp, v_cmp = kvs[:, :, 0, 0], kvs[:, :, 0, 1]
    k_slc, v_slc = kvs[:, :, 1, 0], kvs[:, :, 1, 1]
    k_win, v_win = kvs[:, :, 2, 0], kvs[:, :, 2, 1]
    kc = compress(k_cmp, pe_k, w_ck1, w_ck2)
    vc = compress(v_cmp, pe_v, w_cv1, w_cv2)
    n_c = kc.shape[1]
    n_s = S // SEL_BLOCK
    n_top = min(SEL_TOPK, n_s)
    c_start = jnp.arange(n_c) * CMP_STRIDE
    pos_c = (c_start + CMP_BLOCK - 1).astype(jnp.float32)
    s_start = jnp.arange(n_s) * SEL_BLOCK
    overlap = jnp.clip(jnp.minimum(c_start[:, None] + CMP_BLOCK, s_start[None, :] + SEL_BLOCK)
                       - jnp.maximum(c_start[:, None], s_start[None, :]), 0).astype(jnp.float32) / CMP_BLOCK
    kb = k_slc.reshape(B, n_s, SEL_BLOCK, G, hd).transpose(0, 3, 1, 2, 4)
    vb = v_slc.reshape(B, n_s, SEL_BLOCK, G, hd).transpose(0, 3, 1, 2, 4)
    pad_w = ((0, 0), (NSA_WINDOW, 0), (0, 0), (0, 0))
    kw = jnp.pad(k_win, pad_w)
    vw = jnp.pad(v_win, pad_w)
    qs = (q * (hd ** -0.5)).reshape(B, S, G, Hg, hd)
    gs = gates.reshape(B, S, G, Hg, 3)
    m = slopes.reshape(G, Hg)[:, :, None, None]
    bi = jnp.arange(B)[:, None, None, None]
    gi = jnp.arange(G)[None, :, None, None]
    j = jnp.arange(n_s)

    def block(i):
        s0 = i * Q_BLOCK
        qb = lax.dynamic_slice_in_dim(qs, s0, Q_BLOCK, axis=1)
        gb = lax.dynamic_slice_in_dim(gs, s0, Q_BLOCK, axis=1)
        t = s0 + jnp.arange(Q_BLOCK)
        tf = t.astype(jnp.float32)
        sc = jnp.einsum('bqghd,bngd->bghqn', qb, kc).astype(jnp.float32)
        dc = tf[:, None] - pos_c[None, :]
        pc, _ = masked_softmax(sc - m * dc, dc >= 0)
        o_c = jnp.einsum('bghqn,bngd->bqghd', pc, vc)
        imp = jnp.einsum('bghqn,nj->bgqj', pc, overlap)
        jt = t // SEL_BLOCK
        valid = j[None, :] <= jt[:, None]
        forced = (j[None, :] == 0) | (j[None, :] == jt[:, None]) | (j[None, :] == jt[:, None] - 1)
        score = jnp.where(forced, FORCE_SCORE, jnp.where(valid, imp, -1.0))
        top, idx = lax.top_k(score, n_top)
        ks = kb[bi, gi, idx]
        vs = vb[bi, gi, idx]
        pos_s = idx[..., None] * SEL_BLOCK + jnp.arange(SEL_BLOCK)
        ds = (t[:, None, None] - pos_s).astype(jnp.float32)
        mask_s = ((top >= 0)[..., None] & (ds >= 0)).reshape(B, G, 1, Q_BLOCK, n_top * SEL_BLOCK)
        ss = jnp.einsum('bqghd,bgqnld->bghqnl', qb, ks).astype(jnp.float32)
        ss = ss.reshape(B, G, Hg, Q_BLOCK, n_top * SEL_BLOCK)
        ps, _ = masked_softmax(ss - m[None] * ds.reshape(B, G, 1, Q_BLOCK, n_top * SEL_BLOCK), mask_s)
        o_s = jnp.einsum('bghqk,bgqkd->bqghd', ps, vs.reshape(B, G, Q_BLOCK, n_top * SEL_BLOCK, hd))
        kwb = lax.dynamic_slice_in_dim(kw, s0, Q_BLOCK + NSA_WINDOW, axis=1)
        vwb = lax.dynamic_slice_in_dim(vw, s0, Q_BLOCK + NSA_WINDOW, axis=1)
        pos_w = s0 - NSA_WINDOW + jnp.arange(Q_BLOCK + NSA_WINDOW)
        dw = t[:, None] - pos_w[None, :]
        mask_w = (dw >= 0) & (dw < NSA_WINDOW) & (pos_w[None, :] >= 0)
        sw = jnp.einsum('bqghd,bkgd->bghqk', qb, kwb).astype(jnp.float32)
        pw, _ = masked_softmax(sw - m * dw.astype(jnp.float32), mask_w)
        o_w = jnp.einsum('bghqk,bkgd->bqghd', pw, vwb)
        o = gb[..., 0:1] * o_c + gb[..., 1:2] * o_s + gb[..., 2:3] * o_w
        return o.reshape(B, Q_BLOCK, H * hd)

    out = lax.map(block, jnp.arange(S // Q_BLOCK))
    return out.transpose(1, 0, 2, 3).reshape(B, S, H * hd)

def dilated_group(q, k, v, window, dil, slopes):
    B, S, Hg, hd = q.shape
    L = S // dil
    steps = window // dil
    c = DIL_BLOCK
    nb = -(-L // c)
    Lp = nb * c

    def sub(a):
        a = a.reshape(B, L, dil, Hg, hd).transpose(0, 2, 3, 1, 4)
        return jnp.pad(a, ((0, 0), (0, 0), (0, 0), (0, Lp - L), (0, 0)))

    def band(a):
        ap = jnp.pad(sub(a), ((0, 0), (0, 0), (0, 0), (c, 0), (0, 0)))
        prev = ap[:, :, :, :Lp].reshape(B, dil, Hg, nb, c, hd)
        cur = ap[:, :, :, c:].reshape(B, dil, Hg, nb, c, hd)
        return jnp.concatenate([prev, cur], axis=4)

    qs = (sub(q) * (hd ** -0.5)).reshape(B, dil, Hg, nb, c, hd)
    kband, vband = band(k), band(v)
    s = jnp.einsum('brhnqd,brhnkd->brhnqk', qs, kband).astype(jnp.float32)
    qi = jnp.arange(c)
    ki = jnp.arange(2 * c)
    delta = qi[:, None] + c - ki[None, :]
    k_abs = jnp.arange(nb)[:, None] * c - c + ki[None, :]
    mask = (delta >= 0)[None] & (delta <= steps)[None] & (k_abs[:, None, :] >= 0)
    bias = slopes[:, None, None, None] * (delta * dil).astype(jnp.float32)[None, None]
    p, lse = masked_softmax(s - bias, mask)
    o = jnp.einsum('brhnqk,brhnkd->brhnqd', p, vband).reshape(B, dil, Hg, Lp, hd)[:, :, :, :L]
    o = o.transpose(0, 3, 1, 2, 4).reshape(B, S, Hg, hd)
    lse = lse.reshape(B, dil, Hg, Lp)[..., :L].transpose(0, 3, 1, 2).reshape(B, S, Hg)
    return o, lse

def setup_inputs(seed: int = 0) -> dict:
    key = jax.random.key(seed)
    ks = jax.random.split(key, 16)

    def nrm(k, shape, fan):
        return jax.random.normal(k, shape, jnp.float32) * (fan ** -0.5)

    def gain(k, shape):
        return 1.0 + 0.01 * jax.random.normal(k, shape, jnp.float32)

    return {
        "x": jax.random.normal(ks[0], (BATCH, SEQ, D_MODEL), jnp.float32),
        "norm_mix": gain(ks[1], (DEPTH, D_MODEL)),
        "w_in": nrm(ks[2], (DEPTH, D_MODEL, D_IN), D_MODEL),
        "pe_k": 0.1 * jax.random.normal(ks[3], (DEPTH, CMP_BLOCK, HEAD_DIM), jnp.float32),
        "pe_v": 0.1 * jax.random.normal(ks[4], (DEPTH, CMP_BLOCK, HEAD_DIM), jnp.float32),
        "w_ck1": nrm(ks[5], (DEPTH, CMP_BLOCK * HEAD_DIM, CMP_HIDDEN), CMP_BLOCK * HEAD_DIM),
        "w_ck2": nrm(ks[6], (DEPTH, CMP_HIDDEN, HEAD_DIM), CMP_HIDDEN),
        "w_cv1": nrm(ks[7], (DEPTH, CMP_BLOCK * HEAD_DIM, CMP_HIDDEN), CMP_BLOCK * HEAD_DIM),
        "w_cv2": nrm(ks[8], (DEPTH, CMP_HIDDEN, HEAD_DIM), CMP_HIDDEN),
        "w_up_nsa": nrm(ks[9], (DEPTH, NSA_OUT, D_MODEL), NSA_OUT),
        "w_up_dil": nrm(ks[10], (DEPTH, DIL_OUT, D_MODEL), DIL_OUT),
        "w_out": nrm(ks[11], (DEPTH, D_MODEL, D_MODEL), D_MODEL),
        "norm_ffn": gain(ks[12], (DEPTH, D_MODEL)),
        "w_ffn_in": nrm(ks[13], (DEPTH, D_MODEL, 2 * D_FF), D_MODEL),
        "w_ffn_out": nrm(ks[14], (DEPTH, D_FF, D_MODEL), D_FF),
        "norm_final": gain(ks[15], (D_MODEL,)),
    }

def reference(x, norm_mix, w_in, pe_k, pe_v, w_ck1, w_ck2, w_cv1, w_cv2, w_up_nsa, w_up_dil,
              w_out, norm_ffn, w_ffn_in, w_ffn_out, norm_final):
    B, S, D = x.shape
    slopes_nsa, slopes_dil = alibi_slopes()
    for l in range(DEPTH):
        h = rmsnorm(x, norm_mix[l])
        proj = h @ w_in[l]
        q_a, kv_a, g_a, qkv_b, g_m = jnp.split(proj, IN_SPLITS, axis=-1)
        q_a = q_a.reshape(B, S, NSA_HEADS, HEAD_DIM)
        kv_a = kv_a.reshape(B, S, 3, 2, NSA_KV_GROUPS, HEAD_DIM)
        g_a = jax.nn.sigmoid(g_a).reshape(B, S, NSA_HEADS, 3)
        y_a = nsa_attention(q_a, kv_a, g_a, pe_k[l], pe_v[l], w_ck1[l], w_ck2[l],
                            w_cv1[l], w_cv2[l], slopes_nsa)
        qkv_b = qkv_b.reshape(B, S, 3, len(DIL_GROUPS), DIL_HPG, HEAD_DIM)
        outs, lses = [], []
        for gidx, (window, dil) in enumerate(DIL_GROUPS):
            o_g, lse_g = dilated_group(qkv_b[:, :, 0, gidx], qkv_b[:, :, 1, gidx],
                                       qkv_b[:, :, 2, gidx], window, dil, slopes_dil[gidx])
            outs.append(o_g)
            lses.append(lse_g)
        wts = jax.nn.softmax(jnp.stack(lses, axis=-1), axis=-1)
        y_b = jnp.sum(jnp.stack(outs, axis=-1) * wts[..., None, :], axis=-1).reshape(B, S, DIL_OUT)
        gate_a, gate_b = jnp.split(jax.nn.sigmoid(g_m), 2, axis=-1)
        merged = gate_a * (y_a @ w_up_nsa[l]) + gate_b * (y_b @ w_up_dil[l])
        x = x + (merged @ w_out[l]).astype(x.dtype)
        h = rmsnorm(x, norm_ffn[l])
        gt, up = jnp.split(h @ w_ffn_in[l], 2, axis=-1)
        x = x + ((jax.nn.silu(gt) * up) @ w_ffn_out[l]).astype(x.dtype)
    return rmsnorm(x, norm_final)


_drawn_inputs = setup_inputs


def setup_inputs(seed=0):
    import zlib

    import numpy as np

    out = dict(_drawn_inputs(seed))
    spreads = {}
    factors = {'norm_mix': 8.0, 'pe_k': 8.0, 'pe_v': 10.514, 'norm_ffn': 33.077, 'norm_final': 32.717}
    for name, (base, spread) in spreads.items():
        noise = np.random.default_rng([zlib.crc32(name.encode()), seed]).standard_normal(out[name].shape)
        drawn = base * np.exp(spread * noise) if base else spread * noise
        out[name] = __import__('jax').numpy.asarray(drawn.astype(out[name].dtype))
    for name, factor in factors.items():
        out[name] = (out[name] * factor).astype(out[name].dtype)
    return out
```

```python
from contextlib import ExitStack

import concourse.bass as bass
from concourse import mybir

F32 = mybir.dt.float32
F32R = mybir.dt.float32r
I32 = mybir.dt.int32
ALU = mybir.AluOpType
ACT = mybir.ActivationFunctionType
AX = mybir.AxisListType

P = 128
D = 1024
S = 512
KC = D // P
TT = S // P
HD = 64
NH = 8
NG = 3
DIL = (1, 4, 16)
FF = 2816
FT = FF // P
CMP = 32
PP = 16
CH = 256
EPS = 1e-6
NEG = -1e30
TINY = 1e-30
QSCALE = HD ** -0.5

SLOPE = [2.0 ** (-8.0 * k / 20) for k in range(1, 21)]
SLOPE_DIL = [SLOPE[0:4], SLOPE[4:8], SLOPE[16:20]]
SLOPE_NSA = SLOPE[8:16]

C_Q, C_KC, C_KS, C_VS, C_KW, C_VW = 0, 512, 768, 896, 1024, 1152
C_QB, C_GM = 1304, 3608
VA_N = 280

U_CMP, U_QB, U_KB, U_VB, U_QA, U_KA, U_VA, U_GM, U_UP, U_WO, U_IN, U_OUT = 0, 1, 4, 7, 10, 12, 13, 14, 22, 26, 30, 52
N_UNITS = U_OUT + FT // 2
SLOT = KC * VA_N

TILES = [(u, a) for u in range(U_UP) for a in range(4 if u in (7, 8, 9, 13) else 2)]
FIRST_TILE = {u: TILES.index((u, 0)) for u in range(U_UP)}
LAST_TILE = {u: max(n for n, t in enumerate(TILES) if t[0] == u) for u in range(U_UP)}

Q_OFF = [0, 128, 384, 768]
S_PLACE = [(1, 384), (2, 0), (1, 0), (0, 0)]
K_OFF = [0, 512, 1024, 896]
K_PLACE = [(3, 0), (4, 0), (5, 0), (4, 384)]
B_OFF = [0, 128, 384, 640]
B_PLACE = [(1, 256), (0, 0), (0, 256), (1, 0)]


def schedule():
    jobs = [("tile", n) for n in range(FIRST_TILE[2])]
    jobs.append(("compress", 0))
    jobs += [("tile", n) for n in range(FIRST_TILE[2], FIRST_TILE[U_QA])]
    tile = iter(range(FIRST_TILE[U_QA], len(TILES)))
    for m in range(6):
        jobs += [("dil_scores", m), ("tile", next(tile))]
    jobs.append(("dil_merge", 0))
    jobs += [("tile", next(tile)) for _ in range(4)]
    for m in range(6):
        jobs += [("dil_turn", m), ("dil_scores", 6 + m), ("dil_out", m)]
    jobs += [("cmp_scores", 0), ("dil_merge", 1), ("tile", next(tile)), ("tile", next(tile)), ("cmp_turn", 0)]
    for m in range(6, 12):
        jobs += [("dil_turn", m)]
        if m > 6:
            jobs += [("dil_out", m - 1)]
    jobs += [("dil_out", 11), ("nsa_bias", 0)]
    for n in range(4 * 4):
        jobs.append(("scores", n))
        if n:
            jobs.append(("turn", n - 1))
        if n not in (7, 15):
            jobs.append(("tile", next(tile)))
        if n:
            jobs.append(("out", n - 1))
    jobs += [("turn", 15), ("out", 15)]
    return jobs


SCHEDULE = schedule()
NSA_FROM = SCHEDULE.index(("nsa_bias", 0))
TILE_BANK = {}
for _at, (_job, _n) in enumerate(SCHEDULE):
    if _job == "tile":
        TILE_BANK[_n] = 4 + _n if _n < 2 else 7 if _at > NSA_FROM else 6 + _n % 2


def unit_parts(u):
    if u == U_VA:
        return 2, KC * VA_N
    if U_QA <= u < U_KA:
        return 4, KC * 256
    if U_UP <= u < U_WO:
        return 3, 6 * 256
    return 2, KC * 256


def raw_count(u):
    return 16 * sum(unit_parts(v)[0] for v in range(u % 2, u + 1, 2))


def trunk(nc, x, norm_mix, w_in, pe_k, pe_v, w_ck1, w_ck2, w_cv1, w_cv2, w_up_nsa, w_up_dil,
          w_out, norm_ffn, w_ffn_in, w_ffn_out, norm_final, out, scratch):
    with ExitStack() as ctx:
        def sem(name):
            return ctx.enter_context(nc.semaphore(name))

        def at(name, shape, offset, dt=F32):
            return nc.alloc_sbuf_tensor_at(name, [P, *shape], dt, offset=offset)

        A = BASE
        E = A + 32768
        Fo = E + 26624
        B = Fo + 10240
        C = B + 6 * 4 * SLOT
        Dd = C + 16384
        G = Dd + 36864
        H = G + 4 * 4400
        nhi, nlo = (at(f"n_{k}", [KC, S], A + o, F32R) for k, o in (("hi", 0), ("lo", 16384)))
        raw = [at(f"w_raw{i}", [SLOT], B + 4 * SLOT * i) for i in range(2)]
        whi = [at(f"w_hi{i}", [SLOT], B + 4 * SLOT * (2 + i), F32R) for i in range(2)]
        wlo = [at(f"w_lo{i}", [SLOT], B + 4 * SLOT * (4 + i), F32R) for i in range(2)]
        qa = at("qa", [4, S], C)
        ka = at("ka", [2, S], C + 8192)
        va = at("va", [TT, 256], C + 12288)
        qb = at("qb", [6, S], Dd)
        kb = at("kb", [6, S], Dd + 12288)
        vb = at("vb", [NG, TT, 256], Dd + 24576)
        gm = at("gm", [16, S], Dd)
        wck = [at("wck_k", [PP, CH], C), at("wck_v", [PP, CH], Dd + 12288)]
        xs = at("xs", [TT, D], E)
        xn = at("xn", [2, D], E + 16384)
        blk = [at(f"blk_{k}", [PP, 2, CMP], E + 4096 * i) for i, k in enumerate("kv")]
        dp = at("dil_p", [2, 1920], E)
        dbias = at("dil_bias", [4, 512], E + 15360)
        nbias = at("nsa_bias", [NH, S], E)
        sp = at("probs", [2, 1280], E + 16384)
        cbias = at("cmp_bias", [TT, NH, CMP], E + 20480)
        yhi, ylo = (at(f"y_{k}", [6, S], E + o, F32R) for k, o in (("hi", 0), ("lo", 12288)))
        pt = at("probs_t", [2, 1280], Fo)
        ident = at("ident", [P], G)
        dist = at("dist", [S], G + 512, I32)
        cmask = at("cmask", [S], G + 2560)
        mask0 = at("mask0", [256], G + 4608)
        mask2 = at("mask2", [P], G + 5632)
        distc = at("distc", [TT, CMP], G + 6144, I32)
        maskc = at("maskc", [TT, CMP], G + 6656)
        pc_t = at("pc_t", [2, S], G + 7168)
        hs = at("hs", [4, 2 * CMP], G + 11264)
        kc = at("kc", [2 * CMP], G + 12288)
        vc = at("vc", [2, HD], G + 12544)
        w2k = at("w2k", [2, 2, HD], G + 13056)
        w2v = at("w2v", [2, HD], G + 14080)
        crows = at("crows", [P], G + 14592)
        cvec = at("cvec", [48], G + 15104)
        gate = at("gate", [TT, NH * 3], G + 15296)
        st = at("st", [4, 8], G + 15680)
        ust = at("ust", [2, 4, TT], G + 15808)
        cst = at("cst", [2, 32], G + 15936)
        dm = at("dm", [NG, TT, 4], G + 16192)
        dneg = at("dneg", [2, TT], G + 16384)
        tok = at("tok", [TT, 2, 4], G + 16416)
        dmx = at("dmx", [3, TT, 2], G + 16544)
        de = at("de", [NG, TT, 2], G + 16640)
        dz = at("dz", [NG, TT, 2], G + 16736)
        dw = at("dw", [NG, TT, 2], G + 16832)
        dwl = at("dwl", [2, TT, 2], G + 16928)
        umx = at("umx", [2, TT], G + 16992)
        ya = at("ya", [4, S], H)
        yb = at("yb", [2, S], H + 8192)
        sc = at("cmp_p", [TT, NH, CMP], H)
        th = at("tanh_h", [4 * 2 * CMP], H + 4096)
        mhi, mlo = nhi, nlo
        x2 = at("x2", [TT, D], C)
        hhi, hlo = (at(f"h_{k}", [KC, S], Dd + o, F32R) for k, o in (("hi", 0), ("lo", 16384)))
        hn = at("hn", [2, D], E)
        mt = at("merge_tmp", [2, 3, S], Fo - 2048)
        actt = at("act_t", [FT, S], A)
        ahi, alo = (at(f"a_{k}", [2, 2, S], A + 45056 + o, F32R) for k, o in (("hi", 0), ("lo", 8192)))
        tg = at("tanh_g", [2, S], A + 61440)
        tm = at("gate_mul", [2, S], A + 65536)
        gfin = at("gfin", [D], G + 512)
        sq = at("square", [D], H)
        fin = at("fin", [2, D], Dd)

        ps = [ctx.enter_context(nc.psum_tensor(f"bank{i}", [P, 512], F32)) for i in range(8)]

        x_in = [sem(f"x_in{i}") for i in range(TT)]
        rows_in, w2_in, gfin_in, x2_in = sem("rows_in"), sem("w2_in"), sem("gfin_in"), sem("x2_in")
        wck_in = [sem("wck_k_in"), sem("wck_v_in")]
        raw_full = [sem("raw_full0"), sem("raw_full1")]
        hi_done, lo_done, w_used = sem("hi_done"), sem("lo_done"), sem("w_used")
        pool_step, consts_ready = sem("pool_step"), sem("consts_ready")
        dve_step, act_step = sem("dve_step"), sem("act_step")
        rows_turned, cvec_ready = sem("rows_turned"), sem("cvec_ready")
        ss_ready, n_scaled, n_turned, n_hi, n_lo = (sem(k) for k in ("ss_ready", "n_scaled", "n_turned", "n_hi", "n_lo"))
        tile_ready, tile_evac = sem("tile_ready"), sem("tile_evac")
        cmp_tile_ready, blk_ready, h_ready, h_tanh, hs_ready = (
            sem(k) for k in ("cmp_tile_ready", "blk_ready", "h_ready", "h_tanh", "hs_ready"))
        kv_ready, kv_evac = sem("kv_ready"), sem("kv_evac")
        ds_ready, ds_max, ds_exp, dstat_out, dstat_in, de_sub, de_exp, dw_ready, dw_out, dw_in = (
            sem(k) for k in ("ds_ready", "ds_max", "ds_exp", "dstat_out", "dstat_in", "de_sub", "de_exp",
                             "dw_ready", "dw_out", "dw_in"))
        dp_ready, dt_ready, dt_evac_act, dt_evac_dve, do_ready, do_evac = (
            sem(k) for k in ("dp_ready", "dt_ready", "dt_evac_act", "dt_evac_dve", "do_ready", "do_evac"))
        cs_ready, cs_added, cs_sub, cs_exp, cp_ready, ct_ready, ct_evac = (
            sem(k) for k in ("cs_ready", "cs_added", "cs_sub", "cs_exp", "cp_ready", "ct_ready", "ct_evac"))
        gate_tanh, gate_ready = sem("gate_tanh"), sem("gate_ready")
        s_ready, s_max, s_exp, p_ready, t_ready, t_evac_act, t_evac_dve, o_ready, y_evac = (
            sem(k) for k in ("s_ready", "s_max", "s_exp", "p_ready", "t_ready", "t_evac_act", "t_evac_dve",
                             "o_ready", "y_evac"))
        y_hi, y_lo = sem("y_hi"), sem("y_lo")
        ab_ready, m_sum, m_hi, m_lo = (sem(k) for k in ("ab_ready", "m_sum", "m_hi", "m_lo"))
        wo_ready, x2_sum, x2_ss, h_scaled, h_turned, h_hi, h_lo = (
            sem(k) for k in ("wo_ready", "x2_sum", "x2_ss", "h_scaled", "h_turned", "h_hi", "h_lo"))
        gu_ready, gu_tanh, gt_mul, gu_free = (sem(k) for k in ("gu_ready", "gu_tanh", "gt_mul", "gu_free"))
        a_hi, a_lo, fo_ready, x3_sum, x3_ss, fin_ready = (
            sem(k) for k in ("a_hi", "a_lo", "fo_ready", "x3_sum", "x3_ss", "fin_ready"))
        out_done = [sem("out_done0"), sem("out_done1")]

        def slot_view(ring, u, k, n):
            return ring[u % 2][:, 0:k * n].rearrange("p (k n) -> p k n", k=k)

        def unit_used(u):
            if u == U_CMP:
                return cmp_tile_ready, 2
            if u < U_UP:
                return tile_ready, LAST_TILE[u] - 1
            if u < U_WO:
                return ab_ready, 2 * (u - U_UP) + 2
            if u < U_IN - 1:
                return w_used, u - U_WO + 1
            return wo_ready, TT

        block = ctx.enter_context(nc.Block())

        @block.sync
        def _(sp_):
            w_in_v = w_in[0].rearrange("(k p) n -> p k n", p=P)

            def load(u):
                if u >= 2:
                    sp_.wait_ge(lo_done, u - 1)
                full = raw_full[u % 2]
                if u < U_UP:
                    dst = slot_view(raw, u, KC, VA_N if u == U_VA else 256)
                    if U_QA <= u < U_KA:
                        cuts = [(128 * h + HD * t, 128 * h + HD * t + HD, C_Q + 256 * t + 128 * (u - U_QA) + HD * h)
                                for h in range(2) for t in range(2)]
                    elif u == U_KA:
                        cuts = [(0, 128, C_KS), (128, 256, C_KW)]
                    elif u == U_VA:
                        cuts = [(0, 128, C_VS), (128, VA_N, C_VW)]
                    else:
                        c = C_KC if u == U_CMP else C_QB + 256 * (u - U_QB) if u < U_QA else C_GM + 256 * (u - U_GM)
                        for k in (0, 4):
                            sp_.dma_start(dst[:, k:k + 4, :], w_in_v[:, k:k + 4, c:c + 256]).then_inc(full, 16)
                        return
                    for a, b, c in cuts:
                        sp_.dma_start(dst[:, :, a:b], w_in_v[:, :, c:c + b - a]).then_inc(full, 16)
                elif u < U_WO:
                    cols = slice(256 * (u - U_UP), 256 * (u - U_UP) + 256)
                    dst = slot_view(raw, u, 6, 256)
                    for t in range(2):
                        src = w_up_nsa[0, 256 * t:256 * t + 256, cols].rearrange("(j d) n -> d j n", d=HD)
                        sp_.dma_start(dst[HD * t:HD * t + HD, 0:4, :], src).then_inc(full, 16)
                    src = w_up_dil[0, :, cols].rearrange("(t p) n -> p t n", p=P)
                    sp_.dma_start(dst[:, 4:6, :], src).then_inc(full, 16)
                else:
                    dst = slot_view(raw, u, 2, D)
                    for k in range(2):
                        r = 256 * (u - U_WO) + P * k if u < U_IN else 256 * (u - U_OUT) + P * k
                        w = w_out if u < U_IN else w_ffn_out
                        sp_.dma_start(dst[:, k, :], w[0, r:r + P, :]).then_inc(full, 16)

            for t in range(TT):
                sp_.dma_start(xs[:, t, :], x[0, P * t:P * t + P, :]).then_inc(x_in[t], 16)
            for row, src in ((0, norm_mix[0]), (8, norm_ffn[0])):
                sp_.dma_start(crows[row:row + 8, :], src.rearrange("(a b) -> a b", b=P)).then_inc(rows_in, 16)
            for row, src in ((16, pe_k), (32, pe_v)):
                sp_.dma_start(crows[row:row + PP, :],
                              src[0].rearrange("(a two) d -> a (two d)", two=2)).then_inc(rows_in, 16)
            load(0)
            load(1)
            for kv, w in enumerate((w_ck1, w_cv1)):
                sp_.dma_start(wck[kv][:], w[0].rearrange("(a p) n -> p a n", p=P)).then_inc(wck_in[kv], 16)
            for r in range(2):
                sp_.dma_start(w2k[:, :, r, :], w_ck2[0].rearrange("(m p) d -> p m d", p=P)).then_inc(w2_in, 16)
            sp_.dma_start(w2v[:], w_cv2[0].rearrange("(m p) d -> p m d", p=P)).then_inc(w2_in, 16)

            def dil_merge(half):
                sp_.wait_ge(ds_exp, 6 * half + 6)
                for g in (1, 2):
                    d = scratch[half][g - 1]
                    sp_.dma_start(d.rearrange("(p r) e -> p r e", r=4), dm[:, g, :, :]).then_inc(dstat_out, 16)
                sp_.wait_ge(dstat_out, 32 * half + 32)
                for g in (1, 2):
                    sp_.dma_start(tok[:, :, g - 1, :],
                                  scratch[half][g - 1].rearrange("(i p) e -> p i e", p=P)).then_inc(dstat_in, 16)
                sp_.wait_ge(dw_ready, half + 1)
                for g in (1, 2):
                    sp_.dma_start(scratch[half][g + 1].rearrange("(i p) e -> p i e", p=P),
                                  dw[:, g, :, :]).then_inc(dw_out, 16)
                sp_.wait_ge(dw_out, 32 * half + 32)
                for g in (1, 2):
                    sp_.dma_start(dwl[:, g - 1, :, :],
                                  scratch[half][g + 1].rearrange("(p r) e -> p r e", r=4)).then_inc(dw_in, 16)

            for job, n in SCHEDULE:
                if job == "tile" and TILES[n][1] == 0:
                    load(TILES[n][0] + 2)
                elif job == "dil_merge":
                    dil_merge(n)
            sp_.wait_ge(o_ready, 16)
            for t in range(TT):
                sp_.dma_start(x2[:, t, :], x[0, P * t:P * t + P, :]).then_inc(x2_in, 16)
            sp_.dma_start(gfin[:], norm_final.partition_broadcast(P)).then_inc(gfin_in, 16)
            for u in range(U_UP + 2, U_IN):
                load(u)
            gt_v = w_ffn_in[0].rearrange("(k p) n -> p k n", p=P)

            def load_in(s, j, count):
                sp_.wait_ge(lo_done, count)
                dst = slot_view(raw, s, KC, 256)
                for half in range(2):
                    sp_.dma_start(dst[:, :, P * half:P * half + P],
                                  gt_v[:, :, bass.ds(j * P + FF * half, P)]).then_inc(raw_full[s], 16)

            with sp_.Fori(0, FT // 2) as i:
                for s in range(2):
                    load_in(s, i * 2 + s, i * 2 + (U_IN + s - 1))
            wo_v = w_ffn_out[0].rearrange("(u k p) n -> u p k n", p=P, k=2)
            with sp_.Fori(0, FT // 4) as i:
                for s in range(2):
                    sp_.wait_ge(lo_done, i * 2 + (U_OUT + s - 1))
                    dst = slot_view(raw, s, 2, D)
                    for k in range(2):
                        sp_.dma_start(dst[:, k, :], w_ffn_out[0, bass.ds((i * 2 + s) * 256 + P * k, P), :]
                                      ).then_inc(raw_full[s], 16)
            load(N_UNITS - 1)
            for t in range(TT):
                sp_.wait_ge(fin_ready, t + 1)
                sp_.dma_start(out[0, P * t:P * t + P, :], fin[:, t % 2, :]).then_inc(out_done[t % 2], 16)
            for s in range(2):
                sp_.wait_ge(out_done[s], 16 * TT // 2)

        @block.gpsimd
        def _(pool):
            steps = [0]

            def link(ins):
                steps[0] += 1
                ins.then_inc(pool_step, 1)
                pool.wait_ge(pool_step, steps[0])

            link(pool.memset(ident[:], 0.0))
            pool.affine_select(out=ident[:], in_=ident[:], compare_op=ALU.not_equal, fill=1.0, base=0,
                               pattern=[[-1, P]], channel_multiplier=1).then_inc(consts_ready, 1)
            pool.iota(dist[:], [[-1, S]], base=384, channel_multiplier=1).then_inc(consts_ready, 1)
            link(pool.memset(cmask[:], 0.0))
            link(pool.affine_select(out=cmask[:], in_=cmask[:], compare_op=ALU.is_ge, fill=NEG, base=384,
                                    pattern=[[-1, S]], channel_multiplier=1))
            pool.affine_select(out=mask0[:], in_=cmask[:, 256:512], compare_op=ALU.is_ge, fill=NEG, base=0,
                               pattern=[[1, 256]], channel_multiplier=-1).then_inc(consts_ready, 1)
            pool.iota(distc[:], [[P, TT], [-16, CMP]], base=-31, channel_multiplier=1).then_inc(consts_ready, 1)
            link(pool.memset(maskc[:], 0.0))
            pool.affine_select(out=maskc[:], in_=maskc[:], compare_op=ALU.is_ge, fill=NEG, base=-31,
                               pattern=[[P, TT], [-16, CMP]], channel_multiplier=1).then_inc(consts_ready, 1)

        @block.scalar
        def _(act):
            def split_hi(u):
                act.wait_ge(raw_full[u % 2], raw_count(u))
                if u >= 2:
                    act.wait_ge(*unit_used(u - 2))
                n = unit_parts(u)[1]
                act.copy(whi[u % 2][:, 0:n], raw[u % 2][:, 0:n]).then_inc(hi_done, 1)

            for t in range(TT):
                act.wait_ge(x_in[t], 16)
                if t >= 2:
                    act.wait_ge(ss_ready, t - 1)
                act.activation(xn[:, t % 2, :], xs[:, t, :], ACT.Square,
                               accum_out=st[:, 0, t:t + 1]).then_inc(ss_ready, 1)
            split_hi(0)
            act.wait_ge(cvec_ready, 1)
            for t in range(TT):
                for half in range(2):
                    act.wait_ge(n_turned, 2 * t + half + 1)
                    for k in range(4 * half, 4 * half + 4):
                        ins = act.activation(nhi[:, k, P * t:P * t + P], ps[(2 * t + half) % 4][:, P * (k % 4):P * (k % 4) + P],
                                             ACT.Copy, scale=cvec[:, k:k + 1])
                    ins.then_inc(n_hi, 1)

            def tile(n):
                u, a = TILES[n]
                if a == 0:
                    split_hi(u + 1)
                if u == U_CMP:
                    return
                b = ps[TILE_BANK[n]]
                act.wait_ge(tile_ready, n - 1)
                if u < U_VB:
                    g = (u - U_QB) % 3
                    dst = (qb if u < U_KB else kb)[:, 2 * g + a, :]
                    if g:
                        dst = dst.rearrange("p (r t) -> p r t", r=4)
                        src = b[:].rearrange("p (t r) -> p r t", r=4)
                    else:
                        src = b[:]
                    ins = act.activation(dst, src, ACT.Copy, scale=QSCALE if u < U_KB else 1.0)
                elif u < U_QA:
                    ins = act.copy(vb[:, u - U_VB, a, :], b[:, 0:256])
                elif u < U_KA:
                    ins = act.activation(qa[:, 2 * (u - U_QA) + a, :], b[:], ACT.Copy, scale=QSCALE)
                elif u == U_KA:
                    ins = act.copy(ka[:, a, :], b[:])
                elif u == U_VA:
                    act.activation(gate[:, a, :], b[:, 256:VA_N], ACT.Tanh, scale=0.5).then_inc(gate_tanh, 1)
                    ins = act.copy(va[:, a, :], b[:, 0:256])
                else:
                    ins = act.activation(gm[:, 2 * (u - U_GM) + a, :], b[:], ACT.Tanh, scale=0.5)
                ins.then_inc(tile_evac, 1)

            def compress():
                act.wait_ge(h_ready, 1)
                act.activation(th[:], ps[2][:, 0:256], ACT.Tanh, scale=0.5).then_inc(h_tanh, 1)

            def exps(buf, cuts, bias, sums, done):
                for i, (a, b) in enumerate(cuts):
                    ins = act.activation(buf[:, a:b], buf[:, a:b], ACT.Exp, bias=bias[i], accum_out=sums[i])
                ins.then_inc(done, 1)

            for job, n in SCHEDULE:
                if job == "tile":
                    tile(n)
                elif job == "compress":
                    compress()
                elif job == "dil_scores":
                    m = n % 6
                    g, hh = m // 2, m % 2
                    act.wait_ge(ds_max, n + 1)
                    exps(dp[:, hh, :], dil_cuts(g), [dneg[:, n % 2, i:i + 1] for i in range(TT)],
                         [dm[:, g, i, 2 + hh:3 + hh] for i in range(TT)], ds_exp)
                elif job == "dil_merge":
                    act.wait_ge(de_sub, n + 1)
                    act.activation(de[:], de[:], ACT.Exp).then_inc(de_exp, 1)
                elif job == "dil_turn":
                    act.wait_ge(dt_ready, 2 * n + 1)
                    if n >= 2:
                        act.wait_ge(do_ready, n - 1)
                    act.copy(pt[:, n % 2, 0:512], ps[2][:]).then_inc(dt_evac_act, 1)
                elif job == "cmp_scores":
                    act.wait_ge(cs_sub, 1)
                    act.activation(sc[:], sc[:], ACT.Exp).then_inc(cs_exp, 1)
                elif job == "cmp_turn":
                    for g in range(2):
                        act.wait_ge(ct_ready, g + 1)
                        act.copy(pc_t[:, g, :], ps[2 + g][:]).then_inc(ct_evac, 1)
                elif job == "scores":
                    act.wait_ge(s_max, n + 1)
                    exps(sp[:, n % 2, :], [(Q_OFF[i], Q_OFF[i] + P * (i + 1)) for i in range(TT)],
                         [ust[:, n % 2, 0, i:i + 1] for i in range(TT)],
                         [ust[:, n % 2, 1, i:i + 1] for i in range(TT)], s_exp)
                elif job == "turn":
                    if n >= 2:
                        act.wait_ge(o_ready, n - 1)
                    act.wait_ge(t_ready, 3 * n + 1)
                    act.copy(pt[:, n % 2, 0:512], ps[3][:])
                    act.wait_ge(t_ready, 3 * n + 3)
                    act.copy(pt[:, n % 2, 1024:1280], ps[5][:, 0:256]).then_inc(t_evac_act, 1)
                elif job == "out" and n % 4 == 3:
                    act.wait_ge(o_ready, n + 1)
                    act.copy(ya[:, n // 4, :], ps[6][:]).then_inc(y_evac, 1)

            act.wait_ge(y_evac, 4)
            act.wait_ge(o_ready, 16)
            act.copy(yhi[:, 4:6, :], yb[:]).then_inc(y_hi, 1)
            act.copy(yhi[:, 0:4, :], ya[:]).then_inc(y_hi, 1)
            for f in range(KC):
                if f % 2 == 0:
                    split_hi(U_UP + f // 2 + 1)
                act.wait_ge(m_sum, f + 1)
                act.copy(mhi[:, f, :], mt[:, f % 2, 2, :]).then_inc(m_hi, 1)
            for u in range(U_WO + 1, U_IN):
                split_hi(u)

            for t in range(TT):
                act.wait_ge(x2_sum, t + 1)
                if t >= 1:
                    act.wait_ge(x2_ss, t)
                act.activation(sq[:], x2[:, t, :], ACT.Square, accum_out=st[:, 1, t:t + 1]).then_inc(x2_ss, 1)
            split_hi(U_IN)
            for t in range(TT):
                for half in range(2):
                    act.wait_ge(h_turned, 2 * t + half + 1)
                    for k in range(4 * half, 4 * half + 4):
                        ins = act.activation(hhi[:, k, P * t:P * t + P], ps[2 * t + half][:, P * (k % 4):P * (k % 4) + P],
                                             ACT.Copy, scale=cvec[:, 8 + k:9 + k])
                    ins.then_inc(h_hi, 1)

            def tanh_gate(s, count):
                act.wait_ge(gu_ready, count + 1)
                act.wait_ge(gt_mul, count)
                act.activation(tg[:, s, :], ps[2 * s][:], ACT.Tanh, scale=0.5).then_inc(gu_tanh, 1)

            with act.Fori(0, FT // 2) as i:
                for s in range(2):
                    o = 1 - s
                    act.wait_ge(raw_full[o], i * 32 + (raw_count(U_IN + 1 + s)))
                    act.wait_ge(gu_ready, i * 2 + (s + 1))
                    act.copy(whi[o][:, 0:2048], raw[o][:, 0:2048]).then_inc(hi_done, 1)
                    tanh_gate(s, i * 2 + (s + 1))

            act.wait_ge(gu_free, 24)
            act.copy(ahi[:, 0, :, :], actt[:, 0:2, :]).then_inc(a_hi, 1)
            with act.Fori(0, FT // 4) as i:
                for s in range(2):
                    o = 1 - s
                    act.wait_ge(w_used, i * 2 + (s + 3))
                    act.copy(ahi[:, o, :, :], actt[:, bass.ds(i * 4 + (2 * s + 2), 2), :]).then_inc(a_hi, 1)
                    act.wait_ge(raw_full[o], i * 32 + raw_count(U_OUT + 1 + s))
                    act.copy(whi[o][:, 0:2048], raw[o][:, 0:2048]).then_inc(hi_done, 1)
            for t in range(TT):
                act.wait_ge(x3_sum, t + 1)
                if t >= 1:
                    act.wait_ge(x3_ss, t)
                act.activation(sq[:], x2[:, t, :], ACT.Square, accum_out=st[:, 2, t:t + 1]).then_inc(x3_ss, 1)

        @block.vector
        def _(dve):
            steps = [0]

            def link(ins):
                steps[0] += 1
                ins.then_inc(dve_step, 1)
                dve.wait_ge(dve_step, steps[0])

            def split_lo(u):
                dve.wait_ge(hi_done, u + 1)
                n = unit_parts(u)[1]
                dve.tensor_tensor(wlo[u % 2][:, 0:n], raw[u % 2][:, 0:n], whi[u % 2][:, 0:n].bitcast(F32),
                                  ALU.subtract).then_inc(lo_done, 1)

            def rsqrt(ss, v, y, t1):
                link(dve.tensor_scalar(v, ss, 1.0 / D, EPS, ALU.mult, ALU.add))
                link(dve.tensor_scalar(t1.bitcast(I32), v.bitcast(I32), 1, None, ALU.logical_shift_right))
                link(dve.tensor_scalar(y.bitcast(I32), t1.bitcast(I32), -1.0, float(0x5F3759DF), ALU.mult, ALU.add))
                for _ in range(4):
                    link(dve.tensor_tensor(t1, y, y, ALU.mult))
                    link(dve.scalar_tensor_tensor(out=t1, in0=t1, scalar=-0.5, in1=v, op0=ALU.mult, op1=ALU.mult))
                    link(dve.scalar_tensor_tensor(out=y, in0=t1, scalar=1.5, in1=y, op0=ALU.add, op1=ALU.mult))

            dve.wait_ge(ss_ready, TT)
            rsqrt(st[:, 0, 0:4], st[:, 0, 4:8], st[:, 3, 0:4], st[:, 3, 4:8])
            split_lo(0)
            dve.wait_ge(rows_turned, 1)
            dve.tensor_copy(cvec[:], ps[4][:, 0:48]).then_inc(cvec_ready, 1)
            dve.wait_ge(cvec_ready, 1)

            def turned_lo(lo, hi, bank, gain, t, half, done):
                for k in range(4 * half, 4 * half + 4):
                    ins = dve.scalar_tensor_tensor(
                        out=lo[:, k, P * t:P * t + P], in0=bank[:, P * (k % 4):P * (k % 4) + P],
                        scalar=gain[:, k:k + 1], in1=hi[:, k, P * t:P * t + P].bitcast(F32),
                        op0=ALU.mult, op1=ALU.subtract)
                ins.then_inc(done, 1)

            def n_row(t):
                if t >= 2:
                    dve.wait_ge(n_turned, 2 * t - 2)
                dve.tensor_scalar(xn[:, t % 2, :], xs[:, t, :], st[:, 3, t:t + 1], None, ALU.mult).then_inc(n_scaled, 1)

            def n_low(t):
                for half in range(2):
                    dve.wait_ge(n_hi, 2 * t + half + 1)
                    turned_lo(nlo, nhi, ps[(2 * t + half) % 4], cvec, t, half, n_lo)

            n_row(0)
            n_row(1)
            for t in range(TT):
                n_low(t)
                if t + 2 < TT:
                    n_row(t + 2)

            def dil_bias():
                dve.wait_ge(consts_ready, 5)
                m2i = mask2[:].bitcast(I32)
                link(dve.tensor_scalar(m2i, dist[:, 384:512], 3, None, ALU.bitwise_and))
                link(dve.tensor_scalar(mask2[:], m2i, 0.0, NEG, ALU.is_gt, ALU.mult))
                link(dve.tensor_tensor(mask2[:], mask2[:], cmask[:, 384:512], ALU.add))
                for h in range(4):
                    for g, (a, b, mask) in enumerate(((0, 256, mask0[:]), (256, 384, cmask[:, 384:512]), (384, 512, mask2[:]))):
                        ins = dve.scalar_tensor_tensor(
                            out=dbias[:, h, a:b], in0=dist[:, 512 - (b - a):512],
                            scalar=-SLOPE_DIL[g][h] * min(DIL[g], 4), in1=mask, op0=ALU.mult, op1=ALU.add)
                link(ins)

            def cmp_bias():
                for h in range(NH):
                    ins = dve.scalar_tensor_tensor(out=cbias[:, :, h, :], in0=distc[:], scalar=-SLOPE_NSA[h],
                                                   in1=maskc[:], op0=ALU.mult, op1=ALU.add)
                link(ins)

            def nsa_bias():
                dve.wait_ge(dt_ready, 24)
                for h in range(NH):
                    ins = dve.scalar_tensor_tensor(out=nbias[:, h, :], in0=dist[:], scalar=-SLOPE_NSA[h],
                                                   in1=cmask[:], op0=ALU.mult, op1=ALU.add)
                link(ins)

            def tile(n):
                u, a = TILES[n]
                if a == 0:
                    split_lo(u + 1)
                if u == U_CMP:
                    if a == 0:
                        link(dve.memset(blk[0][:], 0.0))
                        link(dve.memset(blk[1][:], 0.0))
                    dve.wait_ge(cmp_tile_ready, a + 1)
                    for g in range(2):
                        for s in range(2):
                            rows = slice(HD * s, HD * s + HD)
                            src = ps[4 + a][HD * g:HD * g + HD, :].rearrange("p (c q s) -> p s q c", q=8, s=2)[:, s]
                            code = cvec[rows, 16 + PP * a:32 + PP * a].rearrange("p (b q) -> p b q", q=8)
                            for b in range(2):
                                ins = dve.tensor_tensor(
                                    blk[a][rows, 8 * b:8 * b + 8, g, 0:31], src[:, :, b:b + 31],
                                    code[:, b, :].unsqueeze(2).to_broadcast([HD, 8, 31]), ALU.add)
                    ins.then_inc(blk_ready, 1)
                elif u == U_VA:
                    dve.wait_ge(gate_tanh, a + 1)
                    dve.tensor_scalar(gate[:, a, :], gate[:, a, :], 0.5, 0.5, ALU.mult, ALU.add).then_inc(gate_ready, 1)

            def compress():
                dve.wait_ge(h_tanh, 1)
                dve.scalar_tensor_tensor(out=hs[:].rearrange("p a b -> p (a b)"), in0=th[:], scalar=1.0,
                                         in1=ps[2][:, 0:256], op0=ALU.add, op1=ALU.mult).then_inc(hs_ready, 1)
                dve.wait_ge(kv_ready, 1)
                dve.tensor_scalar(kc[:], ps[3][:, 0:2 * CMP], 0.5, None, ALU.mult).then_inc(kv_evac, 1)
                dve.wait_ge(kv_ready, 2)
                dve.tensor_scalar(vc[:].rearrange("p g d -> p (g d)"), ps[3][:, 128:256], 0.5, None, ALU.mult).then_inc(kv_evac, 1)
                dil_bias()

            def dil_scores(n):
                m = n % 6
                g, hh = m // 2, m % 2
                h = 2 * (n // 6) + hh
                dve.wait_ge(ds_ready, n + 1)
                if n >= 6:
                    dve.wait_ge(dt_ready, 2 * (n - 6) + 2)
                if n >= 2:
                    dve.wait_ge(ds_exp, n - 1)
                for i in range(TT):
                    a, b = dil_cuts(g)[i]
                    bank, c = B_PLACE[i] if g == 0 else (0, P * i)
                    base = (0, 256, 384)[g]
                    end = base + (256 if g == 0 else P)
                    ins = dve.tensor_tensor_reduce(
                        dp[:, hh, a:b], ps[bank][:, c:c + b - a], dbias[:, h, end - (b - a):end], 1.0, NEG,
                        ALU.add, ALU.max, dm[:, g, i, hh:hh + 1])
                link(ins)
                dve.tensor_scalar(dneg[:, n % 2, :], dm[:, g, :, hh], -1.0, None, ALU.mult).then_inc(ds_max, 1)

            def dil_merge(half):
                dve.wait_ge(ds_exp, 6 * half + 6)
                dve.wait_ge(dstat_in, 32 * half + 32)
                stat = [dm[:, 0, :, :], tok[:, :, 0, :], tok[:, :, 1, :]]
                link(dve.tensor_tensor(dmx[:, 0], stat[0][:, :, 0:2], stat[1][:, :, 0:2], ALU.max))
                link(dve.tensor_tensor(dmx[:, 1], stat[2][:, :, 0:2], dmx[:, 0], ALU.max))
                for g in range(NG):
                    ins = dve.tensor_tensor(de[:, g], stat[g][:, :, 0:2], dmx[:, 1], ALU.subtract)
                ins.then_inc(de_sub, 1)
                dve.wait_ge(de_exp, half + 1)
                for g in range(NG):
                    link(dve.tensor_tensor(dz[:, g], stat[g][:, :, 2:4], de[:, g], ALU.mult))
                link(dve.tensor_tensor(dmx[:, 0], dz[:, 0], dz[:, 1], ALU.add))
                link(dve.tensor_tensor(dmx[:, 1], dz[:, 2], dmx[:, 0], ALU.add))
                link(dve.reciprocal(dmx[:, 2], dmx[:, 1]))
                if half:
                    dve.wait_ge(dw_out, 32)
                for g in range(NG):
                    ins = dve.tensor_tensor(dw[:, g], de[:, g], dmx[:, 2], ALU.mult)
                ins.then_inc(dw_ready, 1)

            def dil_scale(n):
                m = n % 6
                g, hh = m // 2, m % 2
                if m == 0:
                    dve.wait_ge(dw_ready, n // 6 + 1)
                if m == 2:
                    dve.wait_ge(dw_in, 32 * (n // 6) + 32)
                for i, (a, b) in enumerate(dil_cuts(g)):
                    w = dw[:, 0, i, hh:hh + 1] if g == 0 else dwl[:, g - 1, i, hh:hh + 1]
                    ins = dve.tensor_scalar(dp[:, hh, a:b], dp[:, hh, a:b], w, None, ALU.mult)
                ins.then_inc(dp_ready, 1)

            def dil_turn(n):
                if n % 6 == 0:
                    dil_scale(n)
                if n % 6 < 5:
                    dil_scale(n + 1)
                if (n % 6) // 2 == 0:
                    dve.wait_ge(dt_ready, 2 * n + 2)
                    if n >= 2:
                        dve.wait_ge(do_ready, n - 1)
                    dve.tensor_copy(pt[:, n % 2, 512:896], ps[3][:, 0:384]).then_inc(dt_evac_dve, 1)

            def dil_out(n):
                m = n % 6
                g, hh = m // 2, m % 2
                dve.wait_ge(do_ready, n + 1)
                rows = slice(HD * hh, HD * hh + HD)
                y = yb[rows, n // 6, :]
                o = ps[4 + n % 2][rows, :]
                if g == 0:
                    dve.tensor_copy(y, o).then_inc(do_evac, 1)
                else:
                    dve.wait_ge(do_evac, n - 1)
                    yv = y.rearrange("p (t r) -> p r t", r=4)
                    dve.tensor_tensor(yv, o.rearrange("p (r t) -> p r t", r=4), yv, ALU.add).then_inc(do_evac, 1)

            def cmp_scores():
                cmp_bias()
                dve.wait_ge(cs_ready, 1)
                for b in range(2):
                    ins = dve.tensor_tensor(sc[:, :, 4 * b:4 * b + 4].rearrange("p i h n -> p i (h n)"),
                                            ps[b][:].rearrange("p (i q) -> p i q", i=TT),
                                            cbias[:, :, 4 * b:4 * b + 4].rearrange("p i h n -> p i (h n)"), ALU.add)
                ins.then_inc(cs_added, 1)
                dve.wait_ge(cs_added, 1)
                s3 = sc[:].rearrange("p i h n -> p (i h) n")
                link(dve.tensor_reduce(cst[:, 0], s3, AX.X, ALU.max))
                link(dve.tensor_scalar(cst[:, 0], cst[:, 0], NEG / 10, None, ALU.max))
                dve.tensor_tensor(s3, s3, cst[:, 0].unsqueeze(2).to_broadcast([P, 32, CMP]),
                                  ALU.subtract).then_inc(cs_sub, 1)
                dve.wait_ge(cs_exp, 1)
                link(dve.tensor_reduce(cst[:, 1], s3, AX.X, ALU.add))
                link(dve.tensor_scalar(cst[:, 1], cst[:, 1], TINY, None, ALU.max))
                link(dve.reciprocal(cst[:, 0], cst[:, 1]))
                dve.wait_ge(gate_ready, TT)
                c0 = cst[:, 0].rearrange("p (i h) -> p i h", i=TT)
                g0 = gate[:].rearrange("p i (h b) -> p i h b", b=3)
                link(dve.tensor_tensor(cst[:, 1].rearrange("p (i h) -> p i h", i=TT), c0, g0[:, :, :, 0], ALU.mult))
                dve.tensor_tensor(s3, s3, cst[:, 1].unsqueeze(2).to_broadcast([P, 32, CMP]),
                                  ALU.mult).then_inc(cp_ready, 1)

            def scores(n):
                j, b, g = n // 4, n // 2 % 2, n % 2
                h = j + 4 * g
                dve.wait_ge(s_ready, n + 1)
                if n >= 2:
                    dve.wait_ge(t_ready, 3 * (n - 1))
                for i in range(TT):
                    bank, c = S_PLACE[i]
                    w = P * (i + 1)
                    ins = dve.tensor_tensor_reduce(
                        sp[:, n % 2, Q_OFF[i]:Q_OFF[i] + w], ps[bank][:, c:c + w], nbias[:, h, 384 - P * i:512],
                        1.0, NEG, ALU.add, ALU.max, umx[:, n % 2, i:i + 1])
                link(ins)
                dve.tensor_scalar(ust[:, n % 2, 0, :], umx[:, n % 2, :], -1.0, None, ALU.mult).then_inc(s_max, 1)

            def scale(n):
                j, b, g = n // 4, n // 2 % 2, n % 2
                h = j + 4 * g
                dve.wait_ge(s_exp, n + 1)
                link(dve.reciprocal(ust[:, n % 2, 2, :], ust[:, n % 2, 1, :]))
                link(dve.tensor_tensor(ust[:, n % 2, 3, :], ust[:, n % 2, 2, :], gate[:, :, 3 * h + 1 + b], ALU.mult))
                for i in range(TT):
                    q = sp[:, n % 2, Q_OFF[i]:Q_OFF[i] + P * (i + 1)]
                    ins = dve.tensor_scalar(q, q, ust[:, n % 2, 3, i:i + 1], None, ALU.mult)
                ins.then_inc(p_ready, 1)

            def turn(n):
                if n >= 2:
                    dve.wait_ge(o_ready, n - 1)
                dve.wait_ge(t_ready, 3 * n + 2)
                dve.tensor_copy(pt[:, n % 2, 512:1024], ps[4][:]).then_inc(t_evac_dve, 1)

            for at_, (job, n) in enumerate(SCHEDULE):
                if job == "tile":
                    tile(n)
                elif job == "compress":
                    compress()
                elif job == "dil_scores":
                    dil_scores(n)
                elif job == "dil_merge":
                    dil_merge(n)
                elif job == "dil_turn":
                    dil_turn(n)
                elif job == "dil_out":
                    dil_out(n)
                elif job == "cmp_scores":
                    cmp_scores()
                elif job == "nsa_bias":
                    nsa_bias()
                elif job == "scores":
                    scores(n)
                    if n == 0:
                        scale(0)
                elif job == "turn":
                    turn(n)
                    if n < 15:
                        scale(n + 1)

            for k, (a, b, src) in enumerate(((4, 6, yb), (0, 4, ya))):
                dve.wait_ge(y_hi, k + 1)
                dve.tensor_tensor(ylo[:, a:b, :], src[:], yhi[:, a:b, :].bitcast(F32), ALU.subtract).then_inc(y_lo, 1)
            for f in range(KC):
                if f % 2 == 0:
                    split_lo(U_UP + f // 2 + 1)
                dve.wait_ge(ab_ready, f + 1)
                if f >= 2:
                    dve.wait_ge(m_hi, f - 1)
                    dve.wait_ge(m_lo, f - 1)
                for k in range(2):
                    ins = dve.scalar_tensor_tensor(out=mt[:, f % 2, k, :], in0=gm[:, 8 * k + f, :], scalar=1.0,
                                                   in1=ps[2 * (f % 2) + k][:], op0=ALU.add, op1=ALU.mult)
                link(ins)
                dve.tensor_tensor(mt[:, f % 2, 2, :], mt[:, f % 2, 0, :], mt[:, f % 2, 1, :], ALU.add).then_inc(m_sum, 1)
                dve.wait_ge(m_hi, f + 1)
                dve.tensor_tensor(mlo[:, f, :], mt[:, f % 2, 2, :], mhi[:, f, :].bitcast(F32),
                                  ALU.subtract).then_inc(m_lo, 1)
            for u in range(U_WO + 1, U_IN):
                split_lo(u)

            dve.wait_ge(x2_in, 16 * TT)
            dve.wait_ge(y_lo, 2)

            def residual(t, done):
                for half in range(2):
                    q = x2[:, t, 512 * half:512 * half + 512]
                    ins = dve.scalar_tensor_tensor(out=q, in0=ps[2 * t + half][:], scalar=0.5, in1=q,
                                                   op0=ALU.mult, op1=ALU.add)
                ins.then_inc(done, 1)

            for t in range(TT):
                dve.wait_ge(wo_ready, t + 1)
                residual(t, x2_sum)
                dve.wait_ge(x2_ss, t + 1)
                rsqrt(st[:, 1, t:t + 1], st[:, 1, 4 + t:5 + t], st[:, 3, t:t + 1], st[:, 3, 4 + t:5 + t])
                if t >= 2:
                    dve.wait_ge(h_turned, 2 * t - 2)
                dve.tensor_scalar(hn[:, t % 2, :], x2[:, t, :], st[:, 3, t:t + 1], None, ALU.mult).then_inc(h_scaled, 1)
            split_lo(U_IN)
            for t in range(TT):
                for half in range(2):
                    dve.wait_ge(h_hi, 2 * t + half + 1)
                    turned_lo(hlo, hhi, ps[2 * t + half], cvec[:, 8:16], t, half, h_lo)

            dve.sem_inc(gt_mul, 2)
            dve.sem_inc(gu_free, 2)
            with dve.Fori(0, FT // 2) as i:
                for s in range(2):
                    o = 1 - s
                    dve.wait_ge(hi_done, i * 2 + (U_IN + 2 + s))
                    dve.tensor_tensor(wlo[o][:, 0:2048], raw[o][:, 0:2048], whi[o][:, 0:2048].bitcast(F32),
                                      ALU.subtract).then_inc(lo_done, 1)
                    dve.wait_ge(gu_tanh, i * 2 + (s + 1))
                    dve.wait_ge(gu_free, i * 2 + (s + 1))
                    dve.scalar_tensor_tensor(out=tm[:, s, :], in0=tg[:, s, :], scalar=1.0, in1=ps[2 * s][:],
                                             op0=ALU.add, op1=ALU.mult).then_inc(gt_mul, 1)
                    dve.wait_ge(gt_mul, i * 2 + (s + 3))
                    dve.tensor_tensor(actt[:, i * 2 + s, :], ps[2 * s + 1][:], tm[:, s, :],
                                      ALU.mult).then_inc(gu_free, 1)

            dve.wait_ge(gu_free, 24)
            dve.wait_ge(a_hi, 1)
            dve.tensor_tensor(alo[:, 0, :, :], actt[:, 0:2, :], ahi[:, 0, :, :].bitcast(F32), ALU.subtract).then_inc(a_lo, 1)
            with dve.Fori(0, FT // 4) as i:
                for s in range(2):
                    o = 1 - s
                    dve.wait_ge(a_hi, i * 2 + (s + 2))
                    dve.tensor_tensor(alo[:, o, :, :], actt[:, bass.ds(i * 4 + (2 * s + 2), 2), :],
                                      ahi[:, o, :, :].bitcast(F32), ALU.subtract).then_inc(a_lo, 1)
                    dve.wait_ge(hi_done, i * 2 + (U_OUT + 2 + s))
                    dve.tensor_tensor(wlo[o][:, 0:2048], raw[o][:, 0:2048], whi[o][:, 0:2048].bitcast(F32),
                                      ALU.subtract).then_inc(lo_done, 1)
            dve.wait_ge(gfin_in, 16)
            for t in range(TT):
                dve.wait_ge(fo_ready, t + 1)
                residual(t, x3_sum)
                dve.wait_ge(x3_ss, t + 1)
                rsqrt(st[:, 2, t:t + 1], st[:, 2, 4 + t:5 + t], st[:, 3, t:t + 1], st[:, 3, 4 + t:5 + t])
                if t >= 2:
                    dve.wait_ge(out_done[t % 2], 16 * (t // 2))
                dve.scalar_tensor_tensor(out=fin[:, t % 2, :], in0=x2[:, t, :], scalar=st[:, 3, t:t + 1],
                                         in1=gfin[:], op0=ALU.mult, op1=ALU.mult).then_inc(fin_ready, 1)

        @block.tensor
        def _(pe):
            def split_product(dst, w, x_, start, stop):
                pe.matmul(dst, w[0], x_[0], start=start, stop=False)
                pe.matmul(dst, w[0], x_[1], start=False, stop=False)
                return pe.matmul(dst, w[1], x_[0], start=False, stop=stop)

            def turn_rows(src, t, half, banks, done):
                for k in range(4 * half, 4 * half + 4):
                    ins = pe.transpose(ps[banks][:, P * (k % 4):P * (k % 4) + P], src[:, P * k:P * k + P], ident[:])
                ins.then_inc(done, 1)

            pe.wait_ge(rows_in, 64)
            pe.wait_ge(consts_ready, 1)
            pe.transpose(ps[4][:, 0:48], crows[0:48, :], ident[0:48, 0:48]).then_inc(rows_turned, 1)
            for t in range(TT):
                pe.wait_ge(n_scaled, t + 1)
                for half in range(2):
                    if t >= 2:
                        pe.wait_ge(n_lo, 2 * t + half - 3)
                    turn_rows(xn[:, t % 2, :], t, half, (2 * t + half) % 4, n_turned)
            pe.wait_ge(n_lo, 2 * TT)
            pe.wait_ge(cvec_ready, 1)

            def token_cols(n_, k, g, a):
                if g == 0:
                    return n_[:, k, P * a:P * a + P]
                return n_[:, k, :].rearrange("p (t r) -> p r t", r=4)[:, a]

            def tile(n):
                u, a = TILES[n]
                if a == 0:
                    pe.wait_ge(hi_done, u + 1)
                    pe.wait_ge(lo_done, u + 1)
                bank = TILE_BANK[n]
                before = [v for v in range(2, n) if TILE_BANK[v] == bank]
                if before:
                    pe.wait_ge(tile_evac, before[-1] - 1)
                natural = U_VB <= u < U_QA or u == U_VA
                w = [slot_view(r, u, KC, VA_N if u == U_VA else 256) for r in (whi, wlo)]
                for k in range(KC):
                    if natural:
                        g = 0 if u == U_VA else u - U_VB
                        cols = VA_N if u == U_VA else 256
                        ins = split_product(ps[bank][:, 0:cols], [token_cols(v, k, g, a) for v in (nhi, nlo)],
                                            [v[:, k, :] for v in w], k == 0, k == KC - 1)
                    else:
                        wk = [v[:, k, P * a:P * a + P] for v in w]
                        ins = split_product(ps[bank][:], wk, (nhi[:, k, :], nlo[:, k, :]), k == 0, k == KC - 1)
                ins.then_inc(cmp_tile_ready if u == U_CMP else tile_ready, 1)

            def compress():
                for kv in range(2):
                    pe.wait_ge(wck_in[kv], 16)
                    pe.wait_ge(blk_ready, kv + 1)
                    for m in range(2):
                        o = ps[2][:, 64 * (2 * kv + m):64 * (2 * kv + m) + 64]
                        for q in range(PP):
                            ins = pe.matmul(o, wck[kv][:, q, P * m:P * m + P], blk[kv][:, q].rearrange("p g c -> p (g c)"),
                                            start=(q == 0), stop=(q == PP - 1))
                ins.then_inc(h_ready, 1)
                pe.wait_ge(w2_in, 48)
                pe.wait_ge(hs_ready, 1)
                for m in range(2):
                    ins = pe.matmul(ps[3][:, 0:64], w2k[:, m].rearrange("p r d -> p (r d)"), hs[:, m, :],
                                    start=(m == 0), stop=(m == 1))
                ins.then_inc(kv_ready, 1)
                pe.wait_ge(kv_evac, 1)
                for g in range(2):
                    for r in range(4):
                        for m in range(2):
                            ins = pe.matmul(ps[3][32 * r:32 * r + 32, 128 + HD * g:128 + HD * g + HD],
                                            hs[:, 2 + m, CMP * g:CMP * g + CMP], w2v[:, m, :],
                                            start=(m == 0), stop=(m == 1))
                ins.then_inc(kv_ready, 1)

            def dil_scores(n):
                m = n % 6
                g, hh, t = m // 2, m % 2, n // 6
                pe.wait_ge(tile_evac, LAST_TILE[U_KB + 2] - 1)
                if n:
                    pe.wait_ge(ds_max, n)
                rows = slice(HD * hh, HD * hh + HD)
                q, k = qb[rows, 2 * g + t, :], kb[rows, 2 * g + t, :]
                for i in range(TT):
                    lo = P * (i - 1) if g == 0 and i else P * i
                    bank, c = B_PLACE[i] if g == 0 else (0, P * i)
                    ins = pe.matmul(ps[bank][:, c:c + P * (i + 1) - lo], q[:, P * i:P * i + P], k[:, lo:P * (i + 1)],
                                    start=True, stop=True)
                ins.then_inc(ds_ready, 1)

            def dil_evacuated(n):
                pe.wait_ge(dt_evac_act, n + 1)
                pe.wait_ge(dt_evac_dve, sum(v % 6 < 2 for v in range(n + 1)))

            def dil_turn(n):
                m = n % 6
                g, hh = m // 2, m % 2
                pe.wait_ge(dp_ready, n + 1)
                if n:
                    dil_evacuated(n - 1)
                if n == 0:
                    pe.wait_ge(kv_evac, 2)
                if n == 6:
                    pe.wait_ge(ct_evac, 2)
                p_ = dp[:, hh, :]
                if g == 0:
                    for j in range(TT):
                        bank, c = ps[2 + j // 2], 256 * (j % 2)
                        a = B_OFF[j] + (P if j else 0)
                        ins = pe.transpose(bank[:, c:c + P], p_[:, a:a + P], ident[:])
                        if j < 3:
                            ins = pe.transpose(bank[:, c + P:c + 256], p_[:, B_OFF[j + 1]:B_OFF[j + 1] + P], ident[:])
                        if j % 2:
                            ins.then_inc(dt_ready, 1)
                else:
                    a = dil_cuts(g)[0][0]
                    for i in range(TT):
                        ins = pe.transpose(ps[2][:, P * i:P * i + P], p_[:, a + P * i:a + P * i + P], ident[:])
                    ins.then_inc(dt_ready, 2)

            def dil_out(n):
                m = n % 6
                g, hh, t = m // 2, m % 2, n // 6
                dil_evacuated(n)
                if n >= 2:
                    pe.wait_ge(do_evac, n - 1)
                rows = slice(HD * hh, HD * hh + HD)
                h = 2 * t + hh
                o = ps[4 + n % 2]
                for i in range(TT):
                    q = slice(P * i, P * i + P)
                    if g == 0 and i:
                        pe.matmul(o[rows, q], vb[:, g, i - 1, HD * h:HD * h + HD], pt[:, n % 2, 256 * (i - 1) + P:256 * i], start=True, stop=False)
                    c = 256 * i if g == 0 else P * i
                    ins = pe.matmul(o[rows, q], vb[:, g, i, HD * h:HD * h + HD], pt[:, n % 2, c:c + P], start=not (g == 0 and i), stop=True)
                ins.then_inc(do_ready, 1)

            def cmp_scores():
                pe.wait_ge(ds_max, 12)
                for i in range(TT):
                    for h in range(NH):
                        g, j = h // 4, h % 4
                        rows = slice(HD * g, HD * g + HD)
                        c = P * i + CMP * j
                        ins = pe.matmul(ps[g][:, c:c + CMP], qa[rows, j, P * i:P * i + P],
                                        kc[rows, CMP * g:CMP * g + CMP], start=True, stop=True)
                ins.then_inc(cs_ready, 1)

            def cmp_turn():
                pe.wait_ge(cp_ready, 1)
                dil_evacuated(5)
                for g in range(2):
                    for i in range(TT):
                        ins = pe.transpose(ps[2 + g][:, P * i:P * i + P],
                                           sc[:, i, 4 * g:4 * g + 4, :].rearrange("p h n -> p (h n)"), ident[:])
                    ins.then_inc(ct_ready, 1)

            def scores(n):
                j, b, g = n // 4, n // 2 % 2, n % 2
                if n == 0:
                    pe.wait_ge(cs_added, 1)
                else:
                    pe.wait_ge(s_max, n)
                rows = slice(HD * g, HD * g + HD)
                for i in range(TT):
                    bank, c = S_PLACE[i]
                    ins = pe.matmul(ps[bank][:, c:c + P * (i + 1)], qa[rows, j, P * i:P * i + P],
                                    ka[rows, b, 0:P * (i + 1)], start=True, stop=True)
                ins.then_inc(s_ready, 1)

            def turn(n):
                pe.wait_ge(p_ready, n + 1)
                if n:
                    pe.wait_ge(t_evac_act, n)
                    pe.wait_ge(t_evac_dve, n)
                else:
                    pe.wait_ge(do_evac, 12)
                    pe.wait_ge(ct_evac, 2)
                for js in ((0,), (1, 3), (2,)):
                    for j in js:
                        bank, c = K_PLACE[j]
                        for i in range(j, TT):
                            a = Q_OFF[i] + P * j
                            ins = pe.transpose(ps[bank][:, c + P * (i - j):c + P * (i - j) + P],
                                               sp[:, n % 2, a:a + P], ident[:])
                    ins.then_inc(t_ready, 1)

            def out_(n):
                j, b, g = n // 4, n // 2 % 2, n % 2
                pe.wait_ge(t_evac_act, n + 1)
                pe.wait_ge(t_evac_dve, n + 1)
                rows = slice(HD * g, HD * g + HD)
                o = ps[6]
                if b == 0:
                    if n == 0:
                        pe.wait_ge(tile_evac, max(v for v in TILE_BANK if TILE_BANK[v] == 6) - 1)
                    if n % 4 == 0 and n:
                        pe.wait_ge(y_evac, n // 4)
                    pe.matmul(o[rows, :], vc[CMP * j:CMP * j + CMP, g, :], pc_t[CMP * j:CMP * j + CMP, g, :],
                              start=True, stop=False)
                for k in range(TT):
                    ins = pe.matmul(o[rows, P * k:], va[:, k, 128 * b + HD * g:128 * b + HD * g + HD],
                                    pt[:, n % 2, K_OFF[k]:K_OFF[k] + P * (TT - k)],
                                    start=False, stop=(b == 1 and k == TT - 1))
                ins.then_inc(o_ready, 1)

            for job, n in SCHEDULE:
                if job == "tile":
                    tile(n)
                elif job == "compress":
                    compress()
                elif job == "dil_scores":
                    dil_scores(n)
                elif job == "dil_turn":
                    dil_turn(n)
                elif job == "dil_out":
                    dil_out(n)
                elif job == "cmp_scores":
                    cmp_scores()
                elif job == "cmp_turn":
                    cmp_turn()
                elif job == "scores":
                    scores(n)
                elif job == "turn":
                    turn(n)
                elif job == "out":
                    out_(n)

            pe.wait_ge(y_lo, 2)
            for f in range(KC):
                u = U_UP + f // 2
                if f % 2 == 0:
                    pe.wait_ge(hi_done, u + 1)
                    pe.wait_ge(lo_done, u + 1)
                if f >= 2:
                    pe.wait_ge(m_sum, f - 1)
                w = [slot_view(r, u, 6, 256) for r in (whi, wlo)]
                for k, (lo, hi) in enumerate(((0, 4), (4, 6))):
                    for c in range(lo, hi):
                        ins = split_product(ps[2 * (f % 2) + k][:], [v[:, c, P * (f % 2):P * (f % 2) + P] for v in w],
                                            (yhi[:, c, :], ylo[:, c, :]), c == lo, c == hi - 1)
                ins.then_inc(ab_ready, 1)

            def to_tokens(act_pairs, w_pairs, first, last, done):
                for t in range(TT):
                    for k in range(2):
                        for half in range(2):
                            ins = split_product(
                                ps[2 * t + half][:], [v[:, k, P * t:P * t + P] for v in act_pairs],
                                [v[:, k, 512 * half:512 * half + 512] for v in w_pairs],
                                first and k == 0, last and k == 1)
                    if last:
                        ins.then_inc(done, 1)
                if not last:
                    ins.then_inc(w_used, 1)

            pe.wait_ge(m_hi, KC)
            pe.wait_ge(m_lo, KC)
            for c in range(4):
                u = U_WO + c
                pe.wait_ge(hi_done, u + 1)
                pe.wait_ge(lo_done, u + 1)
                to_tokens([v[:, 2 * c:2 * c + 2, :] for v in (mhi, mlo)],
                          [slot_view(r, u, 2, D) for r in (whi, wlo)], c == 0, c == 3, wo_ready)
            for t in range(TT):
                pe.wait_ge(h_scaled, t + 1)
                for half in range(2):
                    turn_rows(hn[:, t % 2, :], t, half, 2 * t + half, h_turned)
            pe.wait_ge(h_lo, 2 * TT)

            pe.sem_inc(gu_ready, 1)
            with pe.Fori(0, FT // 2) as i:
                for s in range(2):
                    pe.wait_ge(hi_done, i * 2 + (U_IN + s + 1))
                    pe.wait_ge(lo_done, i * 2 + (U_IN + s + 1))
                    pe.wait_ge(gu_free, i * 2 + (s + 1))
                    for half in range(2):
                        for k in range(KC):
                            w = [slot_view(r, s, KC, 256)[:, k, P * half:P * half + P] for r in (whi, wlo)]
                            ins = split_product(ps[2 * s + half][:], w, (hhi[:, k, :], hlo[:, k, :]), k == 0, k == KC - 1)
                    ins.then_inc(gu_ready, 1)

            def ffn_out(s, first, last):
                to_tokens((ahi[:, s], alo[:, s]), [slot_view(r, s, 2, D) for r in (whi, wlo)],
                                 first, last, fo_ready)

            pe.wait_ge(gu_free, 24)
            for s in range(2):
                pe.wait_ge(hi_done, U_OUT + s + 1)
                pe.wait_ge(lo_done, U_OUT + s + 1)
                pe.wait_ge(a_lo, s + 1)
                ffn_out(s, s == 0, False)
            with pe.Fori(1, FT // 4) as i:
                for s in range(2):
                    pe.wait_ge(hi_done, i * 2 + (U_OUT + s + 1))
                    pe.wait_ge(lo_done, i * 2 + (U_OUT + s + 1))
                    pe.wait_ge(a_lo, i * 2 + (s + 1))
                    ffn_out(s, False, False)
            pe.wait_ge(hi_done, N_UNITS)
            pe.wait_ge(lo_done, N_UNITS)
            pe.wait_ge(a_lo, FT // 2)
            ffn_out(0, False, True)


def dil_cuts(g):
    if g == 0:
        return [(B_OFF[i], B_OFF[i] + (256 if i else P)) for i in range(TT)]
    base = 896 + 512 * (g - 1)
    return [(base + P * i, base + P * i + P) for i in range(TT)]


BASE = 16512

_INS = ['x', 'norm_mix', 'w_in', 'pe_k', 'pe_v', 'w_ck1', 'w_ck2', 'w_cv1', 'w_cv2', 'w_up_nsa', 'w_up_dil',
        'w_out', 'norm_ffn', 'w_ffn_in', 'w_ffn_out', 'norm_final']


def kernel(**inputs):
    import numpy as _np
    import concourse.bacc as _bacc
    from concourse import mybir as _mybir
    from concourse.bass_utils import run_bass_kernel_spmd as _run

    nc = _bacc.Bacc("TRN2", target_bir_lowering=False, num_devices=1)
    arrays, args = {}, []
    for name in _INS:
        a = _np.ascontiguousarray(inputs[name])
        arrays[f"in_{name}_dram"] = a
        args.append(nc.dram_tensor(f"in_{name}_dram", a.shape, _mybir.dt.from_np(a.dtype), kind="ExternalInput").ap())
    args.append(nc.dram_tensor("out_0_dram", (1, S, D), F32, kind="ExternalOutput").ap())
    args.append([[nc.dram_tensor(f"scratch_{half}_{k}", (S, 4 if k < 2 else 2), F32, kind="Internal").ap()
                  for k in range(4)] for half in range(2)])
    trunk(nc, *args)
    r = _run(nc, [arrays], core_ids=[0])
    return r.results[0]["out_0_dram"]
```

```python
from contextlib import ExitStack

import concourse.bass as bass
from concourse import mybir

F32 = mybir.dt.float32
F32R = mybir.dt.float32r
I32 = mybir.dt.int32
ALU = mybir.AluOpType
ACT = mybir.ActivationFunctionType
AX = mybir.AxisListType

P = 128
D = 1024
S = 512
KC = D // P
TT = S // P
HD = 64
NH = 8
NG = 3
DIL = (1, 4, 16)
FF = 2816
FT = FF // P
CMP = 32
PP = 16
CH = 256
EPS = 1e-6
NEG = -1e30
TINY = 1e-30
QSCALE = HD ** -0.5

SLOPE = [2.0 ** (-8.0 * k / 20) for k in range(1, 21)]
SLOPE_DIL = [SLOPE[0:4], SLOPE[4:8], SLOPE[16:20]]
SLOPE_NSA = SLOPE[8:16]

C_Q, C_KC, C_KS, C_VS, C_KW, C_VW = 0, 512, 768, 896, 1024, 1152
C_QB, C_GM = 1304, 3608
VA_N = 280

U_CMP, U_QB, U_KB, U_VB, U_QA, U_KA, U_VA, U_GM, U_UP, U_WO, U_IN, U_OUT = 0, 1, 4, 7, 10, 12, 13, 14, 22, 26, 30, 52
N_UNITS = U_OUT + FT // 2
SLOT = KC * VA_N

TILES = [(u, a) for u in range(U_UP) for a in range(4 if u in (7, 8, 9, 13) else 2)]
FIRST_TILE = {u: TILES.index((u, 0)) for u in range(U_UP)}
LAST_TILE = {u: max(n for n, t in enumerate(TILES) if t[0] == u) for u in range(U_UP)}

Q_OFF = [0, 128, 384, 768]
S_PLACE = [(1, 384), (2, 0), (1, 0), (0, 0)]
K_OFF = [0, 512, 1024, 896]
K_PLACE = [(3, 0), (4, 0), (5, 0), (4, 384)]
B_OFF = [0, 128, 384, 640]
B_PLACE = [(1, 256), (0, 0), (0, 256), (1, 0)]


def schedule():
    jobs = [("tile", n) for n in range(FIRST_TILE[U_QB + 2] + 1)]
    jobs += [("cmp_hidden", 0), ("tile", FIRST_TILE[U_QB + 2] + 1), ("cmp_kv", 0)]
    jobs += [("tile", n) for n in range(FIRST_TILE[U_KB], FIRST_TILE[U_QA])]
    tile = iter(range(FIRST_TILE[U_QA], len(TILES)))
    for m in range(6):
        jobs += [("dil_scores", m), ("tile", next(tile))]
    jobs.append(("dil_merge", 0))
    jobs += [("tile", next(tile)) for _ in range(4)]
    for m in range(6):
        jobs += [("dil_turn", m), ("dil_scores", 6 + m), ("dil_out", m)]
    jobs += [("cmp_scores", 0), ("dil_merge", 1), ("tile", next(tile)), ("tile", next(tile)), ("cmp_turn", 0)]
    for m in range(6, 12):
        jobs += [("dil_turn", m)]
        if m > 6:
            jobs += [("dil_out", m - 1)]
    jobs += [("dil_out", 11), ("nsa_bias", 0)]
    for n in range(4 * 4):
        jobs.append(("scores", n))
        if n:
            jobs.append(("turn", n - 1))
        if n not in (0, 8, 12, 15):
            jobs.append(("tile", next(tile)))
        if n:
            jobs.append(("out", n - 1))
    jobs += [("turn", 15), ("tile", next(tile)), ("out", 15), ("tile", next(tile))]
    return jobs


SCHEDULE = schedule()
NSA_FROM = SCHEDULE.index(("nsa_bias", 0))
TILE_BANK = {}
for _at, (_job, _n) in enumerate(SCHEDULE):
    if _job == "tile":
        TILE_BANK[_n] = 4 + _n if _n < 2 else 7 if _at > NSA_FROM else 6 + _n % 2


def by_act(n):
    return U_VB <= TILES[n][0] < U_QA or TILES[n][0] == U_VA


def evac_count(n):
    return sum(by_act(v) == by_act(n) for v in range(LAST_TILE[U_CMP] + 1, n + 1))


def unit_parts(u):
    if u == U_CMP:
        return 1, KC * 256
    if u == U_VA:
        return 2, KC * VA_N
    if U_QA <= u < U_KA:
        return 4, KC * 256
    if U_UP <= u < U_WO:
        return 3, 6 * 256
    return 2, KC * 256


def raw_count(u):
    return 16 * sum(unit_parts(v)[0] for v in range(u % 2, u + 1, 2))


def trunk(nc, x, norm_mix, w_in, pe_k, pe_v, w_ck1, w_ck2, w_cv1, w_cv2, w_up_nsa, w_up_dil,
          w_out, norm_ffn, w_ffn_in, w_ffn_out, norm_final, out, scratch):
    with ExitStack() as ctx:
        def sem(name):
            return ctx.enter_context(nc.semaphore(name))

        def at(name, shape, offset, dt=F32):
            return nc.alloc_sbuf_tensor_at(name, [P, *shape], dt, offset=offset)

        A = BASE
        E = A + 32768
        Fo = E + 26624
        B = Fo + 10240
        C = B + 6 * 4 * SLOT
        Dd = C + 16384
        G = Dd + 36864
        H = G + 4 * 4400
        nhi, nlo = (at(f"n_{k}", [KC, S], A + o, F32R) for k, o in (("hi", 0), ("lo", 16384)))
        raw = [at(f"w_raw{i}", [SLOT], B + 4 * SLOT * i) for i in range(2)]
        whi = [at(f"w_hi{i}", [SLOT], B + 4 * SLOT * (2 + i), F32R) for i in range(2)]
        wlo = [at(f"w_lo{i}", [SLOT], B + 4 * SLOT * (4 + i), F32R) for i in range(2)]
        qa = at("qa", [4, S], C)
        ka = at("ka", [2, S], C + 8192)
        va = at("va", [TT, 256], C + 12288)
        qb = at("qb", [6, S], Dd)
        kb = at("kb", [6, S], Dd + 12288)
        vb = at("vb", [NG, TT, 256], Dd + 24576)
        gm = at("gm", [16, S], Dd)
        wck = [at("wck_k", [PP, CH], C), at("wck_v", [PP, CH], Dd + 12288)]
        xs = at("xs", [TT, D], E)
        xsq = at("xsq", [2, D], E + 16384)
        blk = [at(f"blk_{k}", [PP, 2, CMP], E + 4096 * i) for i, k in enumerate("kv")]
        dp = at("dil_p", [2, 1920], E)
        dbias = at("dil_bias", [4, 512], E + 15360)
        nbias = at("nsa_bias", [NH, S], E)
        sp = at("probs", [2, 1280], E + 16384)
        cbias = at("cmp_bias", [TT, NH, CMP], E + 20480)
        yhi, ylo = (at(f"y_{k}", [6, S], E + o, F32R) for k, o in (("hi", 0), ("lo", 12288)))
        pt = at("probs_t", [2, 1280], Fo)
        ident = at("ident", [P], G)
        dist = at("dist", [S], G + 512, I32)
        cmask = at("cmask", [S], G + 2560)
        mask0 = at("mask0", [256], G + 4608)
        mask2 = at("mask2", [P], G + 5632)
        distc = at("distc", [TT, CMP], G + 6144, I32)
        maskc = at("maskc", [TT, CMP], G + 6656)
        pc_t = at("pc_t", [2, S], G + 7168)
        hs = at("hs", [4, 2 * CMP], G + 11264)
        kc = at("kc", [2 * CMP], G + 12288)
        vc = at("vc", [2, HD], G + 12544)
        w2k = at("w2k", [2, 2, HD], G + 13056)
        w2v = at("w2v", [2, HD], G + 14080)
        crows = at("crows", [P], G + 14592)
        cvec = at("cvec", [48], G + 15104)
        gate = at("gate", [TT, NH * 3], G + 15296)
        st = at("st", [4, 8], G + 15680)
        ust = at("ust", [2, 4, TT], G + 15808)
        cst = at("cst", [2, 32], G + 15936)
        dm = at("dm", [NG, TT, 4], G + 16192)
        dneg = at("dneg", [2, TT], G + 16384)
        tok = at("tok", [TT, 2, 4], G + 16416)
        dmx = at("dmx", [3, TT, 2], G + 16544)
        de = at("de", [NG, TT, 2], G + 16640)
        dz = at("dz", [NG, TT, 2], G + 16736)
        dw = at("dw", [NG, TT, 2], G + 16832)
        dwl = at("dwl", [2, TT, 2], G + 16928)
        umx = at("umx", [2, TT], G + 16992)
        rrow = at("rrow", [S], H + 12288)
        rcol = at("rcol", [TT], H + 14336)
        rhalf = at("rhalf", [2, TT], H + 14368)
        ctmp = at("cmp_tmp", [2, S], Fo)
        ya = at("ya", [4, S], H)
        yb = at("yb", [2, S], H + 8192)
        sc = at("cmp_p", [TT, NH, CMP], H)
        th = at("tanh_h", [4 * 2 * CMP], H + 4096)
        mhi, mlo = nhi, nlo
        x2 = at("x2", [TT, D], C)
        hhi, hlo = (at(f"h_{k}", [KC, S], Dd + o, F32R) for k, o in (("hi", 0), ("lo", 16384)))
        mt = at("merge_tmp", [2, 3, S], Fo - 2048)
        actt = at("act_t", [FT, S], A)
        ahi, alo = (at(f"a_{k}", [2, 2, S], A + 45056 + o, F32R) for k, o in (("hi", 0), ("lo", 8192)))
        tg = at("tanh_g", [2, S], A + 61440)
        tm = at("gate_mul", [2, S], A + 65536)
        gfin = at("gfin", [D], G + 512)
        sq = at("square", [D], H)
        gs = at("gate_scaled", [2, S], H + 4096)
        xg = at("xg", [TT, D], Dd)

        ps = [ctx.enter_context(nc.psum_tensor(f"bank{i}", [P, 512], F32)) for i in range(8)]

        x_in = [sem(f"x_in{i}") for i in range(TT)]
        rows_in, w2_in, gfin_in, x2_in = sem("rows_in"), sem("w2_in"), sem("gfin_in"), sem("x2_in")
        wck_in = [sem("wck_k_in"), sem("wck_v_in")]
        raw_full = [sem("raw_full0"), sem("raw_full1")]
        hi_done, lo_done, w_used = sem("hi_done"), sem("lo_done"), sem("w_used")
        pool_step, consts_ready = sem("pool_step"), sem("consts_ready")
        dve_step, act_step = sem("dve_step"), sem("act_step")
        rows_turned, cvec_ready = sem("rows_turned"), sem("cvec_ready")
        ss_ready, n_turned, n_hi, n_lo = (sem(k) for k in ("ss_ready", "n_turned", "n_hi", "n_lo"))
        first_raw, first_hi, first_lo = (sem(k) for k in ("first_raw", "first_hi", "first_lo"))
        r_ready, r_out, r_in = (sem(k) for k in ("r_ready", "r_out", "r_in"))
        tile_ready, tile_evac_act, tile_evac_dve = (sem(k) for k in ("tile_ready", "tile_evac_act", "tile_evac_dve"))
        gm_tanh = sem("gm_tanh")
        cmp_tile_ready, blk_ready, h_ready, h_tanh, hs_ready = (
            sem(k) for k in ("cmp_tile_ready", "blk_ready", "h_ready", "h_tanh", "hs_ready"))
        kv_ready, kv_evac = sem("kv_ready"), sem("kv_evac")
        ds_ready, ds_max, ds_exp, dstat_out, dstat_in, de_sub, de_exp, dw_ready, dw_out, dw_in = (
            sem(k) for k in ("ds_ready", "ds_max", "ds_exp", "dstat_out", "dstat_in", "de_sub", "de_exp",
                             "dw_ready", "dw_out", "dw_in"))
        dp_ready, dt_ready, dt_evac_act, dt_evac_dve, do_ready, do_evac = (
            sem(k) for k in ("dp_ready", "dt_ready", "dt_evac_act", "dt_evac_dve", "do_ready", "do_evac"))
        cs_ready, cs_added, cs_sub, cs_exp, cp_ready, ct_ready, ct_evac = (
            sem(k) for k in ("cs_ready", "cs_added", "cs_sub", "cs_exp", "cp_ready", "ct_ready", "ct_evac"))
        gate_tanh, gate_ready = sem("gate_tanh"), sem("gate_ready")
        s_ready, s_max, s_exp, p_ready, t_ready, t_evac_act, t_evac_dve, o_ready, y_evac = (
            sem(k) for k in ("s_ready", "s_max", "s_exp", "p_ready", "t_ready", "t_evac_act", "t_evac_dve",
                             "o_ready", "y_evac"))
        y_hi, y_lo = sem("y_hi"), sem("y_lo")
        ab_ready, m_sum, m_hi, m_lo = (sem(k) for k in ("ab_ready", "m_sum", "m_hi", "m_lo"))
        wo_ready, x2_sum, x2_ss, h_turned, h_hi, h_lo = (
            sem(k) for k in ("wo_ready", "x2_sum", "x2_ss", "h_turned", "h_hi", "h_lo"))
        gu_ready, g_scaled, gu_tanh, gt_mul, gu_free = (
            sem(k) for k in ("gu_ready", "g_scaled", "gu_tanh", "gt_mul", "gu_free"))
        a_hi, a_lo, fo_ready, x3_sum, x3_ss, fin_ready, out_done = (
            sem(k) for k in ("a_hi", "a_lo", "fo_ready", "x3_sum", "x3_ss", "fin_ready", "out_done"))

        def slot_view(ring, u, k, n):
            return ring[u % 2][:, 0:k * n].rearrange("p (k n) -> p k n", k=k)

        def unit_used(u):
            if u == U_CMP:
                return cmp_tile_ready, 2
            if u < U_UP:
                return tile_ready, LAST_TILE[u] - 1
            if u < U_WO:
                return ab_ready, 2 * (u - U_UP) + 2
            if u < U_IN - 1:
                return w_used, u - U_WO + 1
            return wo_ready, 2 * TT

        block = ctx.enter_context(nc.Block())

        @block.sync
        def _(sp_):
            w_in_v = w_in[0].rearrange("(k p) n -> p k n", p=P)

            def load(u):
                if u >= 2:
                    sp_.wait_ge(lo_done, u - 1)
                full = raw_full[u % 2]
                if u < U_UP:
                    dst = slot_view(raw, u, KC, VA_N if u == U_VA else 256)
                    if U_QA <= u < U_KA:
                        cuts = [(128 * h + HD * t, 128 * h + HD * t + HD, C_Q + 256 * t + 128 * (u - U_QA) + HD * h)
                                for h in range(2) for t in range(2)]
                    elif u == U_KA:
                        cuts = [(0, 128, C_KS), (128, 256, C_KW)]
                    elif u == U_VA:
                        cuts = [(0, 128, C_VS), (128, VA_N, C_VW)]
                    else:
                        c = C_KC if u == U_CMP else C_QB + 256 * (u - U_QB) if u < U_QA else C_GM + 256 * (u - U_GM)
                        for k in (0, 4):
                            done = first_raw if u == U_CMP and k == 0 else full
                            sp_.dma_start(dst[:, k:k + 4, :], w_in_v[:, k:k + 4, c:c + 256]).then_inc(done, 16)
                        return
                    for a, b, c in cuts:
                        sp_.dma_start(dst[:, :, a:b], w_in_v[:, :, c:c + b - a]).then_inc(full, 16)
                elif u < U_WO:
                    cols = slice(256 * (u - U_UP), 256 * (u - U_UP) + 256)
                    dst = slot_view(raw, u, 6, 256)
                    for t in range(2):
                        src = w_up_nsa[0, 256 * t:256 * t + 256, cols].rearrange("(j d) n -> d j n", d=HD)
                        sp_.dma_start(dst[HD * t:HD * t + HD, 0:4, :], src).then_inc(full, 16)
                    src = w_up_dil[0, :, cols].rearrange("(t p) n -> p t n", p=P)
                    sp_.dma_start(dst[:, 4:6, :], src).then_inc(full, 16)
                else:
                    dst = slot_view(raw, u, 2, D)
                    for k in range(2):
                        r = 256 * (u - U_WO) + P * k if u < U_IN else 256 * (u - U_OUT) + P * k
                        w = w_out if u < U_IN else w_ffn_out
                        sp_.dma_start(dst[:, k, :], w[0, r:r + P, :]).then_inc(full, 16)

            for t in range(TT):
                sp_.dma_start(xs[:, t, :], x[0, P * t:P * t + P, :]).then_inc(x_in[t], 16)
            load(0)
            load(1)
            def dil_merge(half):
                sp_.wait_ge(ds_exp, 6 * half + 6)
                for g in (1, 2):
                    d = scratch[half][g - 1]
                    sp_.dma_start(d.rearrange("(p r) e -> p r e", r=4), dm[:, g, :, :]).then_inc(dstat_out, 16)
                sp_.wait_ge(dstat_out, 32 * half + 32)
                for g in (1, 2):
                    sp_.dma_start(tok[:, :, g - 1, :],
                                  scratch[half][g - 1].rearrange("(i p) e -> p i e", p=P)).then_inc(dstat_in, 16)
                sp_.wait_ge(dw_ready, half + 1)
                for g in (1, 2):
                    sp_.dma_start(scratch[half][g + 1].rearrange("(i p) e -> p i e", p=P),
                                  dw[:, g, :, :]).then_inc(dw_out, 16)
                sp_.wait_ge(dw_out, 32 * half + 32)
                for g in (1, 2):
                    sp_.dma_start(dwl[:, g - 1, :, :],
                                  scratch[half][g + 1].rearrange("(p r) e -> p r e", r=4)).then_inc(dw_in, 16)

            def spread_r(norm):
                sp_.wait_ge(r_ready, norm + 1)
                flat = scratch[2][norm]
                sp_.dma_start(flat.rearrange("(t p) -> p t", p=P), st[:, 3, 0:4],
                              allow_slow_non_contiguous=True).then_inc(r_out, 16)
                sp_.wait_ge(r_out, 16 * norm + 16)
                sp_.dma_start(rrow[:], flat.partition_broadcast(P)).then_inc(r_in, 16)
                if norm == 0:
                    sp_.dma_start(rcol[:], flat.rearrange("(p a) -> p a", a=TT)).then_inc(r_in, 16)

            load(2)
            spread_r(0)
            for kv, w in enumerate((w_ck1, w_cv1)):
                sp_.dma_start(wck[kv][:], w[0].rearrange("(a p) n -> p a n", p=P)).then_inc(wck_in[kv], 16)
            for r in range(2):
                sp_.dma_start(w2k[:, :, r, :], w_ck2[0].rearrange("(m p) d -> p m d", p=P)).then_inc(w2_in, 16)
            sp_.dma_start(w2v[:], w_cv2[0].rearrange("(m p) d -> p m d", p=P)).then_inc(w2_in, 16)

            for job, n in SCHEDULE:
                if job == "tile" and n and TILES[n][1] == 0:
                    load(TILES[n][0] + 2)
                elif job == "dil_merge":
                    dil_merge(n)
            sp_.wait_ge(o_ready, 16)
            for t in range(TT):
                sp_.dma_start(x2[:, t, :], x[0, P * t:P * t + P, :]).then_inc(x2_in, 16)
            sp_.dma_start(gfin[:], norm_final.partition_broadcast(P)).then_inc(gfin_in, 16)
            for u in range(U_UP + 2, U_IN):
                load(u)
            gt_v = w_ffn_in[0].rearrange("(k p) n -> p k n", p=P)

            def load_in(s, j, count):
                sp_.wait_ge(lo_done, count)
                dst = slot_view(raw, s, KC, 256)
                for half in range(2):
                    sp_.dma_start(dst[:, :, P * half:P * half + P],
                                  gt_v[:, :, bass.ds(j * P + FF * half, P)]).then_inc(raw_full[s], 16)

            for s in range(2):
                load_in(s, s, U_IN + s - 1)
            spread_r(1)
            with sp_.Fori(1, FT // 2) as i:
                for s in range(2):
                    load_in(s, i * 2 + s, i * 2 + (U_IN + s - 1))
            wo_v = w_ffn_out[0].rearrange("(u k p) n -> u p k n", p=P, k=2)
            with sp_.Fori(0, FT // 4) as i:
                for s in range(2):
                    sp_.wait_ge(lo_done, i * 2 + (U_OUT + s - 1))
                    dst = slot_view(raw, s, 2, D)
                    for k in range(2):
                        sp_.dma_start(dst[:, k, :], w_ffn_out[0, bass.ds((i * 2 + s) * 256 + P * k, P), :]
                                      ).then_inc(raw_full[s], 16)
            load(N_UNITS - 1)
            for t in range(TT):
                sp_.wait_ge(fin_ready, t + 1)
                sp_.dma_start(out[0, P * t:P * t + P, :], xg[:, t, :]).then_inc(out_done, 16)
            sp_.wait_ge(out_done, 16 * TT)

        @block.gpsimd
        def _(pool):
            steps = [0]

            def link(ins):
                steps[0] += 1
                ins.then_inc(pool_step, 1)
                pool.wait_ge(pool_step, steps[0])

            link(pool.memset(ident[:], 0.0))
            pool.affine_select(out=ident[:], in_=ident[:], compare_op=ALU.not_equal, fill=1.0, base=0,
                               pattern=[[-1, P]], channel_multiplier=1).then_inc(consts_ready, 1)
            pool.iota(dist[:], [[-1, S]], base=384, channel_multiplier=1).then_inc(consts_ready, 1)
            link(pool.memset(cmask[:], 0.0))
            link(pool.affine_select(out=cmask[:], in_=cmask[:], compare_op=ALU.is_ge, fill=NEG, base=384,
                                    pattern=[[-1, S]], channel_multiplier=1))
            pool.affine_select(out=mask0[:], in_=cmask[:, 256:512], compare_op=ALU.is_ge, fill=NEG, base=0,
                               pattern=[[1, 256]], channel_multiplier=-1).then_inc(consts_ready, 1)
            pool.iota(distc[:], [[P, TT], [-16, CMP]], base=-31, channel_multiplier=1).then_inc(consts_ready, 1)
            link(pool.memset(maskc[:], 0.0))
            pool.affine_select(out=maskc[:], in_=maskc[:], compare_op=ALU.is_ge, fill=NEG, base=-31,
                               pattern=[[P, TT], [-16, CMP]], channel_multiplier=1).then_inc(consts_ready, 1)

        @block.scalar
        def _(act):
            def split_hi(u):
                act.wait_ge(raw_full[u % 2], raw_count(u))
                if u >= 2:
                    act.wait_ge(*unit_used(u - 2))
                n = unit_parts(u)[1]
                act.copy(whi[u % 2][:, 0:n], raw[u % 2][:, 0:n]).then_inc(hi_done, 1)

            for row, src in ((0, norm_mix[0]), (8, norm_ffn[0])):
                act.dma_start(crows[row:row + 8, :], src.rearrange("(a b) -> a b", b=P)).then_inc(rows_in, 16)
            for row, src in ((16, pe_k), (32, pe_v)):
                act.dma_start(crows[row:row + PP, :],
                              src[0].rearrange("(a two) d -> a (two d)", two=2)).then_inc(rows_in, 16)
            for t in range(TT):
                act.wait_ge(x_in[t], 16)
                if t >= 2:
                    act.wait_ge(ss_ready, t - 1)
                act.activation(xsq[:, t % 2, :], xs[:, t, :], ACT.Square,
                               accum_out=st[:, 0, t:t + 1]).then_inc(ss_ready, 1)
            act.wait_ge(cvec_ready, 1)

            def turned_hi(k):
                act.wait_ge(n_turned, k + 1)
                act.activation(nhi[:, k, :], ps[k % 4][:], ACT.Copy, scale=cvec[:, k:k + 1]).then_inc(n_hi, 1)

            for k in range(2):
                turned_hi(k)
            act.wait_ge(first_raw, 16)
            act.copy(whi[0][:, 0:1024], raw[0][:, 0:1024]).then_inc(first_hi, 1)
            for k in range(2, 5):
                turned_hi(k)
            act.wait_ge(raw_full[0], 16)
            act.copy(whi[0][:, 1024:2048], raw[0][:, 1024:2048]).then_inc(hi_done, 1)
            for k in range(5, KC):
                turned_hi(k)

            def tile(n):
                u, a = TILES[n]
                if a == 0:
                    split_hi(u + 1)
                if u == U_CMP:
                    return
                b = ps[TILE_BANK[n]]
                if u >= U_GM:
                    act.wait_ge(tile_evac_dve, evac_count(n))
                    f = 2 * (u - U_GM) + a
                    act.activation(gm[:, f, :], gm[:, f, :], ACT.Tanh, scale=0.5).then_inc(gm_tanh, 1)
                elif by_act(n):
                    act.wait_ge(tile_ready, n - 1)
                    if u == U_VB:
                        act.wait_ge(r_in, 32)
                    if u == U_VA:
                        act.activation(gate[:, a, :], b[:, 256:VA_N], ACT.Tanh, scale=rhalf[:, 0, a:a + 1]).then_inc(gate_tanh, 1)
                    dst = va[:, a, :] if u == U_VA else vb[:, u - U_VB, a, :]
                    r_ = st[:, 3, a:a + 1] if u in (U_VB, U_VA) else rcol[:, a:a + 1]
                    act.activation(dst, b[:, 0:256], ACT.Copy, scale=r_).then_inc(tile_evac_act, 1)

            def compress():
                act.wait_ge(h_ready, 1)
                act.activation(th[:], ps[2][:, 0:256], ACT.Tanh, scale=0.5).then_inc(h_tanh, 1)

            def exps(buf, cuts, bias, sums, done):
                for i, (a, b) in enumerate(cuts):
                    ins = act.activation(buf[:, a:b], buf[:, a:b], ACT.Exp, bias=bias[i], accum_out=sums[i])
                ins.then_inc(done, 1)

            def y_split_hi(part):
                if part == 0:
                    act.wait_ge(do_evac, 12)
                    act.wait_ge(s_max, 16)
                    act.wait_ge(t_ready, 48)
                    act.copy(yhi[:, 4:6, :], yb[:]).then_inc(y_hi, 1)
                    act.wait_ge(y_evac, 3)
                    act.copy(yhi[:, 0:3, :], ya[:, 0:3, :]).then_inc(y_hi, 1)
                else:
                    act.wait_ge(y_evac, 4)
                    act.copy(yhi[:, 3, :], ya[:, 3, :]).then_inc(y_hi, 1)

            for job, n in SCHEDULE:
                if job == "tile":
                    tile(n)
                elif job == "cmp_hidden":
                    compress()
                elif job == "dil_scores":
                    m = n % 6
                    g, hh = m // 2, m % 2
                    act.wait_ge(ds_max, n + 1)
                    exps(dp[:, hh, :], dil_cuts(g), [dneg[:, n % 2, i:i + 1] for i in range(TT)],
                         [dm[:, g, i, 2 + hh:3 + hh] for i in range(TT)], ds_exp)
                elif job == "dil_merge":
                    act.wait_ge(de_sub, n + 1)
                    act.activation(de[:], de[:], ACT.Exp).then_inc(de_exp, 1)
                elif job == "dil_turn":
                    act.wait_ge(dt_ready, 2 * n + 1)
                    if n >= 2:
                        act.wait_ge(do_ready, n - 1)
                    act.copy(pt[:, n % 2, 0:512], ps[2][:]).then_inc(dt_evac_act, 1)
                elif job == "cmp_scores":
                    act.wait_ge(cs_sub, 1)
                    act.activation(sc[:], sc[:], ACT.Exp).then_inc(cs_exp, 1)
                elif job == "cmp_turn":
                    for g in range(2):
                        act.wait_ge(ct_ready, g + 1)
                        act.copy(pc_t[:, g, :], ps[2 + g][:]).then_inc(ct_evac, 1)
                elif job == "scores":
                    act.wait_ge(s_max, n + 1)
                    exps(sp[:, n % 2, :], [(Q_OFF[i], Q_OFF[i] + P * (i + 1)) for i in range(TT)],
                         [ust[:, n % 2, 0, i:i + 1] for i in range(TT)],
                         [ust[:, n % 2, 1, i:i + 1] for i in range(TT)], s_exp)
                elif job == "turn":
                    if n >= 2:
                        act.wait_ge(o_ready, n - 1)
                    act.wait_ge(t_ready, 3 * n + 1)
                    act.copy(pt[:, n % 2, 0:512], ps[3][:])
                    act.wait_ge(t_ready, 3 * n + 3)
                    act.copy(pt[:, n % 2, 1024:1280], ps[5][:, 0:256]).then_inc(t_evac_act, 1)
                    if n == 15:
                        y_split_hi(0)
                elif job == "out" and n % 4 == 3:
                    act.wait_ge(o_ready, n + 1)
                    act.copy(ya[:, n // 4, :], ps[6][:]).then_inc(y_evac, 1)
                    if n == 15:
                        y_split_hi(1)

            for f in range(KC):
                if f % 2 == 0:
                    split_hi(U_UP + f // 2 + 1)
                act.wait_ge(m_sum, f + 1)
                act.copy(mhi[:, f, :], mt[:, f % 2, 2, :]).then_inc(m_hi, 1)
            for u in range(U_WO + 1, U_IN + 1):
                split_hi(u)

            for t in range(TT):
                for half in range(2):
                    act.wait_ge(h_turned, 2 * t + half + 1)
                    for k in range(4 * half, 4 * half + 4):
                        ins = act.activation(hhi[:, k, P * t:P * t + P], ps[2 * t + half][:, P * (k % 4):P * (k % 4) + P],
                                             ACT.Copy, scale=cvec[:, 8 + k:9 + k])
                    ins.then_inc(h_hi, 1)
                act.wait_ge(x2_sum, 2 * t + 2)
                if t >= 1:
                    act.wait_ge(x2_ss, t)
                act.activation(sq[:], x2[:, t, :], ACT.Square, accum_out=st[:, 1, t:t + 1]).then_inc(x2_ss, 1)

            def ffn_in(i, s):
                o = 1 - s
                act.wait_ge(raw_full[o], i * 32 + (raw_count(U_IN + 1 + s)))
                act.wait_ge(gu_ready, i * 2 + (s + 1))
                act.copy(whi[o][:, 0:2048], raw[o][:, 0:2048]).then_inc(hi_done, 1)

            def tanh_gate(i, s):
                act.wait_ge(g_scaled, i * 2 + (s + 1))
                act.wait_ge(gt_mul, i * 2 + (s + 1))
                act.activation(tg[:, s, :], gs[:, s, :], ACT.Tanh, scale=0.5).then_inc(gu_tanh, 1)

            with act.Fori(0, FT // 2 - 1) as i:
                for s in range(2):
                    ffn_in(i, s)
                    tanh_gate(i, s)
            for s in range(2):
                ffn_in(FT // 2 - 1, s)
                if s:
                    act.copy(ahi[:, 0, :, :], actt[:, 0:2, :]).then_inc(a_hi, 1)
                tanh_gate(FT // 2 - 1, s)

            act.wait_ge(gu_free, 24)
            with act.Fori(0, FT // 4) as i:
                for s in range(2):
                    o = 1 - s
                    act.wait_ge(w_used, i * 2 + (s + 3))
                    act.copy(ahi[:, o, :, :], actt[:, bass.ds(i * 4 + (2 * s + 2), 2), :]).then_inc(a_hi, 1)
                    act.wait_ge(raw_full[o], i * 32 + raw_count(U_OUT + 1 + s))
                    act.copy(whi[o][:, 0:2048], raw[o][:, 0:2048]).then_inc(hi_done, 1)
            for t in range(TT):
                act.wait_ge(x3_sum, 2 * t + 2)
                if t >= 1:
                    act.wait_ge(x3_ss, t)
                act.activation(sq[:], x2[:, t, :], ACT.Square, accum_out=st[:, 2, t:t + 1]).then_inc(x3_ss, 1)

        @block.vector
        def _(dve):
            steps = [0]

            def link(ins):
                steps[0] += 1
                ins.then_inc(dve_step, 1)
                dve.wait_ge(dve_step, steps[0])

            def split_lo(u):
                dve.wait_ge(hi_done, u + 1)
                n = unit_parts(u)[1]
                dve.tensor_tensor(wlo[u % 2][:, 0:n], raw[u % 2][:, 0:n], whi[u % 2][:, 0:n].bitcast(F32),
                                  ALU.subtract).then_inc(lo_done, 1)

            def rsqrt(ss, v, y, t1, done=None):
                link(dve.tensor_scalar(v, ss, 1.0 / D, EPS, ALU.mult, ALU.add))
                link(dve.tensor_scalar(t1.bitcast(I32), v.bitcast(I32), 1, None, ALU.logical_shift_right))
                link(dve.tensor_scalar(y.bitcast(I32), t1.bitcast(I32), -1.0, float(0x5F3759DF), ALU.mult, ALU.add))
                for step in range(3):
                    link(dve.tensor_tensor(t1, y, y, ALU.mult))
                    link(dve.scalar_tensor_tensor(out=t1, in0=t1, scalar=-0.5, in1=v, op0=ALU.mult, op1=ALU.mult))
                    last = dve.scalar_tensor_tensor(out=y, in0=t1, scalar=1.5, in1=y, op0=ALU.add, op1=ALU.mult)
                    if done and step == 2:
                        last.then_inc(done[0], 1)
                        dve.wait_ge(*done)
                    else:
                        link(last)

            dve.wait_ge(rows_turned, 1)
            dve.tensor_copy(cvec[:], ps[4][:, 0:48]).then_inc(cvec_ready, 1)
            dve.wait_ge(cvec_ready, 1)

            for k in range(KC):
                dve.wait_ge(n_hi, k + 1)
                dve.scalar_tensor_tensor(out=nlo[:, k, :], in0=ps[k % 4][:], scalar=cvec[:, k:k + 1],
                                         in1=nhi[:, k, :].bitcast(F32), op0=ALU.mult, op1=ALU.subtract).then_inc(n_lo, 1)
                if k in (1, 4):
                    c = slice(0, 1024) if k == 1 else slice(1024, 2048)
                    dve.wait_ge(first_hi if k == 1 else hi_done, 1)
                    dve.tensor_tensor(wlo[0][:, c], raw[0][:, c], whi[0][:, c].bitcast(F32),
                                      ALU.subtract).then_inc(first_lo if k == 1 else lo_done, 1)
            dve.wait_ge(ss_ready, TT)
            rsqrt(st[:, 0, 0:4], st[:, 0, 4:8], st[:, 3, 0:4], st[:, 3, 4:8], (r_ready, 1))
            dve.tensor_scalar(rhalf[:, 0, :], st[:, 3, 0:4], 0.5, None, ALU.mult)

            def turned_lo(lo, hi, bank, gain, t, half, done):
                for k in range(4 * half, 4 * half + 4):
                    ins = dve.scalar_tensor_tensor(
                        out=lo[:, k, P * t:P * t + P], in0=bank[:, P * (k % 4):P * (k % 4) + P],
                        scalar=gain[:, k:k + 1], in1=hi[:, k, P * t:P * t + P].bitcast(F32),
                        op0=ALU.mult, op1=ALU.subtract)
                ins.then_inc(done, 1)

            def dil_bias():
                dve.wait_ge(consts_ready, 5)
                m2i = mask2[:].bitcast(I32)
                link(dve.tensor_scalar(m2i, dist[:, 384:512], 3, None, ALU.bitwise_and))
                link(dve.tensor_scalar(mask2[:], m2i, 0.0, NEG, ALU.is_gt, ALU.mult))
                link(dve.tensor_tensor(mask2[:], mask2[:], cmask[:, 384:512], ALU.add))
                for h in range(4):
                    for g, (a, b, mask) in enumerate(((0, 256, mask0[:]), (256, 384, cmask[:, 384:512]), (384, 512, mask2[:]))):
                        ins = dve.scalar_tensor_tensor(
                            out=dbias[:, h, a:b], in0=dist[:, 512 - (b - a):512],
                            scalar=-SLOPE_DIL[g][h] * min(DIL[g], 4), in1=mask, op0=ALU.mult, op1=ALU.add)
                link(ins)

            def cmp_bias():
                for h in range(NH):
                    ins = dve.scalar_tensor_tensor(out=cbias[:, :, h, :], in0=distc[:], scalar=-SLOPE_NSA[h],
                                                   in1=maskc[:], op0=ALU.mult, op1=ALU.add)
                link(ins)

            def nsa_bias():
                dve.wait_ge(dt_ready, 24)
                for h in range(NH):
                    ins = dve.scalar_tensor_tensor(out=nbias[:, h, :], in0=dist[:], scalar=-SLOPE_NSA[h],
                                                   in1=cmask[:], op0=ALU.mult, op1=ALU.add)
                link(ins)

            def tile(n):
                u, a = TILES[n]
                if a == 0:
                    split_lo(u + 1)
                if u == U_CMP:
                    if a == 0:
                        link(dve.memset(blk[0][:], 0.0))
                        link(dve.memset(blk[1][:], 0.0))
                    dve.wait_ge(cmp_tile_ready, a + 1)
                    if a == 0:
                        dve.wait_ge(r_in, 32)
                    link(dve.tensor_tensor(ctmp[:, a, :], ps[4 + a][:], rrow[:], ALU.mult))
                    for g in range(2):
                        for s in range(2):
                            rows = slice(HD * s, HD * s + HD)
                            src = ctmp[HD * g:HD * g + HD, a, :].rearrange("p (c q s) -> p s q c", q=8, s=2)[:, s]
                            code = cvec[rows, 16 + PP * a:32 + PP * a].rearrange("p (b q) -> p b q", q=8)
                            for b in range(2):
                                ins = dve.tensor_tensor(
                                    blk[a][rows, 8 * b:8 * b + 8, g, 0:31], src[:, :, b:b + 31],
                                    code[:, b, :].unsqueeze(2).to_broadcast([HD, 8, 31]), ALU.add)
                    ins.then_inc(blk_ready, 1)
                elif u == U_VA:
                    dve.wait_ge(gate_tanh, a + 1)
                    dve.tensor_scalar(gate[:, a, :], gate[:, a, :], 0.5, 0.5, ALU.mult, ALU.add).then_inc(gate_ready, 1)
                elif not by_act(n):
                    dve.wait_ge(tile_ready, n - 1)
                    src, row = ps[TILE_BANK[n]][:], rrow[:]
                    if u < U_VB:
                        g = (u - U_QB) % 3
                        dst = (qb if u < U_KB else kb)[:, 2 * g + a, :]
                        if g:
                            dst = dst.rearrange("p (r t) -> p r t", r=4)
                            src, row = (v.rearrange("p (t r) -> p r t", r=4) for v in (src, row))
                    elif u < U_KA:
                        dst = qa[:, 2 * (u - U_QA) + a, :]
                    elif u == U_KA:
                        dst = ka[:, a, :]
                    else:
                        dst = gm[:, 2 * (u - U_GM) + a, :]
                    scale = QSCALE if u < U_KB or U_QA <= u < U_KA else 1.0
                    dve.scalar_tensor_tensor(out=dst, in0=src, scalar=scale, in1=row,
                                             op0=ALU.mult, op1=ALU.mult).then_inc(tile_evac_dve, 1)

            def compress():
                dve.wait_ge(h_tanh, 1)
                dve.scalar_tensor_tensor(out=hs[:].rearrange("p a b -> p (a b)"), in0=th[:], scalar=1.0,
                                         in1=ps[2][:, 0:256], op0=ALU.add, op1=ALU.mult).then_inc(hs_ready, 1)

            def cmp_kv():
                dve.wait_ge(kv_ready, 1)
                dve.tensor_scalar(kc[:], ps[3][:, 0:2 * CMP], 0.5, None, ALU.mult).then_inc(kv_evac, 1)
                dve.wait_ge(kv_ready, 2)
                dve.tensor_scalar(vc[:].rearrange("p g d -> p (g d)"), ps[3][:, 128:256], 0.5, None, ALU.mult).then_inc(kv_evac, 1)
                dil_bias()

            def dil_scores(n):
                m = n % 6
                g, hh = m // 2, m % 2
                h = 2 * (n // 6) + hh
                dve.wait_ge(ds_ready, n + 1)
                if n >= 6:
                    dve.wait_ge(dt_ready, 2 * (n - 6) + 2)
                if n >= 2:
                    dve.wait_ge(ds_exp, n - 1)
                for i in range(TT):
                    a, b = dil_cuts(g)[i]
                    bank, c = B_PLACE[i] if g == 0 else (0, P * i)
                    base = (0, 256, 384)[g]
                    end = base + (256 if g == 0 else P)
                    ins = dve.tensor_tensor_reduce(
                        dp[:, hh, a:b], ps[bank][:, c:c + b - a], dbias[:, h, end - (b - a):end], 1.0, NEG,
                        ALU.add, ALU.max, dm[:, g, i, hh:hh + 1])
                link(ins)
                dve.tensor_scalar(dneg[:, n % 2, :], dm[:, g, :, hh], -1.0, None, ALU.mult).then_inc(ds_max, 1)

            def dil_merge(half):
                dve.wait_ge(ds_exp, 6 * half + 6)
                dve.wait_ge(dstat_in, 32 * half + 32)
                stat = [dm[:, 0, :, :], tok[:, :, 0, :], tok[:, :, 1, :]]
                link(dve.tensor_tensor(dmx[:, 0], stat[0][:, :, 0:2], stat[1][:, :, 0:2], ALU.max))
                link(dve.tensor_tensor(dmx[:, 1], stat[2][:, :, 0:2], dmx[:, 0], ALU.max))
                for g in range(NG):
                    ins = dve.tensor_tensor(de[:, g], stat[g][:, :, 0:2], dmx[:, 1], ALU.subtract)
                ins.then_inc(de_sub, 1)
                dve.wait_ge(de_exp, half + 1)
                for g in range(NG):
                    link(dve.tensor_tensor(dz[:, g], stat[g][:, :, 2:4], de[:, g], ALU.mult))
                link(dve.tensor_tensor(dmx[:, 0], dz[:, 0], dz[:, 1], ALU.add))
                link(dve.tensor_tensor(dmx[:, 1], dz[:, 2], dmx[:, 0], ALU.add))
                link(dve.reciprocal(dmx[:, 2], dmx[:, 1]))
                if half:
                    dve.wait_ge(dw_out, 32)
                for g in range(NG):
                    ins = dve.tensor_tensor(dw[:, g], de[:, g], dmx[:, 2], ALU.mult)
                ins.then_inc(dw_ready, 1)

            def dil_scale(n):
                m = n % 6
                g, hh = m // 2, m % 2
                if m == 0:
                    dve.wait_ge(dw_ready, n // 6 + 1)
                if m == 2:
                    dve.wait_ge(dw_in, 32 * (n // 6) + 32)
                for i, (a, b) in enumerate(dil_cuts(g)):
                    w = dw[:, 0, i, hh:hh + 1] if g == 0 else dwl[:, g - 1, i, hh:hh + 1]
                    ins = dve.tensor_scalar(dp[:, hh, a:b], dp[:, hh, a:b], w, None, ALU.mult)
                ins.then_inc(dp_ready, 1)

            def dil_turn(n):
                if n % 6 == 0:
                    dil_scale(n)
                if n % 6 < 5:
                    dil_scale(n + 1)
                if (n % 6) // 2 == 0:
                    dve.wait_ge(dt_ready, 2 * n + 2)
                    if n >= 2:
                        dve.wait_ge(do_ready, n - 1)
                    dve.tensor_copy(pt[:, n % 2, 512:896], ps[3][:, 0:384]).then_inc(dt_evac_dve, 1)

            def dil_out(n):
                m = n % 6
                g, hh = m // 2, m % 2
                dve.wait_ge(do_ready, n + 1)
                rows = slice(HD * hh, HD * hh + HD)
                y = yb[rows, n // 6, :]
                o = ps[4 + n % 2][rows, :]
                if g == 0:
                    dve.tensor_copy(y, o).then_inc(do_evac, 1)
                else:
                    dve.wait_ge(do_evac, n - 1)
                    yv = y.rearrange("p (t r) -> p r t", r=4)
                    dve.tensor_tensor(yv, o.rearrange("p (r t) -> p r t", r=4), yv, ALU.add).then_inc(do_evac, 1)

            def cmp_scores():
                cmp_bias()
                dve.wait_ge(cs_ready, 1)
                for b in range(2):
                    ins = dve.tensor_tensor(sc[:, :, 4 * b:4 * b + 4].rearrange("p i h n -> p i (h n)"),
                                            ps[b][:].rearrange("p (i q) -> p i q", i=TT),
                                            cbias[:, :, 4 * b:4 * b + 4].rearrange("p i h n -> p i (h n)"), ALU.add)
                ins.then_inc(cs_added, 1)
                dve.wait_ge(cs_added, 1)
                s3 = sc[:].rearrange("p i h n -> p (i h) n")
                link(dve.tensor_reduce(cst[:, 0], s3, AX.X, ALU.max))
                link(dve.tensor_scalar(cst[:, 0], cst[:, 0], NEG / 10, None, ALU.max))
                dve.tensor_tensor(s3, s3, cst[:, 0].unsqueeze(2).to_broadcast([P, 32, CMP]),
                                  ALU.subtract).then_inc(cs_sub, 1)
                dve.wait_ge(cs_exp, 1)
                link(dve.tensor_reduce(cst[:, 1], s3, AX.X, ALU.add))
                link(dve.tensor_scalar(cst[:, 1], cst[:, 1], TINY, None, ALU.max))
                link(dve.reciprocal(cst[:, 0], cst[:, 1]))
                dve.wait_ge(gate_ready, TT)
                c0 = cst[:, 0].rearrange("p (i h) -> p i h", i=TT)
                g0 = gate[:].rearrange("p i (h b) -> p i h b", b=3)
                link(dve.tensor_tensor(cst[:, 1].rearrange("p (i h) -> p i h", i=TT), c0, g0[:, :, :, 0], ALU.mult))
                dve.tensor_tensor(s3, s3, cst[:, 1].unsqueeze(2).to_broadcast([P, 32, CMP]),
                                  ALU.mult).then_inc(cp_ready, 1)

            def scores(n):
                j, b, g = n // 4, n // 2 % 2, n % 2
                h = j + 4 * g
                dve.wait_ge(s_ready, n + 1)
                if n >= 2:
                    dve.wait_ge(t_ready, 3 * (n - 1))
                for i in range(TT):
                    bank, c = S_PLACE[i]
                    w = P * (i + 1)
                    ins = dve.tensor_tensor_reduce(
                        sp[:, n % 2, Q_OFF[i]:Q_OFF[i] + w], ps[bank][:, c:c + w], nbias[:, h, 384 - P * i:512],
                        1.0, NEG, ALU.add, ALU.max, umx[:, n % 2, i:i + 1])
                link(ins)
                dve.tensor_scalar(ust[:, n % 2, 0, :], umx[:, n % 2, :], -1.0, None, ALU.mult).then_inc(s_max, 1)

            def scale(n):
                j, b, g = n // 4, n // 2 % 2, n % 2
                h = j + 4 * g
                dve.wait_ge(s_exp, n + 1)
                link(dve.reciprocal(ust[:, n % 2, 2, :], ust[:, n % 2, 1, :]))
                link(dve.tensor_tensor(ust[:, n % 2, 3, :], ust[:, n % 2, 2, :], gate[:, :, 3 * h + 1 + b], ALU.mult))
                for i in range(TT):
                    q = sp[:, n % 2, Q_OFF[i]:Q_OFF[i] + P * (i + 1)]
                    ins = dve.tensor_scalar(q, q, ust[:, n % 2, 3, i:i + 1], None, ALU.mult)
                ins.then_inc(p_ready, 1)

            def turn(n):
                if n >= 2:
                    dve.wait_ge(o_ready, n - 1)
                dve.wait_ge(t_ready, 3 * n + 2)
                dve.tensor_copy(pt[:, n % 2, 512:1024], ps[4][:]).then_inc(t_evac_dve, 1)

            def y_split_lo(part):
                for k in ((0, 1), (2,))[part]:
                    a, b, src = ((4, 6, yb[:]), (0, 3, ya[:, 0:3, :]), (3, 4, ya[:, 3:4, :]))[k]
                    dve.wait_ge(y_hi, k + 1)
                    dve.tensor_tensor(ylo[:, a:b, :], src, yhi[:, a:b, :].bitcast(F32), ALU.subtract).then_inc(y_lo, 1)

            for job, n in SCHEDULE:
                if job == "tile":
                    tile(n)
                elif job == "cmp_hidden":
                    compress()
                elif job == "cmp_kv":
                    cmp_kv()
                elif job == "dil_scores":
                    dil_scores(n)
                elif job == "dil_merge":
                    dil_merge(n)
                elif job == "dil_turn":
                    dil_turn(n)
                elif job == "dil_out":
                    dil_out(n)
                elif job == "cmp_scores":
                    cmp_scores()
                elif job == "nsa_bias":
                    nsa_bias()
                elif job == "scores":
                    scores(n)
                    if n == 0:
                        scale(0)
                elif job == "turn":
                    turn(n)
                    if n < 15:
                        scale(n + 1)
                    else:
                        y_split_lo(0)
                elif job == "out" and n == 15:
                    y_split_lo(1)

            for f in range(KC):
                if f % 2 == 0:
                    split_lo(U_UP + f // 2 + 1)
                dve.wait_ge(ab_ready, f + 1)
                if f == 0:
                    dve.wait_ge(gm_tanh, 2 * KC)
                if f >= 2:
                    dve.wait_ge(m_hi, f - 1)
                    dve.wait_ge(m_lo, f - 1)
                for k in range(2):
                    ins = dve.scalar_tensor_tensor(out=mt[:, f % 2, k, :], in0=gm[:, 8 * k + f, :], scalar=1.0,
                                                   in1=ps[2 * (f % 2) + k][:], op0=ALU.add, op1=ALU.mult)
                link(ins)
                dve.tensor_tensor(mt[:, f % 2, 2, :], mt[:, f % 2, 0, :], mt[:, f % 2, 1, :], ALU.add).then_inc(m_sum, 1)
                dve.wait_ge(m_hi, f + 1)
                dve.tensor_tensor(mlo[:, f, :], mt[:, f % 2, 2, :], mhi[:, f, :].bitcast(F32),
                                  ALU.subtract).then_inc(m_lo, 1)
            for u in range(U_WO + 1, U_IN + 1):
                split_lo(u)

            dve.wait_ge(x2_in, 16 * TT)

            def residual(t, factor, ready, done):
                for half in range(2):
                    dve.wait_ge(ready, 2 * t + half + 1)
                    q = x2[:, t, 512 * half:512 * half + 512]
                    dve.scalar_tensor_tensor(out=q, in0=ps[2 * t + half][:], scalar=factor, in1=q,
                                             op0=ALU.mult, op1=ALU.add).then_inc(done, 1)

            def h_low(t):
                for half in range(2):
                    dve.wait_ge(h_hi, 2 * t + half + 1)
                    turned_lo(hlo, hhi, ps[2 * t + half], cvec[:, 8:16], t, half, h_lo)

            for t in range(TT):
                residual(t, 0.5, wo_ready, x2_sum)
                if t:
                    h_low(t - 1)
            h_low(TT - 1)
            dve.wait_ge(x2_ss, TT)
            rsqrt(st[:, 1, 0:4], st[:, 1, 4:8], st[:, 3, 0:4], st[:, 3, 4:8], (r_ready, 2))
            link(dve.tensor_scalar(rhalf[:, 1, :], st[:, 3, 0:4], 0.5, None, ALU.mult))

            dve.sem_inc(gt_mul, 2)
            dve.sem_inc(gu_free, 2)

            def ffn_in_lo(i, s):
                o = 1 - s
                dve.wait_ge(hi_done, i * 2 + (U_IN + 2 + s))
                dve.tensor_tensor(wlo[o][:, 0:2048], raw[o][:, 0:2048], whi[o][:, 0:2048].bitcast(F32),
                                  ALU.subtract).then_inc(lo_done, 1)

            def ffn_in_act(i, s):
                dve.wait_ge(gu_ready, i * 2 + (s + 2))
                dve.wait_ge(gu_tanh, i * 2 + (s + 1))
                dve.tensor_tensor(gs[:, s, :], ps[2 * s][:], rrow[:], ALU.mult).then_inc(g_scaled, 1)
                dve.wait_ge(gu_tanh, i * 2 + (s + 3))
                dve.wait_ge(gu_free, i * 2 + (s + 1))
                dve.scalar_tensor_tensor(out=tm[:, s, :], in0=tg[:, s, :], scalar=1.0, in1=gs[:, s, :],
                                         op0=ALU.add, op1=ALU.mult).then_inc(gt_mul, 1)
                dve.wait_ge(gt_mul, i * 2 + (s + 3))
                dve.tensor_tensor(actt[:, i * 2 + s, :], ps[2 * s + 1][:], tm[:, s, :],
                                  ALU.mult).then_inc(gu_free, 1)

            dve.sem_inc(gu_tanh, 2)
            dve.wait_ge(r_in, 48)
            with dve.Fori(0, FT // 2 - 1) as i:
                for s in range(2):
                    ffn_in_lo(i, s)
                    ffn_in_act(i, s)
            for s in range(2):
                ffn_in_lo(FT // 2 - 1, s)
                if s:
                    dve.wait_ge(a_hi, 1)
                    dve.tensor_tensor(alo[:, 0, :, :], actt[:, 0:2, :], ahi[:, 0, :, :].bitcast(F32),
                                      ALU.subtract).then_inc(a_lo, 1)
                ffn_in_act(FT // 2 - 1, s)

            dve.wait_ge(gu_free, 24)
            with dve.Fori(0, FT // 4) as i:
                for s in range(2):
                    o = 1 - s
                    dve.wait_ge(a_hi, i * 2 + (s + 2))
                    dve.tensor_tensor(alo[:, o, :, :], actt[:, bass.ds(i * 4 + (2 * s + 2), 2), :],
                                      ahi[:, o, :, :].bitcast(F32), ALU.subtract).then_inc(a_lo, 1)
                    dve.wait_ge(hi_done, i * 2 + (U_OUT + 2 + s))
                    dve.tensor_tensor(wlo[o][:, 0:2048], raw[o][:, 0:2048], whi[o][:, 0:2048].bitcast(F32),
                                      ALU.subtract).then_inc(lo_done, 1)
            dve.wait_ge(gfin_in, 16)
            dve.wait_ge(h_lo, 2 * TT)
            for pair in range(2):
                for t in (2 * pair, 2 * pair + 1):
                    residual(t, rhalf[:, 1, t:t + 1], fo_ready, x3_sum)
                    dve.wait_ge(x3_sum, 2 * t + 2)
                    ins = dve.tensor_tensor(xg[:, t, :], x2[:, t, :], gfin[:], ALU.mult)
                link(ins)
                dve.wait_ge(x3_ss, 2 * pair + 2)
                a = 2 * pair
                rsqrt(st[:, 2, a:a + 2], st[:, 2, 4 + a:6 + a], st[:, 3, a:a + 2], st[:, 3, 4 + a:6 + a])
                for t in (a, a + 1):
                    dve.tensor_scalar(xg[:, t, :], xg[:, t, :], st[:, 3, t:t + 1], None, ALU.mult).then_inc(fin_ready, 1)

        @block.tensor
        def _(pe):
            def split_product(dst, w, x_, start, stop):
                pe.matmul(dst, w[0], x_[0], start=start, stop=False)
                pe.matmul(dst, w[0], x_[1], start=False, stop=False)
                return pe.matmul(dst, w[1], x_[0], start=False, stop=stop)

            def turn_rows(src, t, half, banks, done):
                for k in range(4 * half, 4 * half + 4):
                    ins = pe.transpose(ps[banks][:, P * (k % 4):P * (k % 4) + P], src[:, P * k:P * k + P], ident[:])
                ins.then_inc(done, 1)

            pe.wait_ge(rows_in, 64)
            pe.wait_ge(consts_ready, 1)
            pe.transpose(ps[4][:, 0:48], crows[0:48, :], ident[0:48, 0:48]).then_inc(rows_turned, 1)

            def turn_x(k):
                if k >= 4:
                    pe.wait_ge(n_lo, k - 3)
                for t in range(TT):
                    if k == 0:
                        pe.wait_ge(x_in[t], 16)
                    ins = pe.transpose(ps[k % 4][:, P * t:P * t + P], xs[:, t, P * k:P * k + P], ident[:])
                ins.then_inc(n_turned, 1)

            for k in range(4):
                turn_x(k)
            pe.wait_ge(cvec_ready, 1)

            def token_cols(n_, k, g, a):
                if g == 0:
                    return n_[:, k, P * a:P * a + P]
                return n_[:, k, :].rearrange("p (t r) -> p r t", r=4)[:, a]

            def tile_evacuated(n):
                pe.wait_ge(tile_evac_act if by_act(n) else tile_evac_dve, evac_count(n))

            def tile(n):
                u, a = TILES[n]
                if a == 0 and n:
                    pe.wait_ge(hi_done, u + 1)
                    pe.wait_ge(lo_done, u + 1)
                bank = TILE_BANK[n]
                before = [v for v in range(2, n) if TILE_BANK[v] == bank]
                if before:
                    tile_evacuated(before[-1])
                natural = U_VB <= u < U_QA or u == U_VA
                w = [slot_view(r, u, KC, VA_N if u == U_VA else 256) for r in (whi, wlo)]
                for k in range(KC):
                    if n == 0:
                        if k % 4 == 0:
                            pe.wait_ge(lo_done if k else first_lo, 1)
                        pe.wait_ge(n_lo, k + 1)
                        if k < 4:
                            turn_x(k + 4)
                    if natural:
                        g = 0 if u == U_VA else u - U_VB
                        cols = VA_N if u == U_VA else 256
                        ins = split_product(ps[bank][:, 0:cols], [token_cols(v, k, g, a) for v in (nhi, nlo)],
                                            [v[:, k, :] for v in w], k == 0, k == KC - 1)
                    else:
                        wk = [v[:, k, P * a:P * a + P] for v in w]
                        ins = split_product(ps[bank][:], wk, (nhi[:, k, :], nlo[:, k, :]), k == 0, k == KC - 1)
                ins.then_inc(cmp_tile_ready if u == U_CMP else tile_ready, 1)

            def compress():
                for kv in range(2):
                    pe.wait_ge(wck_in[kv], 16)
                    pe.wait_ge(blk_ready, kv + 1)
                    for m in range(2):
                        o = ps[2][:, 64 * (2 * kv + m):64 * (2 * kv + m) + 64]
                        for q in range(PP):
                            ins = pe.matmul(o, wck[kv][:, q, P * m:P * m + P], blk[kv][:, q].rearrange("p g c -> p (g c)"),
                                            start=(q == 0), stop=(q == PP - 1))
                ins.then_inc(h_ready, 1)

            def cmp_kv():
                pe.wait_ge(w2_in, 48)
                pe.wait_ge(hs_ready, 1)
                for m in range(2):
                    ins = pe.matmul(ps[3][:, 0:64], w2k[:, m].rearrange("p r d -> p (r d)"), hs[:, m, :],
                                    start=(m == 0), stop=(m == 1))
                ins.then_inc(kv_ready, 1)
                pe.wait_ge(kv_evac, 1)
                for g in range(2):
                    for r in range(4):
                        for m in range(2):
                            ins = pe.matmul(ps[3][32 * r:32 * r + 32, 128 + HD * g:128 + HD * g + HD],
                                            hs[:, 2 + m, CMP * g:CMP * g + CMP], w2v[:, m, :],
                                            start=(m == 0), stop=(m == 1))
                ins.then_inc(kv_ready, 1)

            def dil_scores(n):
                m = n % 6
                g, hh, t = m // 2, m % 2, n // 6
                tile_evacuated(LAST_TILE[U_KB + 2])
                if n:
                    pe.wait_ge(ds_max, n)
                rows = slice(HD * hh, HD * hh + HD)
                q, k = qb[rows, 2 * g + t, :], kb[rows, 2 * g + t, :]
                for i in range(TT):
                    lo = P * (i - 1) if g == 0 and i else P * i
                    bank, c = B_PLACE[i] if g == 0 else (0, P * i)
                    ins = pe.matmul(ps[bank][:, c:c + P * (i + 1) - lo], q[:, P * i:P * i + P], k[:, lo:P * (i + 1)],
                                    start=True, stop=True)
                ins.then_inc(ds_ready, 1)

            def dil_evacuated(n):
                pe.wait_ge(dt_evac_act, n + 1)
                pe.wait_ge(dt_evac_dve, sum(v % 6 < 2 for v in range(n + 1)))

            def dil_turn(n):
                m = n % 6
                g, hh = m // 2, m % 2
                pe.wait_ge(dp_ready, n + 1)
                if n:
                    dil_evacuated(n - 1)
                if n == 0:
                    pe.wait_ge(kv_evac, 2)
                if n == 6:
                    pe.wait_ge(ct_evac, 2)
                p_ = dp[:, hh, :]
                if g == 0:
                    for j in range(TT):
                        bank, c = ps[2 + j // 2], 256 * (j % 2)
                        a = B_OFF[j] + (P if j else 0)
                        ins = pe.transpose(bank[:, c:c + P], p_[:, a:a + P], ident[:])
                        if j < 3:
                            ins = pe.transpose(bank[:, c + P:c + 256], p_[:, B_OFF[j + 1]:B_OFF[j + 1] + P], ident[:])
                        if j % 2:
                            ins.then_inc(dt_ready, 1)
                else:
                    a = dil_cuts(g)[0][0]
                    for i in range(TT):
                        ins = pe.transpose(ps[2][:, P * i:P * i + P], p_[:, a + P * i:a + P * i + P], ident[:])
                    ins.then_inc(dt_ready, 2)

            def dil_out(n):
                m = n % 6
                g, hh, t = m // 2, m % 2, n // 6
                dil_evacuated(n)
                if n >= 2:
                    pe.wait_ge(do_evac, n - 1)
                rows = slice(HD * hh, HD * hh + HD)
                h = 2 * t + hh
                o = ps[4 + n % 2]
                for i in range(TT):
                    q = slice(P * i, P * i + P)
                    if g == 0 and i:
                        pe.matmul(o[rows, q], vb[:, g, i - 1, HD * h:HD * h + HD], pt[:, n % 2, 256 * (i - 1) + P:256 * i], start=True, stop=False)
                    c = 256 * i if g == 0 else P * i
                    ins = pe.matmul(o[rows, q], vb[:, g, i, HD * h:HD * h + HD], pt[:, n % 2, c:c + P], start=not (g == 0 and i), stop=True)
                ins.then_inc(do_ready, 1)

            def cmp_scores():
                pe.wait_ge(ds_max, 12)
                for i in range(TT):
                    for h in range(NH):
                        g, j = h // 4, h % 4
                        rows = slice(HD * g, HD * g + HD)
                        c = P * i + CMP * j
                        ins = pe.matmul(ps[g][:, c:c + CMP], qa[rows, j, P * i:P * i + P],
                                        kc[rows, CMP * g:CMP * g + CMP], start=True, stop=True)
                ins.then_inc(cs_ready, 1)

            def cmp_turn():
                pe.wait_ge(cp_ready, 1)
                dil_evacuated(5)
                for g in range(2):
                    for i in range(TT):
                        ins = pe.transpose(ps[2 + g][:, P * i:P * i + P],
                                           sc[:, i, 4 * g:4 * g + 4, :].rearrange("p h n -> p (h n)"), ident[:])
                    ins.then_inc(ct_ready, 1)

            def scores(n):
                j, b, g = n // 4, n // 2 % 2, n % 2
                if n == 0:
                    pe.wait_ge(cs_added, 1)
                else:
                    pe.wait_ge(s_max, n)
                rows = slice(HD * g, HD * g + HD)
                for i in range(TT):
                    bank, c = S_PLACE[i]
                    ins = pe.matmul(ps[bank][:, c:c + P * (i + 1)], qa[rows, j, P * i:P * i + P],
                                    ka[rows, b, 0:P * (i + 1)], start=True, stop=True)
                ins.then_inc(s_ready, 1)

            def turn(n):
                pe.wait_ge(p_ready, n + 1)
                if n:
                    pe.wait_ge(t_evac_act, n)
                    pe.wait_ge(t_evac_dve, n)
                else:
                    pe.wait_ge(do_evac, 12)
                    pe.wait_ge(ct_evac, 2)
                for js in ((0,), (1, 3), (2,)):
                    for j in js:
                        bank, c = K_PLACE[j]
                        for i in range(j, TT):
                            a = Q_OFF[i] + P * j
                            ins = pe.transpose(ps[bank][:, c + P * (i - j):c + P * (i - j) + P],
                                               sp[:, n % 2, a:a + P], ident[:])
                    ins.then_inc(t_ready, 1)

            def out_(n):
                j, b, g = n // 4, n // 2 % 2, n % 2
                pe.wait_ge(t_evac_act, n + 1)
                pe.wait_ge(t_evac_dve, n + 1)
                rows = slice(HD * g, HD * g + HD)
                o = ps[6]
                if b == 0:
                    if n == 0:
                        tile_evacuated(max(v for v in TILE_BANK if TILE_BANK[v] == 6))
                    if n % 4 == 0 and n:
                        pe.wait_ge(y_evac, n // 4)
                    pe.matmul(o[rows, :], vc[CMP * j:CMP * j + CMP, g, :], pc_t[CMP * j:CMP * j + CMP, g, :],
                              start=True, stop=False)
                for k in range(TT):
                    ins = pe.matmul(o[rows, P * k:], va[:, k, 128 * b + HD * g:128 * b + HD * g + HD],
                                    pt[:, n % 2, K_OFF[k]:K_OFF[k] + P * (TT - k)],
                                    start=False, stop=(b == 1 and k == TT - 1))
                ins.then_inc(o_ready, 1)

            for job, n in SCHEDULE:
                if job == "tile":
                    tile(n)
                elif job == "cmp_hidden":
                    compress()
                elif job == "cmp_kv":
                    cmp_kv()
                elif job == "dil_scores":
                    dil_scores(n)
                elif job == "dil_turn":
                    dil_turn(n)
                elif job == "dil_out":
                    dil_out(n)
                elif job == "cmp_scores":
                    cmp_scores()
                elif job == "cmp_turn":
                    cmp_turn()
                elif job == "scores":
                    scores(n)
                elif job == "turn":
                    turn(n)
                elif job == "out":
                    out_(n)

            for f in range(KC):
                u = U_UP + f // 2
                if f % 2 == 0:
                    pe.wait_ge(hi_done, u + 1)
                    pe.wait_ge(lo_done, u + 1)
                if f >= 2:
                    pe.wait_ge(m_sum, f - 1)
                w = [slot_view(r, u, 6, 256) for r in (whi, wlo)]
                for k, (lo, hi) in ((1, (4, 6)), (0, (0, 4))):
                    if f == 0 and k:
                        pe.wait_ge(y_lo, 2)
                    for c in range(lo, hi):
                        if f == 0 and c == 3:
                            pe.wait_ge(y_lo, 3)
                        ins = split_product(ps[2 * (f % 2) + k][:], [v[:, c, P * (f % 2):P * (f % 2) + P] for v in w],
                                            (yhi[:, c, :], ylo[:, c, :]), c == lo, c == hi - 1)
                ins.then_inc(ab_ready, 1)

            def to_tokens(act_pairs, w_pairs, tiles, first, last, done, between=None):
                for t in tiles:
                    for half in range(2):
                        for k in range(2):
                            ins = split_product(
                                ps[2 * t + half][:], [v[:, k, P * t:P * t + P] for v in act_pairs],
                                [v[:, k, 512 * half:512 * half + 512] for v in w_pairs],
                                first and k == 0, last and k == 1)
                        if last:
                            ins.then_inc(done, 1)
                    if between and t:
                        between(t - 1)
                return ins

            def w_out_unit(c, tiles, between=None):
                return to_tokens([v[:, 2 * c:2 * c + 2, :] for v in (mhi, mlo)],
                                 [slot_view(r, U_WO + c, 2, D) for r in (whi, wlo)], tiles, c == 0, c == 3,
                                 wo_ready, between)

            def turn_x2(t):
                for half in range(2):
                    pe.wait_ge(x2_sum, 2 * t + half + 1)
                    turn_rows(x2[:, t, :], t, half, 2 * t + half, h_turned)

            for c in range(2):
                pe.wait_ge(m_hi, 2 * c + 2)
                pe.wait_ge(m_lo, 2 * c + 2)
                pe.wait_ge(hi_done, U_WO + c + 1)
                pe.wait_ge(lo_done, U_WO + c + 1)
                w_out_unit(c, (2, 3))
            pe.wait_ge(m_sum, KC)
            for c in range(2):
                w_out_unit(c, (0, 1)).then_inc(w_used, 1)
            for c in range(2, 4):
                pe.wait_ge(m_hi, 2 * c + 2)
                pe.wait_ge(m_lo, 2 * c + 2)
                pe.wait_ge(hi_done, U_WO + c + 1)
                pe.wait_ge(lo_done, U_WO + c + 1)
                ins = w_out_unit(c, range(TT), turn_x2 if c == 3 else None)
                if c == 2:
                    ins.then_inc(w_used, 1)
            turn_x2(TT - 1)
            pe.wait_ge(h_lo, 2 * TT - 1)

            pe.sem_inc(gu_ready, 1)
            with pe.Fori(0, FT // 2) as i:
                for s in range(2):
                    pe.wait_ge(hi_done, i * 2 + (U_IN + s + 1))
                    pe.wait_ge(lo_done, i * 2 + (U_IN + s + 1))
                    pe.wait_ge(gu_free, i * 2 + (s + 1))
                    for half in range(2):
                        for k in range(KC):
                            if s == 0 and half == 0 and k == 4:
                                pe.wait_ge(h_lo, 2 * TT)
                            w = [slot_view(r, s, KC, 256)[:, k, P * half:P * half + P] for r in (whi, wlo)]
                            ins = split_product(ps[2 * s + half][:], w, (hhi[:, k, :], hlo[:, k, :]), k == 0, k == KC - 1)
                    ins.then_inc(gu_ready, 1)

            def ffn_out(s, tiles, first, last):
                return to_tokens((ahi[:, s], alo[:, s]), [slot_view(r, s, 2, D) for r in (whi, wlo)],
                                 tiles, first, last, fo_ready)

            pe.wait_ge(hi_done, U_OUT + 1)
            pe.wait_ge(lo_done, U_OUT + 1)
            pe.wait_ge(a_lo, 1)
            ffn_out(0, (2, 3), True, False)
            pe.wait_ge(gu_free, 24)
            ffn_out(0, (0, 1), True, False).then_inc(w_used, 1)
            pe.wait_ge(hi_done, U_OUT + 2)
            pe.wait_ge(lo_done, U_OUT + 2)
            pe.wait_ge(a_lo, 2)
            ffn_out(1, range(TT), False, False).then_inc(w_used, 1)
            with pe.Fori(1, FT // 4) as i:
                for s in range(2):
                    pe.wait_ge(hi_done, i * 2 + (U_OUT + s + 1))
                    pe.wait_ge(lo_done, i * 2 + (U_OUT + s + 1))
                    pe.wait_ge(a_lo, i * 2 + (s + 1))
                    ffn_out(s, range(TT), False, False).then_inc(w_used, 1)
            pe.wait_ge(hi_done, N_UNITS)
            pe.wait_ge(lo_done, N_UNITS)
            pe.wait_ge(a_lo, FT // 2)
            ffn_out(0, range(TT), False, True)


def dil_cuts(g):
    if g == 0:
        return [(B_OFF[i], B_OFF[i] + (256 if i else P)) for i in range(TT)]
    base = 896 + 512 * (g - 1)
    return [(base + P * i, base + P * i + P) for i in range(TT)]


BASE = 16512

_INS = ['x', 'norm_mix', 'w_in', 'pe_k', 'pe_v', 'w_ck1', 'w_ck2', 'w_cv1', 'w_cv2', 'w_up_nsa', 'w_up_dil',
        'w_out', 'norm_ffn', 'w_ffn_in', 'w_ffn_out', 'norm_final']


def kernel(**inputs):
    import numpy as _np
    import concourse.bacc as _bacc
    from concourse import mybir as _mybir
    from concourse.bass_utils import run_bass_kernel_spmd as _run

    nc = _bacc.Bacc("TRN2", target_bir_lowering=False, num_devices=1)
    arrays, args = {}, []
    for name in _INS:
        a = _np.ascontiguousarray(inputs[name])
        arrays[f"in_{name}_dram"] = a
        args.append(nc.dram_tensor(f"in_{name}_dram", a.shape, _mybir.dt.from_np(a.dtype), kind="ExternalInput").ap())
    args.append(nc.dram_tensor("out_0_dram", (1, S, D), F32, kind="ExternalOutput").ap())
    args.append([[nc.dram_tensor(f"scratch_{half}_{k}", (S, 4 if k < 2 else 2), F32, kind="Internal").ap()
                  for k in range(4)] for half in range(2)]
                + [[nc.dram_tensor(f"scratch_r{k}", (S,), F32, kind="Internal").ap() for k in range(2)]])
    trunk(nc, *args)
    r = _run(nc, [arrays], core_ids=[0])
    return r.results[0]["out_0_dram"]
```

```python
from contextlib import ExitStack

import concourse.bass as bass
from concourse import mybir

F32 = mybir.dt.float32
F32R = mybir.dt.float32r
I32 = mybir.dt.int32
ALU = mybir.AluOpType
ACT = mybir.ActivationFunctionType
AX = mybir.AxisListType

P = 128
D = 1024
S = 512
KC = D // P
TT = S // P
HD = 64
NH = 8
NG = 3
DIL = (1, 4, 16)
FF = 2816
FT = FF // P
CMP = 32
PP = 16
CH = 256
EPS = 1e-6
NEG = -1e30
TINY = 1e-30
QSCALE = HD ** -0.5

SLOPE = [2.0 ** (-8.0 * k / 20) for k in range(1, 21)]
SLOPE_DIL = [SLOPE[0:4], SLOPE[4:8], SLOPE[16:20]]
SLOPE_NSA = SLOPE[8:16]

C_Q, C_KC, C_KS, C_VS, C_KW, C_VW = 0, 512, 768, 896, 1024, 1152
C_QB, C_GM = 1304, 3608
VA_N = 280

U_CMP, U_QB, U_KB, U_VB, U_QA, U_KA, U_VA, U_GM, U_UP, U_WO, U_IN, U_OUT = 0, 1, 4, 7, 10, 12, 13, 14, 22, 26, 30, 52
N_UNITS = U_OUT + FT // 2
SLOT = KC * VA_N

TILES = [(u, a) for u in range(U_UP) for a in range(4 if u in (7, 8, 9, 13) else 2)]
FIRST_TILE = {u: TILES.index((u, 0)) for u in range(U_UP)}
LAST_TILE = {u: max(n for n, t in enumerate(TILES) if t[0] == u) for u in range(U_UP)}

Q_OFF = [0, 128, 384, 768]
S_PLACE = [(1, 384), (2, 0), (1, 0), (0, 0)]
K_OFF = [0, 512, 1024, 896]
K_PLACE = [(3, 0), (4, 0), (5, 0), (4, 384)]
T_CUTS = [(0, 512), (512, 1024), (1024, 1280)]
B_OFF = [0, 128, 384, 640]
B_PLACE = [(1, 256), (0, 0), (0, 256), (1, 0)]


LOOP_TILES = 10


def schedule():
    jobs = [("tile", n) for n in range(FIRST_TILE[U_QB + 2] + 1)]
    jobs += [("cmp_hidden", 0), ("tile", FIRST_TILE[U_QB + 2] + 1), ("tile", FIRST_TILE[U_KB]), ("cmp_kv", 0)]
    jobs += [("tile", n) for n in range(FIRST_TILE[U_KB] + 1, FIRST_TILE[U_QA])]
    tile = iter(range(FIRST_TILE[U_QA], len(TILES)))
    for m in range(6):
        jobs += [("dil_scores", m), ("tile", next(tile))]
    jobs += [("tile", next(tile)), ("tile", next(tile)), ("dil_merge", 0), ("tile", next(tile)), ("tile", next(tile))]
    for m in range(6):
        jobs.append(("dil_turn", m))
        if m:
            jobs.append(("dil_out", m - 1))
        jobs.append(("dil_scores", 6 + m))
    jobs += [("dil_out", 5), ("dil_merge", 1), ("cmp_scores", 0), ("tile", next(tile)), ("dil_turn", 6),
             ("cmp_scale", 0), ("tile", next(tile)), ("dil_turn", 7), ("dil_out", 6), ("cmp_turn", 0)]
    for m in range(8, 12):
        jobs += [("dil_turn", m), ("dil_out", m - 1)]
    jobs += [("dil_out", 11), ("split_k", 0), ("split_q", 0), ("split_k", 1), ("tile", next(tile))]
    filled = 0
    for n in range(2 * NH):
        jobs.append(("scores", n))
        if n > 1:
            jobs.append(("out", n - 2))
        if n:
            jobs.append(("turn", n - 1))
        if n % 2 == 0 and n < 2 * NH - 2:
            jobs.append(("split_q", n // 2 + 1))
        if n in (6, 7):
            jobs.append(("split_k", n - 4))
        if n in (0, 1, 8, 9):
            jobs.append(("split_v", n if n < 2 else n - 6))
        if filled < -(-LOOP_TILES * (n + 1) // (2 * NH)):
            filled += 1
            jobs.append(("tile", next(tile)))
    jobs += [("tile", next(tile)), ("out", 14), ("turn", 15), ("tile", next(tile)), ("out", 15), ("tile", next(tile))]
    return jobs


SCHEDULE = schedule()
NSA_FROM = SCHEDULE.index(("scores", 0))
TILE_BANK = {}
for _at, (_job, _n) in enumerate(SCHEDULE):
    if _job in ("tile", "tile_begin") and _n not in TILE_BANK:
        TILE_BANK[_n] = 4 + _n if _n < 2 else 7 if _at > NSA_FROM else 6 + _n % 2


def by_act(n):
    return U_VB <= TILES[n][0] < U_QA or TILES[n][0] == U_VA


def evac_count(n):
    return sum(by_act(v) == by_act(n) for v in range(LAST_TILE[U_CMP] + 1, n + 1))


TILE_BANK[len(TILES) - 1] = 2


def unit_parts(u):
    if u == U_CMP:
        return 1, KC * 256
    if u == U_VA:
        return 2, KC * VA_N
    if U_QA <= u < U_KA:
        return 4, KC * 256
    if U_UP <= u < U_WO:
        return 3, 6 * 256
    return 2, KC * 256


def raw_count(u):
    return 16 * sum(unit_parts(v)[0] for v in range(u % 2, u + 1, 2))


def trunk(nc, x, norm_mix, w_in, pe_k, pe_v, w_ck1, w_ck2, w_cv1, w_cv2, w_up_nsa, w_up_dil,
          w_out, norm_ffn, w_ffn_in, w_ffn_out, norm_final, out, scratch):
    with ExitStack() as ctx:
        def sem(name):
            return ctx.enter_context(nc.semaphore(name))

        def at(name, shape, offset, dt=F32):
            return nc.alloc_sbuf_tensor_at(name, [P, *shape], dt, offset=offset)

        A = BASE
        E = A + 32768
        Fo = E + 26624
        B = Fo + 10240
        C = B + 6 * 4 * SLOT
        Dd = C + 16384
        G = Dd + 36864
        H = G + 4 * 4400
        nhi, nlo = (at(f"n_{k}", [KC, S], A + o, F32R) for k, o in (("hi", 0), ("lo", 16384)))
        raw = [at(f"w_raw{i}", [SLOT], B + 4 * SLOT * i) for i in range(2)]
        whi = [at(f"w_hi{i}", [SLOT], B + 4 * SLOT * (2 + i), F32R) for i in range(2)]
        wlo = [at(f"w_lo{i}", [SLOT], B + 4 * SLOT * (4 + i), F32R) for i in range(2)]
        qa = at("qa", [4, S], C)
        ka = at("ka", [2, S], C + 8192)
        va = at("va", [TT, 256], C + 12288)
        qb = at("qb", [6, S], Dd)
        kb = at("kb", [6, S], Dd + 12288)
        vb = at("vb", [NG, TT, 256], Dd + 24576)
        gm = at("gm", [16, S], Dd)
        wck = [at("wck_k", [PP, CH], C), at("wck_v", [PP, CH], Dd + 12288)]
        xs = at("xs", [TT, D], E)
        xsq = at("xsq", [2, D], E + 16384)
        blk = [at(f"blk_{k}", [PP, 2, CMP], E + 4096 * i) for i, k in enumerate("kv")]
        dp = at("dil_p", [2, 1920], E)
        dbias = at("dil_bias", [4, 512], E + 15360)
        nbias = at("nsa_bias", [2, S], H + 14464)
        qst = at("q_stack", [2, S], E + 8192, F32R)
        kst = at("k_stack", [2, 2, S], E, F32R)
        vst = [at(f"v_stack{b}", [TT, 192], o, F32R)
               for b, o in enumerate((Dd + 32768, G + 11264))]
        ytmp = at("y_tmp", [S], E + 24576)
        pthi, ptlo = (at(f"probs_t_{k}", [1280], Fo + o, F32R) for k, o in (("hi", 0), ("lo", 5120)))
        sp = at("probs", [2, 1280], E + 14336)
        cbias = at("cmp_bias", [TT, NH, CMP], H + 4096)
        yhi, ylo = (at(f"y_{k}", [6, S], E + o, F32R) for k, o in (("hi", 0), ("lo", 12288)))
        pt = at("probs_t", [2, 1280], Fo)
        ident = at("ident", [P], G)
        dist = at("dist", [S], G + 512, I32)
        cmask = at("cmask", [S], G + 2560)
        mask0 = at("mask0", [256], G + 4608)
        mask2 = at("mask2", [P], G + 5632)
        distc = at("distc", [TT, CMP], G + 6144, I32)
        maskc = at("maskc", [TT, CMP], G + 6656)
        pc_t = at("pc_t", [2, S], G + 7168)
        hs = at("hs", [4, 2 * CMP], G + 11264)
        kc = at("kc", [2 * CMP], G + 12288)
        vc = at("vc", [2, 2 * HD], G + 4608)
        w2k = at("w2k", [2, 2, HD], G + 13056)
        w2v = at("w2v", [2, HD], G + 14080)
        crows = at("crows", [P], G + 14592)
        cvec = at("cvec", [48], G + 15104)
        gate = at("gate", [TT, NH * 3], G + 15296)
        st = at("st", [4, 8], G + 15680)
        ust = at("ust", [2, 4, TT], G + 15808)
        cst = at("cst", [2, 32], G + 15936)
        dm = at("dm", [NG, TT, 4], G + 16192)
        dneg = at("dneg", [2, TT], G + 16384)
        tok = at("tok", [TT, 2, 4], G + 16416)
        dmx = at("dmx", [3, TT, 2], G + 16544)
        de = at("de", [NG, TT, 2], G + 16640)
        dz = at("dz", [NG, TT, 2], G + 16736)
        dw = at("dw", [NG, TT, 2], G + 16832)
        dwl = at("dwl", [2, TT, 2], G + 16928)
        umx = at("umx", [2, TT], G + 16992)
        rrow = at("rrow", [S], H + 12288)
        rcol = at("rcol", [TT], H + 14336)
        rhalf = at("rhalf", [2, TT], H + 14368)
        ctmp = at("cmp_tmp", [2, S], Fo)
        ya = at("ya", [4, S], H)
        yb = at("yb", [2, S], H + 8192)
        sc = at("cmp_p", [TT, NH, CMP], H)
        th = at("tanh_h", [4 * 2 * CMP], H + 4096)
        mhi, mlo = nhi, nlo
        x2 = at("x2", [TT, D], C)
        hhi, hlo = (at(f"h_{k}", [KC, S], Dd + o, F32R) for k, o in (("hi", 0), ("lo", 16384)))
        mt = at("merge_tmp", [2, 3, S], Fo - 2048)
        actt = at("act_t", [FT, S], A)
        ahi, alo = (at(f"a_{k}", [2, 2, S], A + 45056 + o, F32R) for k, o in (("hi", 0), ("lo", 8192)))
        tg = at("tanh_g", [2, S], A + 61440)
        tm = at("gate_mul", [2, S], A + 65536)
        gfin = at("gfin", [D], G + 512)
        sq = at("square", [D], H)
        gs = at("gate_scaled", [2, S], H + 4096)
        xg = at("xg", [TT, D], Dd)

        ps = [ctx.enter_context(nc.psum_tensor(f"bank{i}", [P, 512], F32)) for i in range(8)]

        x_in = [sem(f"x_in{i}") for i in range(TT)]
        rows_in, w2_in, gfin_in, x2_in = sem("rows_in"), sem("w2_in"), sem("gfin_in"), sem("x2_in")
        wck_in = [sem("wck_k_in"), sem("wck_v_in")]
        raw_full = [sem("raw_full0"), sem("raw_full1")]
        hi_done, lo_done, w_used = sem("hi_done"), sem("lo_done"), sem("w_used")
        pool_step, consts_ready = sem("pool_step"), sem("consts_ready")
        dve_step, act_step = sem("dve_step"), sem("act_step")
        rows_turned, cvec_ready = sem("rows_turned"), sem("cvec_ready")
        ss_ready, n_turned, n_hi, n_lo = (sem(k) for k in ("ss_ready", "n_turned", "n_hi", "n_lo"))
        first_raw, first_hi, first_lo = (sem(k) for k in ("first_raw", "first_hi", "first_lo"))
        r_ready, r_out, r_in = (sem(k) for k in ("r_ready", "r_out", "r_in"))
        tile_ready, tile_evac_act, tile_evac_dve = (sem(k) for k in ("tile_ready", "tile_evac_act", "tile_evac_dve"))
        gm_tanh = sem("gm_tanh")
        cmp_tile_ready, blk_ready, h_ready, h_tanh, hs_ready = (
            sem(k) for k in ("cmp_tile_ready", "blk_ready", "h_ready", "h_tanh", "hs_ready"))
        kv_ready, kv_evac = sem("kv_ready"), sem("kv_evac")
        ds_ready, ds_max, ds_exp, dstat_out, dstat_in, de_sub, de_exp, dw_ready, dw_out, dw_in = (
            sem(k) for k in ("ds_ready", "ds_max", "ds_exp", "dstat_out", "dstat_in", "de_sub", "de_exp",
                             "dw_ready", "dw_out", "dw_in"))
        dp_ready, dt_ready, dt_evac_act, dt_evac_dve, do_ready, do_evac = (
            sem(k) for k in ("dp_ready", "dt_ready", "dt_evac_act", "dt_evac_dve", "do_ready", "do_evac"))
        cs_ready, cs_added, cs_sub, cs_exp, cp_ready, ct_ready, ct_evac = (
            sem(k) for k in ("cs_ready", "cs_added", "cs_sub", "cs_exp", "cp_ready", "ct_ready", "ct_evac"))
        gate_tanh, gate_ready = sem("gate_tanh"), sem("gate_ready")
        s_ready, s_max, s_exp, p_ready, t_ready, t_hi, t_lo, o_ready, y_half, y_evac = (
            sem(k) for k in ("s_ready", "s_max", "s_exp", "p_ready", "t_ready", "t_hi", "t_lo",
                             "o_ready", "y_half", "y_evac"))
        q_hi, q_lo, k_hi, k_lo, v_hi, v_lo = (sem(k) for k in ("q_hi", "q_lo", "k_hi", "k_lo", "v_hi", "v_lo"))
        y_hi, y_lo = sem("y_hi"), sem("y_lo")
        ab_ready, m_sum, m_hi, m_lo = (sem(k) for k in ("ab_ready", "m_sum", "m_hi", "m_lo"))
        wo_ready, x2_sum, x2_ss, h_turned, h_hi, h_lo = (
            sem(k) for k in ("wo_ready", "x2_sum", "x2_ss", "h_turned", "h_hi", "h_lo"))
        gu_ready, g_scaled, gu_tanh, gt_mul, gu_free = (
            sem(k) for k in ("gu_ready", "g_scaled", "gu_tanh", "gt_mul", "gu_free"))
        a_hi, a_lo, fo_ready, x3_sum, x3_ss, fin_ready, out_done = (
            sem(k) for k in ("a_hi", "a_lo", "fo_ready", "x3_sum", "x3_ss", "fin_ready", "out_done"))

        def slot_view(ring, u, k, n):
            return ring[u % 2][:, 0:k * n].rearrange("p (k n) -> p k n", k=k)

        def unit_used(u):
            if u == U_CMP:
                return cmp_tile_ready, 2
            if u < U_UP:
                return tile_ready, LAST_TILE[u] - 1
            if u < U_WO:
                return ab_ready, 2 * (u - U_UP) + 2
            if u < U_IN - 1:
                return w_used, u - U_WO + 1
            return wo_ready, 2 * TT

        def rows_of(g):
            return slice(HD * g, HD * g + HD)

        def v_columns(b, g):
            return va[:, :, 128 * b + HD * g:128 * b + HD * g + HD]

        block = ctx.enter_context(nc.Block())

        @block.sync
        def _(sp_):
            w_in_v = w_in[0].rearrange("(k p) n -> p k n", p=P)

            def load(u):
                if u >= 2:
                    sp_.wait_ge(lo_done, u - 1)
                full = raw_full[u % 2]
                if u < U_UP:
                    dst = slot_view(raw, u, KC, VA_N if u == U_VA else 256)
                    if U_QA <= u < U_KA:
                        cuts = [(128 * h + HD * t, 128 * h + HD * t + HD, C_Q + 256 * t + 128 * (u - U_QA) + HD * h)
                                for h in range(2) for t in range(2)]
                    elif u == U_KA:
                        cuts = [(0, 128, C_KS), (128, 256, C_KW)]
                    elif u == U_VA:
                        cuts = [(0, 128, C_VS), (128, VA_N, C_VW)]
                    else:
                        c = C_KC if u == U_CMP else C_QB + 256 * (u - U_QB) if u < U_QA else C_GM + 256 * (u - U_GM)
                        for k in (0, 4):
                            done = first_raw if u == U_CMP and k == 0 else full
                            sp_.dma_start(dst[:, k:k + 4, :], w_in_v[:, k:k + 4, c:c + 256]).then_inc(done, 16)
                        return
                    for a, b, c in cuts:
                        sp_.dma_start(dst[:, :, a:b], w_in_v[:, :, c:c + b - a]).then_inc(full, 16)
                elif u < U_WO:
                    cols = slice(256 * (u - U_UP), 256 * (u - U_UP) + 256)
                    dst = slot_view(raw, u, 6, 256)
                    for t in range(2):
                        src = w_up_nsa[0, 256 * t:256 * t + 256, cols].rearrange("(j d) n -> d j n", d=HD)
                        sp_.dma_start(dst[HD * t:HD * t + HD, 0:4, :], src).then_inc(full, 16)
                    src = w_up_dil[0, :, cols].rearrange("(t p) n -> p t n", p=P)
                    sp_.dma_start(dst[:, 4:6, :], src).then_inc(full, 16)
                else:
                    dst = slot_view(raw, u, 2, D)
                    for k in range(2):
                        r = 256 * (u - U_WO) + P * k if u < U_IN else 256 * (u - U_OUT) + P * k
                        w = w_out if u < U_IN else w_ffn_out
                        sp_.dma_start(dst[:, k, :], w[0, r:r + P, :]).then_inc(full, 16)

            for t in range(TT):
                sp_.dma_start(xs[:, t, :], x[0, P * t:P * t + P, :]).then_inc(x_in[t], 16)
            load(0)
            load(1)
            def dil_merge(half):
                sp_.wait_ge(ds_exp, 6 * half + 6)
                for g in (1, 2):
                    d = scratch[half][g - 1]
                    sp_.dma_start(d.rearrange("(p r) e -> p r e", r=4), dm[:, g, :, :]).then_inc(dstat_out, 16)
                sp_.wait_ge(dstat_out, 32 * half + 32)
                for g in (1, 2):
                    sp_.dma_start(tok[:, :, g - 1, :],
                                  scratch[half][g - 1].rearrange("(i p) e -> p i e", p=P)).then_inc(dstat_in, 16)
                sp_.wait_ge(dw_ready, half + 1)
                for g in (1, 2):
                    sp_.dma_start(scratch[half][g + 1].rearrange("(i p) e -> p i e", p=P),
                                  dw[:, g, :, :]).then_inc(dw_out, 16)
                sp_.wait_ge(dw_out, 32 * half + 32)
                for g in (1, 2):
                    sp_.dma_start(dwl[:, g - 1, :, :],
                                  scratch[half][g + 1].rearrange("(p r) e -> p r e", r=4)).then_inc(dw_in, 16)

            def spread_r(norm):
                sp_.wait_ge(r_ready, norm + 1)
                flat = scratch[2][norm]
                sp_.dma_start(flat.rearrange("(t p) -> p t", p=P), st[:, 3, 0:4],
                              allow_slow_non_contiguous=True).then_inc(r_out, 16)
                sp_.wait_ge(r_out, 16 * norm + 16)
                sp_.dma_start(rrow[:], flat.partition_broadcast(P)).then_inc(r_in, 16)
                if norm == 0:
                    sp_.dma_start(rcol[:], flat.rearrange("(p a) -> p a", a=TT)).then_inc(r_in, 16)

            load(2)
            spread_r(0)
            for kv, w in enumerate((w_ck1, w_cv1)):
                sp_.dma_start(wck[kv][:], w[0].rearrange("(a p) n -> p a n", p=P)).then_inc(wck_in[kv], 16)
            for r in range(2):
                sp_.dma_start(w2k[:, :, r, :], w_ck2[0].rearrange("(m p) d -> p m d", p=P)).then_inc(w2_in, 16)
            sp_.dma_start(w2v[:], w_cv2[0].rearrange("(m p) d -> p m d", p=P)).then_inc(w2_in, 16)

            for job, n in SCHEDULE:
                if job == "tile" and n and TILES[n][1] == 0:
                    load(TILES[n][0] + 2)
                elif job == "dil_merge":
                    dil_merge(n)
            sp_.wait_ge(o_ready, 16)
            for t in range(TT):
                sp_.dma_start(x2[:, t, :], x[0, P * t:P * t + P, :]).then_inc(x2_in, 16)
            sp_.dma_start(gfin[:], norm_final.partition_broadcast(P)).then_inc(gfin_in, 16)
            for u in range(U_UP + 2, U_IN):
                load(u)
            gt_v = w_ffn_in[0].rearrange("(k p) n -> p k n", p=P)

            def load_in(s, j, count):
                sp_.wait_ge(lo_done, count)
                dst = slot_view(raw, s, KC, 256)
                for half in range(2):
                    sp_.dma_start(dst[:, :, P * half:P * half + P],
                                  gt_v[:, :, bass.ds(j * P + FF * half, P)]).then_inc(raw_full[s], 16)

            for s in range(2):
                load_in(s, s, U_IN + s - 1)
            spread_r(1)
            with sp_.Fori(1, FT // 2) as i:
                for s in range(2):
                    load_in(s, i * 2 + s, i * 2 + (U_IN + s - 1))
            wo_v = w_ffn_out[0].rearrange("(u k p) n -> u p k n", p=P, k=2)
            with sp_.Fori(0, FT // 4) as i:
                for s in range(2):
                    sp_.wait_ge(lo_done, i * 2 + (U_OUT + s - 1))
                    dst = slot_view(raw, s, 2, D)
                    for k in range(2):
                        sp_.dma_start(dst[:, k, :], w_ffn_out[0, bass.ds((i * 2 + s) * 256 + P * k, P), :]
                                      ).then_inc(raw_full[s], 16)
            load(N_UNITS - 1)
            for t in range(TT):
                sp_.wait_ge(fin_ready, t + 1)
                sp_.dma_start(out[0, P * t:P * t + P, :], xg[:, t, :]).then_inc(out_done, 16)
            sp_.wait_ge(out_done, 16 * TT)

        @block.gpsimd
        def _(pool):
            steps = [0]

            def link(ins):
                steps[0] += 1
                ins.then_inc(pool_step, 1)
                pool.wait_ge(pool_step, steps[0])

            link(pool.memset(ident[:], 0.0))
            pool.affine_select(out=ident[:], in_=ident[:], compare_op=ALU.not_equal, fill=1.0, base=0,
                               pattern=[[-1, P]], channel_multiplier=1).then_inc(consts_ready, 1)
            pool.iota(dist[:], [[-1, S]], base=384, channel_multiplier=1).then_inc(consts_ready, 1)
            link(pool.memset(cmask[:], 0.0))
            link(pool.affine_select(out=cmask[:], in_=cmask[:], compare_op=ALU.is_ge, fill=NEG, base=384,
                                    pattern=[[-1, S]], channel_multiplier=1))
            pool.affine_select(out=mask0[:], in_=cmask[:, 256:512], compare_op=ALU.is_ge, fill=NEG, base=0,
                               pattern=[[1, 256]], channel_multiplier=-1).then_inc(consts_ready, 1)
            pool.iota(distc[:], [[P, TT], [-16, CMP]], base=-31, channel_multiplier=1).then_inc(consts_ready, 1)
            link(pool.memset(maskc[:], 0.0))
            pool.affine_select(out=maskc[:], in_=maskc[:], compare_op=ALU.is_ge, fill=NEG, base=-31,
                               pattern=[[P, TT], [-16, CMP]], channel_multiplier=1).then_inc(consts_ready, 1)

        @block.scalar
        def _(act):
            def split_hi(u):
                act.wait_ge(raw_full[u % 2], raw_count(u))
                if u >= 2:
                    act.wait_ge(*unit_used(u - 2))
                n = unit_parts(u)[1]
                act.copy(whi[u % 2][:, 0:n], raw[u % 2][:, 0:n]).then_inc(hi_done, 1)

            for row, src in ((0, norm_mix[0]), (8, norm_ffn[0])):
                act.dma_start(crows[row:row + 8, :], src.rearrange("(a b) -> a b", b=P)).then_inc(rows_in, 16)
            for row, src in ((16, pe_k), (32, pe_v)):
                act.dma_start(crows[row:row + PP, :],
                              src[0].rearrange("(a two) d -> a (two d)", two=2)).then_inc(rows_in, 16)
            for t in range(TT):
                act.wait_ge(x_in[t], 16)
                if t >= 2:
                    act.wait_ge(ss_ready, t - 1)
                act.activation(xsq[:, t % 2, :], xs[:, t, :], ACT.Square,
                               accum_out=st[:, 0, t:t + 1]).then_inc(ss_ready, 1)
            act.wait_ge(cvec_ready, 1)

            def turned_hi(k):
                act.wait_ge(n_turned, k + 1)
                act.activation(nhi[:, k, :], ps[k % 4][:], ACT.Copy, scale=cvec[:, k:k + 1]).then_inc(n_hi, 1)

            for k in range(2):
                turned_hi(k)
            act.wait_ge(first_raw, 16)
            act.copy(whi[0][:, 0:1024], raw[0][:, 0:1024]).then_inc(first_hi, 1)
            for k in range(2, 5):
                turned_hi(k)
            act.wait_ge(raw_full[0], 16)
            act.copy(whi[0][:, 1024:2048], raw[0][:, 1024:2048]).then_inc(hi_done, 1)
            for k in range(5, KC):
                turned_hi(k)

            def tile(n):
                u, a = TILES[n]
                if a == 0:
                    split_hi(u + 1)
                if u == U_CMP:
                    return
                b = ps[TILE_BANK[n]]
                if u >= U_GM:
                    act.wait_ge(tile_evac_dve, evac_count(n))
                    f = 2 * (u - U_GM) + a
                    act.activation(gm[:, f, :], gm[:, f, :], ACT.Tanh, scale=0.5).then_inc(gm_tanh, 1)
                elif by_act(n):
                    act.wait_ge(tile_ready, n - 1)
                    if u == U_VB:
                        act.wait_ge(r_in, 32)
                    if u == U_VA:
                        act.activation(gate[:, a, :], b[:, 256:VA_N], ACT.Tanh, scale=rhalf[:, 0, a:a + 1]).then_inc(gate_tanh, 1)
                    dst = va[:, a, :] if u == U_VA else vb[:, u - U_VB, a, :]
                    r_ = st[:, 3, a:a + 1] if u in (U_VB, U_VA) else rcol[:, a:a + 1]
                    act.activation(dst, b[:, 0:256], ACT.Copy, scale=r_).then_inc(tile_evac_act, 1)

            def compress():
                act.wait_ge(h_ready, 1)
                act.activation(th[:], ps[2][:, 0:256], ACT.Tanh, scale=0.5).then_inc(h_tanh, 1)

            def exps(buf, cuts, bias, sums, done):
                for i, (a, b) in enumerate(cuts):
                    ins = act.activation(buf[:, a:b], buf[:, a:b], ACT.Exp, bias=bias[i], accum_out=sums[i])
                ins.then_inc(done, 1)

            def nsa_exps(n):
                act.wait_ge(s_max, n + 1)
                exps(sp[:, n % 2, :], [(Q_OFF[i], Q_OFF[i] + P * (i + 1)) for i in range(TT)],
                     [ust[:, n % 2, 0, i:i + 1] for i in range(TT)],
                     [ust[:, n % 2, 1, i:i + 1] for i in range(TT)], s_exp)

            def y_split_hi(part):
                if part == 0:
                    act.wait_ge(do_evac, 12)
                    act.wait_ge(s_max, 16)
                    act.wait_ge(t_ready, 48)
                    act.copy(yhi[:, 4:6, :], yb[:]).then_inc(y_hi, 1)
                    act.wait_ge(y_evac, 7)
                    act.copy(yhi[:, 0:3, :], ya[:, 0:3, :]).then_inc(y_hi, 1)
                else:
                    act.wait_ge(y_evac, 8)
                    act.copy(yhi[:, 3, :], ya[:, 3, :]).then_inc(y_hi, 1)

            for job, n in SCHEDULE:
                if job == "tile":
                    tile(n)
                elif job == "cmp_hidden":
                    compress()
                elif job == "dil_scores":
                    m = n % 6
                    g, hh = m // 2, m % 2
                    act.wait_ge(ds_max, n + 1)
                    exps(dp[:, hh, :], dil_cuts(g), [dneg[:, n % 2, i:i + 1] for i in range(TT)],
                         [dm[:, g, i, 2 + hh:3 + hh] for i in range(TT)], ds_exp)
                elif job == "dil_merge":
                    act.wait_ge(de_sub, n + 1)
                    act.activation(de[:], de[:], ACT.Exp).then_inc(de_exp, 1)
                elif job == "dil_turn":
                    act.wait_ge(dt_ready, 2 * n + 1)
                    if n >= 2:
                        act.wait_ge(do_ready, n - 1)
                    act.copy(pt[:, n % 2, 0:512], ps[2][:]).then_inc(dt_evac_act, 1)
                elif job == "cmp_scores":
                    act.wait_ge(cs_sub, 1)
                    act.activation(sc[:], sc[:], ACT.Exp).then_inc(cs_exp, 1)
                elif job == "cmp_turn":
                    for g in range(2):
                        act.wait_ge(ct_ready, g + 1)
                        act.copy(pc_t[:, g, :], ps[g][:]).then_inc(ct_evac, 1)
                elif job == "split_q":
                    if n >= 2:
                        act.wait_ge(s_ready, 2 * n - 2)
                    else:
                        act.wait_ge(dt_ready, 24)
                    rows = rows_of(n // 4)
                    act.copy(qst[rows, n % 2, :], qa[rows, n % 4, :]).then_inc(q_hi, 1)
                elif job == "split_k":
                    if n >= 2:
                        act.wait_ge(s_ready, 5 + n)
                    else:
                        act.wait_ge(dt_ready, 24)
                    for half in range(2):
                        ins = act.copy(kst[rows_of(half), n % 2, 0, :], ka[rows_of(n // 2), n % 2, :])
                    ins.then_inc(k_hi, 1)
                elif job == "split_v":
                    if n >= 2:
                        act.wait_ge(o_ready, 5 + n)
                    else:
                        act.wait_ge(do_ready, 12)
                    act.copy(vst[n % 2][:, :, HD:2 * HD], v_columns(n % 2, n // 2)).then_inc(v_hi, 1)
                elif job == "scores" and n == 0:
                    nsa_exps(0)
                elif job == "turn":
                    if n:
                        act.wait_ge(o_ready, n)
                    else:
                        act.wait_ge(do_ready, 12)
                    for k, (a, b) in enumerate(T_CUTS):
                        act.wait_ge(t_ready, 3 * n + k + 1)
                        act.copy(pthi[:, a:b], ps[3 + k][:, 0:b - a]).then_inc(t_hi, 1)
                    if n < 15:
                        nsa_exps(n + 1)
                    else:
                        y_split_hi(0)
                elif job == "out" and n % 2:
                    act.wait_ge(o_ready, n + 1)
                    if n > 1:
                        act.wait_ge(y_evac, n // 2)
                    act.copy(ytmp[0:HD, :], ps[6][HD:P, :]).then_inc(y_half, 1)
                    if n == 15:
                        y_split_hi(1)

            for f in range(KC):
                if f % 2 == 0:
                    split_hi(U_UP + f // 2 + 1)
                act.wait_ge(m_sum, f + 1)
                act.copy(mhi[:, f, :], mt[:, f % 2, 2, :]).then_inc(m_hi, 1)
            for u in range(U_WO + 1, U_IN + 1):
                split_hi(u)

            for t in range(TT):
                for half in range(2):
                    act.wait_ge(h_turned, 2 * t + half + 1)
                    for k in range(4 * half, 4 * half + 4):
                        ins = act.activation(hhi[:, k, P * t:P * t + P], ps[2 * t + half][:, P * (k % 4):P * (k % 4) + P],
                                             ACT.Copy, scale=cvec[:, 8 + k:9 + k])
                    ins.then_inc(h_hi, 1)
                for v in ((), (0,), (), (1, 2, 3))[t]:
                    act.wait_ge(x2_sum, 2 * v + 2)
                    if v >= 1:
                        act.wait_ge(x2_ss, v)
                    act.activation(sq[:], x2[:, v, :], ACT.Square, accum_out=st[:, 1, v:v + 1]).then_inc(x2_ss, 1)

            def ffn_in(i, s):
                o = 1 - s
                act.wait_ge(raw_full[o], i * 32 + (raw_count(U_IN + 1 + s)))
                act.wait_ge(gu_ready, i * 2 + (s + 1))
                act.copy(whi[o][:, 0:2048], raw[o][:, 0:2048]).then_inc(hi_done, 1)

            def tanh_gate(i, s):
                act.wait_ge(g_scaled, i * 2 + (s + 1))
                act.wait_ge(gt_mul, i * 2 + (s + 1))
                act.activation(tg[:, s, :], gs[:, s, :], ACT.Tanh, scale=0.5).then_inc(gu_tanh, 1)

            with act.Fori(0, FT // 2 - 1) as i:
                for s in range(2):
                    ffn_in(i, s)
                    tanh_gate(i, s)
            for s in range(2):
                ffn_in(FT // 2 - 1, s)
                if s:
                    act.copy(ahi[:, 0, :, :], actt[:, 0:2, :]).then_inc(a_hi, 1)
                tanh_gate(FT // 2 - 1, s)

            act.wait_ge(gu_free, 24)
            with act.Fori(0, FT // 4) as i:
                for s in range(2):
                    o = 1 - s
                    act.wait_ge(w_used, i * 2 + (s + 3))
                    act.copy(ahi[:, o, :, :], actt[:, bass.ds(i * 4 + (2 * s + 2), 2), :]).then_inc(a_hi, 1)
                    act.wait_ge(raw_full[o], i * 32 + raw_count(U_OUT + 1 + s))
                    act.copy(whi[o][:, 0:2048], raw[o][:, 0:2048]).then_inc(hi_done, 1)
            for t in range(TT):
                act.wait_ge(x3_sum, 2 * t + 2)
                if t >= 1:
                    act.wait_ge(x3_ss, t)
                act.activation(sq[:], x2[:, t, :], ACT.Square, accum_out=st[:, 2, t:t + 1]).then_inc(x3_ss, 1)

        @block.vector
        def _(dve):
            steps = [0]

            def link(ins):
                steps[0] += 1
                ins.then_inc(dve_step, 1)
                dve.wait_ge(dve_step, steps[0])

            def split_lo(u):
                dve.wait_ge(hi_done, u + 1)
                n = unit_parts(u)[1]
                dve.tensor_tensor(wlo[u % 2][:, 0:n], raw[u % 2][:, 0:n], whi[u % 2][:, 0:n].bitcast(F32),
                                  ALU.subtract).then_inc(lo_done, 1)

            def rsqrt(ss, v, y, t1, done=None):
                link(dve.tensor_scalar(v, ss, 1.0 / D, EPS, ALU.mult, ALU.add))
                link(dve.tensor_scalar(t1.bitcast(I32), v.bitcast(I32), 1, None, ALU.logical_shift_right))
                link(dve.tensor_scalar(y.bitcast(I32), t1.bitcast(I32), -1.0, float(0x5F3759DF), ALU.mult, ALU.add))
                for step in range(3):
                    link(dve.tensor_tensor(t1, y, y, ALU.mult))
                    link(dve.scalar_tensor_tensor(out=t1, in0=t1, scalar=-0.5, in1=v, op0=ALU.mult, op1=ALU.mult))
                    last = dve.scalar_tensor_tensor(out=y, in0=t1, scalar=1.5, in1=y, op0=ALU.add, op1=ALU.mult)
                    if done and step == 2:
                        last.then_inc(done[0], 1)
                        dve.wait_ge(*done)
                    else:
                        link(last)

            dve.wait_ge(rows_turned, 1)
            dve.tensor_copy(cvec[:], ps[4][:, 0:48]).then_inc(cvec_ready, 1)
            dve.wait_ge(cvec_ready, 1)

            for k in range(KC):
                dve.wait_ge(n_hi, k + 1)
                dve.scalar_tensor_tensor(out=nlo[:, k, :], in0=ps[k % 4][:], scalar=cvec[:, k:k + 1],
                                         in1=nhi[:, k, :].bitcast(F32), op0=ALU.mult, op1=ALU.subtract).then_inc(n_lo, 1)
                if k in (1, 4):
                    c = slice(0, 1024) if k == 1 else slice(1024, 2048)
                    dve.wait_ge(first_hi if k == 1 else hi_done, 1)
                    dve.tensor_tensor(wlo[0][:, c], raw[0][:, c], whi[0][:, c].bitcast(F32),
                                      ALU.subtract).then_inc(first_lo if k == 1 else lo_done, 1)
            dve.wait_ge(ss_ready, TT)
            rsqrt(st[:, 0, 0:4], st[:, 0, 4:8], st[:, 3, 0:4], st[:, 3, 4:8], (r_ready, 1))
            dve.tensor_scalar(rhalf[:, 0, :], st[:, 3, 0:4], 0.5, None, ALU.mult)

            def turned_lo(lo, hi, bank, gain, t, half, done):
                for k in range(4 * half, 4 * half + 4):
                    ins = dve.scalar_tensor_tensor(
                        out=lo[:, k, P * t:P * t + P], in0=bank[:, P * (k % 4):P * (k % 4) + P],
                        scalar=gain[:, k:k + 1], in1=hi[:, k, P * t:P * t + P].bitcast(F32),
                        op0=ALU.mult, op1=ALU.subtract)
                ins.then_inc(done, 1)

            def dil_bias():
                dve.wait_ge(consts_ready, 5)
                m2i = mask2[:].bitcast(I32)
                link(dve.tensor_scalar(m2i, dist[:, 384:512], 3, None, ALU.bitwise_and))
                link(dve.tensor_scalar(mask2[:], m2i, 0.0, NEG, ALU.is_gt, ALU.mult))
                link(dve.tensor_tensor(mask2[:], mask2[:], cmask[:, 384:512], ALU.add))
                for h in range(4):
                    for g, (a, b, mask) in enumerate(((0, 256, mask0[:]), (256, 384, cmask[:, 384:512]), (384, 512, mask2[:]))):
                        ins = dve.scalar_tensor_tensor(
                            out=dbias[:, h, a:b], in0=dist[:, 512 - (b - a):512],
                            scalar=-SLOPE_DIL[g][h] * min(DIL[g], 4), in1=mask, op0=ALU.mult, op1=ALU.add)
                link(ins)

            def cmp_bias():
                for h in range(NH):
                    ins = dve.scalar_tensor_tensor(out=cbias[:, :, h, :], in0=distc[:], scalar=-SLOPE_NSA[h],
                                                   in1=maskc[:], op0=ALU.mult, op1=ALU.add)
                link(ins)

            def nsa_bias(h):
                link(dve.scalar_tensor_tensor(out=nbias[:, h % 2, :], in0=dist[:], scalar=-SLOPE_NSA[h],
                                              in1=cmask[:], op0=ALU.mult, op1=ALU.add))

            def tile(n):
                u, a = TILES[n]
                if a == 0:
                    split_lo(u + 1)
                if u == U_CMP:
                    if a == 0:
                        link(dve.memset(blk[0][:], 0.0))
                        link(dve.memset(blk[1][:], 0.0))
                    dve.wait_ge(cmp_tile_ready, a + 1)
                    if a == 0:
                        dve.wait_ge(r_in, 32)
                    link(dve.tensor_tensor(ctmp[:, a, :], ps[4 + a][:], rrow[:], ALU.mult))
                    for g in range(2):
                        for s in range(2):
                            rows = slice(HD * s, HD * s + HD)
                            src = ctmp[HD * g:HD * g + HD, a, :].rearrange("p (c q s) -> p s q c", q=8, s=2)[:, s]
                            code = cvec[rows, 16 + PP * a:32 + PP * a].rearrange("p (b q) -> p b q", q=8)
                            for b in range(2):
                                ins = dve.tensor_tensor(
                                    blk[a][rows, 8 * b:8 * b + 8, g, 0:31], src[:, :, b:b + 31],
                                    code[:, b, :].unsqueeze(2).to_broadcast([HD, 8, 31]), ALU.add)
                    ins.then_inc(blk_ready, 1)
                elif u == U_VA:
                    dve.wait_ge(gate_tanh, a + 1)
                    dve.tensor_scalar(gate[:, a, :], gate[:, a, :], 0.5, 0.5, ALU.mult, ALU.add).then_inc(gate_ready, 1)
                elif not by_act(n):
                    dve.wait_ge(tile_ready, n - 1)
                    src, row = ps[TILE_BANK[n]][:], rrow[:]
                    if u < U_VB:
                        g = (u - U_QB) % 3
                        dst = (qb if u < U_KB else kb)[:, 2 * g + a, :]
                        if g:
                            dst = dst.rearrange("p (r t) -> p r t", r=4)
                            src, row = (v.rearrange("p (t r) -> p r t", r=4) for v in (src, row))
                    elif u < U_KA:
                        dst = qa[:, 2 * (u - U_QA) + a, :]
                    elif u == U_KA:
                        dst = ka[:, a, :]
                    else:
                        dst = gm[:, 2 * (u - U_GM) + a, :]
                    scale = QSCALE if u < U_KB or U_QA <= u < U_KA else 1.0
                    dve.scalar_tensor_tensor(out=dst, in0=src, scalar=scale, in1=row,
                                             op0=ALU.mult, op1=ALU.mult).then_inc(tile_evac_dve, 1)

            def compress():
                dve.wait_ge(h_tanh, 1)
                dve.scalar_tensor_tensor(out=hs[:].rearrange("p a b -> p (a b)"), in0=th[:], scalar=1.0,
                                         in1=ps[2][:, 0:256], op0=ALU.add, op1=ALU.mult).then_inc(hs_ready, 1)

                dil_bias()
                cmp_bias()
                nsa_bias(0)
                nsa_bias(1)

            def cmp_kv():
                link(dve.memset(kc[:], 0.0))
                link(dve.memset(vc[:], 0.0))
                dve.wait_ge(kv_ready, 1)
                for g in range(2):
                    rows, cols = slice(HD * g, HD * g + HD), slice(CMP * g, CMP * g + CMP)
                    ins = dve.tensor_scalar(kc[rows, cols], ps[3][rows, cols], 0.5, None, ALU.mult)
                ins.then_inc(kv_evac, 1)
                dve.wait_ge(kv_ready, 2)
                dve.tensor_scalar(vc[:, :, 0:HD], ps[3][:, 128:256].rearrange("p (g d) -> p g d", g=2), 0.5, None, ALU.mult).then_inc(kv_evac, 1)

            def dil_scores(n):
                m = n % 6
                g, hh = m // 2, m % 2
                h = 2 * (n // 6) + hh
                dve.wait_ge(ds_ready, n + 1)
                if n >= 6:
                    dve.wait_ge(dt_ready, 2 * (n - 6) + 2)
                if n >= 2:
                    dve.wait_ge(ds_exp, n - 1)
                for i in range(TT):
                    a, b = dil_cuts(g)[i]
                    bank, c = B_PLACE[i] if g == 0 else (0, P * i)
                    base = (0, 256, 384)[g]
                    end = base + (256 if g == 0 else P)
                    ins = dve.tensor_tensor_reduce(
                        dp[:, hh, a:b], ps[bank][:, c:c + b - a], dbias[:, h, end - (b - a):end], 1.0, NEG,
                        ALU.add, ALU.max, dm[:, g, i, hh:hh + 1])
                link(ins)
                dve.tensor_scalar(dneg[:, n % 2, :], dm[:, g, :, hh], -1.0, None, ALU.mult).then_inc(ds_max, 1)

            def dil_merge(half):
                dve.wait_ge(ds_exp, 6 * half + 6)
                dve.wait_ge(dstat_in, 32 * half + 32)
                stat = [dm[:, 0, :, :], tok[:, :, 0, :], tok[:, :, 1, :]]
                link(dve.tensor_tensor(dmx[:, 0], stat[0][:, :, 0:2], stat[1][:, :, 0:2], ALU.max))
                link(dve.tensor_tensor(dmx[:, 1], stat[2][:, :, 0:2], dmx[:, 0], ALU.max))
                for g in range(NG):
                    ins = dve.tensor_tensor(de[:, g], stat[g][:, :, 0:2], dmx[:, 1], ALU.subtract)
                ins.then_inc(de_sub, 1)
                dve.wait_ge(de_exp, half + 1)
                for g in range(NG):
                    link(dve.tensor_tensor(dz[:, g], stat[g][:, :, 2:4], de[:, g], ALU.mult))
                link(dve.tensor_tensor(dmx[:, 0], dz[:, 0], dz[:, 1], ALU.add))
                link(dve.tensor_tensor(dmx[:, 1], dz[:, 2], dmx[:, 0], ALU.add))
                link(dve.reciprocal(dmx[:, 2], dmx[:, 1]))
                if half:
                    dve.wait_ge(dw_out, 32)
                for g in range(NG):
                    ins = dve.tensor_tensor(dw[:, g], de[:, g], dmx[:, 2], ALU.mult)
                ins.then_inc(dw_ready, 1)
                dil_scale(6 * half)
                dil_scale(6 * half + 1)

            def dil_scale(n):
                m = n % 6
                g, hh = m // 2, m % 2
                if m == 0:
                    dve.wait_ge(dw_ready, n // 6 + 1)
                if m == 2:
                    dve.wait_ge(dw_in, 32 * (n // 6) + 32)
                for i, (a, b) in enumerate(dil_cuts(g)):
                    w = dw[:, 0, i, hh:hh + 1] if g == 0 else dwl[:, g - 1, i, hh:hh + 1]
                    ins = dve.tensor_scalar(dp[:, hh, a:b], dp[:, hh, a:b], w, None, ALU.mult)
                ins.then_inc(dp_ready, 1)

            def dil_turn(n):
                if 1 <= n % 6 < 5:
                    dil_scale(n + 1)
                if (n % 6) // 2 == 0:
                    dve.wait_ge(dt_ready, 2 * n + 2)
                    if n >= 2:
                        dve.wait_ge(do_ready, n - 1)
                    dve.tensor_copy(pt[:, n % 2, 512:896], ps[3][:, 0:384]).then_inc(dt_evac_dve, 1)

            def dil_out(n):
                m = n % 6
                g, hh = m // 2, m % 2
                dve.wait_ge(do_ready, n + 1)
                rows = slice(HD * hh, HD * hh + HD)
                y = yb[rows, n // 6, :]
                o = ps[4 + n % 2][rows, :]
                if g == 0:
                    dve.tensor_copy(y, o).then_inc(do_evac, 1)
                else:
                    dve.wait_ge(do_evac, n - 1)
                    yv = y.rearrange("p (t r) -> p r t", r=4)
                    dve.tensor_tensor(yv, o.rearrange("p (r t) -> p r t", r=4), yv, ALU.add).then_inc(do_evac, 1)

            def cmp_scores():
                dve.wait_ge(cs_ready, 1)
                for i in range(TT):
                    dst, bias = (v[:, i].rearrange("p (g j) n -> p j g n", g=2) for v in (sc, cbias))
                    src = ps[i // 2][:, 256 * (i % 2):256 * (i % 2) + 256].rearrange("p (j g n) -> p j g n", j=4, g=2)
                    ins = dve.tensor_tensor(dst, src, bias, ALU.add)
                ins.then_inc(cs_added, 1)
                dve.wait_ge(cs_added, 1)
                s3 = sc[:].rearrange("p i h n -> p (i h) n")
                link(dve.tensor_reduce(cst[:, 0], s3, AX.X, ALU.max))
                link(dve.tensor_scalar(cst[:, 0], cst[:, 0], NEG / 10, None, ALU.max))
                dve.tensor_tensor(s3, s3, cst[:, 0].unsqueeze(2).to_broadcast([P, 32, CMP]),
                                  ALU.subtract).then_inc(cs_sub, 1)

            def cmp_scale():
                s3 = sc[:].rearrange("p i h n -> p (i h) n")
                dve.wait_ge(cs_exp, 1)
                link(dve.tensor_reduce(cst[:, 1], s3, AX.X, ALU.add))
                link(dve.tensor_scalar(cst[:, 1], cst[:, 1], TINY, None, ALU.max))
                link(dve.reciprocal(cst[:, 0], cst[:, 1]))
                dve.wait_ge(gate_ready, TT)
                c0 = cst[:, 0].rearrange("p (i h) -> p i h", i=TT)
                g0 = gate[:].rearrange("p i (h b) -> p i h b", b=3)
                link(dve.tensor_tensor(cst[:, 1].rearrange("p (i h) -> p i h", i=TT), c0, g0[:, :, :, 0], ALU.mult))
                dve.tensor_tensor(s3, s3, cst[:, 1].unsqueeze(2).to_broadcast([P, 32, CMP]),
                                  ALU.mult).then_inc(cp_ready, 1)

            def split_q(h):
                rows, others = rows_of(h // 4), rows_of(1 - h // 4)
                dve.wait_ge(q_hi, h + 1)
                dve.tensor_tensor(qst[others, h % 2, :], qa[rows, h % 4, :], qst[rows, h % 2, :].bitcast(F32),
                                  ALU.subtract).then_inc(q_lo, 1)

            def split_k(m):
                rows = rows_of(m // 2)
                dve.wait_ge(k_hi, m + 1)
                for half in range(2):
                    ins = dve.tensor_tensor(kst[rows_of(half), m % 2, 1, :], ka[rows, m % 2, :],
                                            kst[rows, m % 2, 0, :].bitcast(F32), ALU.subtract)
                ins.then_inc(k_lo, 1)

            def split_v(m):
                v = vst[m % 2]
                dve.wait_ge(v_hi, m + 1)
                if m < 2:
                    dve.tensor_tensor(v[:, :, 2 * HD:], ident[:, 0:HD].unsqueeze(1).to_broadcast([P, TT, HD]),
                                      ident[:, 0:HD].unsqueeze(1).to_broadcast([P, TT, HD]), ALU.subtract)
                dve.tensor_tensor(v[:, :, 0:HD], v_columns(m % 2, m // 2), v[:, :, HD:2 * HD].bitcast(F32),
                                  ALU.subtract).then_inc(v_lo, 1)

            def scores(n):
                dve.wait_ge(s_ready, n + 1)
                if n == 0:
                    dve.wait_ge(dt_ready, 24)
                if n >= 2:
                    dve.wait_ge(t_ready, 3 * (n - 1))
                for i in range(TT):
                    bank, c = S_PLACE[i]
                    w = P * (i + 1)
                    ins = dve.tensor_tensor_reduce(
                        sp[:, n % 2, Q_OFF[i]:Q_OFF[i] + w], ps[bank][:, c:c + w], nbias[:, n // 2 % 2, 384 - P * i:512],
                        1.0, NEG, ALU.add, ALU.max, umx[:, n % 2, i:i + 1])
                link(ins)
                dve.tensor_scalar(ust[:, n % 2, 0, :], umx[:, n % 2, :], -1.0, None, ALU.mult).then_inc(s_max, 1)

            def scale(n):
                h, b = n // 2, n % 2
                dve.wait_ge(s_exp, n + 1)
                link(dve.reciprocal(ust[:, n % 2, 2, :], ust[:, n % 2, 1, :]))
                link(dve.tensor_tensor(ust[:, n % 2, 3, :], ust[:, n % 2, 2, :], gate[:, :, 3 * h + 1 + b], ALU.mult))
                for i in range(TT):
                    q = sp[:, n % 2, Q_OFF[i]:Q_OFF[i] + P * (i + 1)]
                    ins = dve.tensor_scalar(q, q, ust[:, n % 2, 3, i:i + 1], None, ALU.mult)
                ins.then_inc(p_ready, 1)

            def turn(n):
                for k, (a, b) in enumerate(T_CUTS):
                    dve.wait_ge(t_hi, 3 * n + k + 1)
                    dve.tensor_tensor(ptlo[:, a:b], ps[3 + k][:, 0:b - a], pthi[:, a:b].bitcast(F32),
                                      ALU.subtract).then_inc(t_lo, 1)

            def head_out(h):
                dve.wait_ge(y_half, h + 1)
                dve.tensor_tensor(ya[rows_of(h // 4), h % 4, :], ps[6][0:HD, :], ytmp[0:HD, :], ALU.add).then_inc(y_evac, 1)

            def y_split_lo(part):
                for k in ((0, 1), (2,))[part]:
                    a, b, src = ((4, 6, yb[:]), (0, 3, ya[:, 0:3, :]), (3, 4, ya[:, 3:4, :]))[k]
                    dve.wait_ge(y_hi, k + 1)
                    dve.tensor_tensor(ylo[:, a:b, :], src, yhi[:, a:b, :].bitcast(F32), ALU.subtract).then_inc(y_lo, 1)

            for job, n in SCHEDULE:
                if job == "tile":
                    tile(n)
                elif job == "cmp_hidden":
                    compress()
                elif job == "cmp_kv":
                    cmp_kv()
                elif job == "dil_scores":
                    dil_scores(n)
                elif job == "dil_merge":
                    dil_merge(n)
                elif job == "dil_turn":
                    dil_turn(n)
                elif job == "dil_out":
                    dil_out(n)
                elif job == "cmp_scale":
                    cmp_scale()
                elif job == "cmp_scores":
                    cmp_scores()
                elif job == "scores":
                    scores(n)
                    if n == 0:
                        scale(0)
                elif job == "turn":
                    turn(n)
                    if n < 15:
                        scale(n + 1)
                    else:
                        y_split_lo(0)
                elif job == "out" and n % 2:
                    head_out(n // 2)
                    if n == 15:
                        y_split_lo(1)
                    elif n < 12:
                        nsa_bias(n // 2 + 2)
                elif job == "split_q":
                    split_q(n)
                elif job == "split_k":
                    split_k(n)
                elif job == "split_v":
                    split_v(n)

            for f in range(KC):
                if f % 2 == 0:
                    split_lo(U_UP + f // 2 + 1)
                dve.wait_ge(ab_ready, f + 1)
                if f == 0:
                    dve.wait_ge(gm_tanh, 2 * KC)
                if f >= 2:
                    dve.wait_ge(m_hi, f - 1)
                    dve.wait_ge(m_lo, f - 1)
                for k in range(2):
                    ins = dve.scalar_tensor_tensor(out=mt[:, f % 2, k, :], in0=gm[:, 8 * k + f, :], scalar=1.0,
                                                   in1=ps[2 * (f % 2) + k][:], op0=ALU.add, op1=ALU.mult)
                link(ins)
                dve.tensor_tensor(mt[:, f % 2, 2, :], mt[:, f % 2, 0, :], mt[:, f % 2, 1, :], ALU.add).then_inc(m_sum, 1)
                dve.wait_ge(m_hi, f + 1)
                dve.tensor_tensor(mlo[:, f, :], mt[:, f % 2, 2, :], mhi[:, f, :].bitcast(F32),
                                  ALU.subtract).then_inc(m_lo, 1)
            for u in range(U_WO + 1, U_IN + 1):
                split_lo(u)

            dve.sem_inc(gt_mul, 2)
            dve.sem_inc(gu_free, 2)
            dve.sem_inc(gu_tanh, 2)

            dve.wait_ge(x2_in, 16 * TT)

            def residual(t, factor, ready, done):
                for half in range(2):
                    dve.wait_ge(ready, 2 * t + half + 1)
                    q = x2[:, t, 512 * half:512 * half + 512]
                    dve.scalar_tensor_tensor(out=q, in0=ps[2 * t + half][:], scalar=factor, in1=q,
                                             op0=ALU.mult, op1=ALU.add).then_inc(done, 1)

            def h_low(t):
                for half in range(2):
                    dve.wait_ge(h_hi, 2 * t + half + 1)
                    turned_lo(hlo, hhi, ps[2 * t + half], cvec[:, 8:16], t, half, h_lo)

            for t in range(TT):
                residual(t, 0.5, wo_ready, x2_sum)
                if t:
                    h_low(t - 1)
            h_low(TT - 1)
            dve.wait_ge(x2_ss, TT)
            rsqrt(st[:, 1, 0:4], st[:, 1, 4:8], st[:, 3, 0:4], st[:, 3, 4:8], (r_ready, 2))
            link(dve.tensor_scalar(rhalf[:, 1, :], st[:, 3, 0:4], 0.5, None, ALU.mult))

            def ffn_in_lo(i, s):
                o = 1 - s
                dve.wait_ge(hi_done, i * 2 + (U_IN + 2 + s))
                dve.tensor_tensor(wlo[o][:, 0:2048], raw[o][:, 0:2048], whi[o][:, 0:2048].bitcast(F32),
                                  ALU.subtract).then_inc(lo_done, 1)

            def ffn_in_act(i, s):
                dve.wait_ge(gu_ready, i * 2 + (s + 2))
                dve.wait_ge(gu_tanh, i * 2 + (s + 1))
                dve.tensor_tensor(gs[:, s, :], ps[2 * s][:], rrow[:], ALU.mult).then_inc(g_scaled, 1)
                dve.wait_ge(gu_tanh, i * 2 + (s + 3))
                dve.wait_ge(gu_free, i * 2 + (s + 1))
                dve.scalar_tensor_tensor(out=tm[:, s, :], in0=tg[:, s, :], scalar=1.0, in1=gs[:, s, :],
                                         op0=ALU.add, op1=ALU.mult).then_inc(gt_mul, 1)
                dve.wait_ge(gt_mul, i * 2 + (s + 3))
                dve.tensor_tensor(actt[:, i * 2 + s, :], ps[2 * s + 1][:], tm[:, s, :],
                                  ALU.mult).then_inc(gu_free, 1)

            dve.wait_ge(r_in, 48)
            with dve.Fori(0, FT // 2 - 1) as i:
                for s in range(2):
                    ffn_in_lo(i, s)
                    ffn_in_act(i, s)
            for s in range(2):
                ffn_in_lo(FT // 2 - 1, s)
                if s:
                    dve.wait_ge(a_hi, 1)
                    dve.tensor_tensor(alo[:, 0, :, :], actt[:, 0:2, :], ahi[:, 0, :, :].bitcast(F32),
                                      ALU.subtract).then_inc(a_lo, 1)
                ffn_in_act(FT // 2 - 1, s)

            dve.wait_ge(gu_free, 24)
            with dve.Fori(0, FT // 4) as i:
                for s in range(2):
                    o = 1 - s
                    dve.wait_ge(a_hi, i * 2 + (s + 2))
                    dve.tensor_tensor(alo[:, o, :, :], actt[:, bass.ds(i * 4 + (2 * s + 2), 2), :],
                                      ahi[:, o, :, :].bitcast(F32), ALU.subtract).then_inc(a_lo, 1)
                    dve.wait_ge(hi_done, i * 2 + (U_OUT + 2 + s))
                    dve.tensor_tensor(wlo[o][:, 0:2048], raw[o][:, 0:2048], whi[o][:, 0:2048].bitcast(F32),
                                      ALU.subtract).then_inc(lo_done, 1)
            dve.wait_ge(gfin_in, 16)
            dve.wait_ge(h_lo, 2 * TT)
            for pair in range(2):
                for t in (2 * pair, 2 * pair + 1):
                    residual(t, rhalf[:, 1, t:t + 1], fo_ready, x3_sum)
                    dve.wait_ge(x3_sum, 2 * t + 2)
                    ins = dve.tensor_tensor(xg[:, t, :], x2[:, t, :], gfin[:], ALU.mult)
                link(ins)
                dve.wait_ge(x3_ss, 2 * pair + 2)
                a = 2 * pair
                rsqrt(st[:, 2, a:a + 2], st[:, 2, 4 + a:6 + a], st[:, 3, a:a + 2], st[:, 3, 4 + a:6 + a])
                for t in (a, a + 1):
                    dve.tensor_scalar(xg[:, t, :], xg[:, t, :], st[:, 3, t:t + 1], None, ALU.mult).then_inc(fin_ready, 1)

        @block.tensor
        def _(pe):
            def split_product(dst, w, x_, start, stop):
                pe.matmul(dst, w[0], x_[0], start=start, stop=False)
                pe.matmul(dst, w[0], x_[1], start=False, stop=False)
                return pe.matmul(dst, w[1], x_[0], start=False, stop=stop)

            def turn_rows(src, t, half, banks, done):
                for k in range(4 * half, 4 * half + 4):
                    ins = pe.transpose(ps[banks][:, P * (k % 4):P * (k % 4) + P], src[:, P * k:P * k + P], ident[:])
                ins.then_inc(done, 1)

            pe.wait_ge(rows_in, 64)
            pe.wait_ge(consts_ready, 1)
            pe.transpose(ps[4][:, 0:48], crows[0:48, :], ident[0:48, 0:48]).then_inc(rows_turned, 1)

            def turn_x(k):
                if k >= 4:
                    pe.wait_ge(n_lo, k - 3)
                for t in range(TT):
                    if k == 0:
                        pe.wait_ge(x_in[t], 16)
                    ins = pe.transpose(ps[k % 4][:, P * t:P * t + P], xs[:, t, P * k:P * k + P], ident[:])
                ins.then_inc(n_turned, 1)

            for k in range(4):
                turn_x(k)
            pe.wait_ge(cvec_ready, 1)

            def token_cols(n_, k, g, a):
                if g == 0:
                    return n_[:, k, P * a:P * a + P]
                return n_[:, k, :].rearrange("p (t r) -> p r t", r=4)[:, a]

            def tile_evacuated(n):
                pe.wait_ge(tile_evac_act if by_act(n) else tile_evac_dve, evac_count(n))

            def tile(n, chunks):
                u, a = TILES[n]
                if a == 0 and n:
                    pe.wait_ge(hi_done, u + 1)
                    pe.wait_ge(lo_done, u + 1)
                bank = TILE_BANK[n]
                before = [v for v in range(2, n) if TILE_BANK[v] == bank]
                if before:
                    tile_evacuated(before[-1])
                natural = U_VB <= u < U_QA or u == U_VA
                w = [slot_view(r, u, KC, VA_N if u == U_VA else 256) for r in (whi, wlo)]
                for k in chunks:
                    if n == 0:
                        if k % 4 == 0:
                            pe.wait_ge(lo_done if k else first_lo, 1)
                        pe.wait_ge(n_lo, k + 1)
                        if k < 4:
                            turn_x(k + 4)
                    if natural:
                        g = 0 if u == U_VA else u - U_VB
                        cols = VA_N if u == U_VA else 256
                        ins = split_product(ps[bank][:, 0:cols], [token_cols(v, k, g, a) for v in (nhi, nlo)],
                                            [v[:, k, :] for v in w], k == 0, k == KC - 1)
                    else:
                        wk = [v[:, k, P * a:P * a + P] for v in w]
                        ins = split_product(ps[bank][:], wk, (nhi[:, k, :], nlo[:, k, :]), k == 0, k == KC - 1)
                if k == KC - 1:
                    ins.then_inc(cmp_tile_ready if u == U_CMP else tile_ready, 1)

            def compress():
                for kv in range(2):
                    pe.wait_ge(wck_in[kv], 16)
                    pe.wait_ge(blk_ready, kv + 1)
                    for m in range(2):
                        o = ps[2][:, 64 * (2 * kv + m):64 * (2 * kv + m) + 64]
                        for q in range(PP):
                            ins = pe.matmul(o, wck[kv][:, q, P * m:P * m + P], blk[kv][:, q].rearrange("p g c -> p (g c)"),
                                            start=(q == 0), stop=(q == PP - 1))
                ins.then_inc(h_ready, 1)

            def cmp_kv():
                pe.wait_ge(w2_in, 48)
                pe.wait_ge(hs_ready, 1)
                for m in range(2):
                    ins = pe.matmul(ps[3][:, 0:64], w2k[:, m].rearrange("p r d -> p (r d)"), hs[:, m, :],
                                    start=(m == 0), stop=(m == 1))
                ins.then_inc(kv_ready, 1)
                pe.wait_ge(kv_evac, 1)
                for g in range(2):
                    for r in range(4):
                        for m in range(2):
                            ins = pe.matmul(ps[3][32 * r:32 * r + 32, 128 + HD * g:128 + HD * g + HD],
                                            hs[:, 2 + m, CMP * g:CMP * g + CMP], w2v[:, m, :],
                                            start=(m == 0), stop=(m == 1))
                ins.then_inc(kv_ready, 1)

            def dil_scores(n):
                m = n % 6
                g, hh, t = m // 2, m % 2, n // 6
                tile_evacuated(LAST_TILE[U_KB + 2])
                if n:
                    pe.wait_ge(ds_max, n)
                rows = slice(HD * hh, HD * hh + HD)
                q, k = qb[rows, 2 * g + t, :], kb[rows, 2 * g + t, :]
                for i in range(TT):
                    lo = P * (i - 1) if g == 0 and i else P * i
                    bank, c = B_PLACE[i] if g == 0 else (0, P * i)
                    ins = pe.matmul(ps[bank][:, c:c + P * (i + 1) - lo], q[:, P * i:P * i + P], k[:, lo:P * (i + 1)],
                                    start=True, stop=True)
                ins.then_inc(ds_ready, 1)

            def dil_evacuated(n):
                pe.wait_ge(dt_evac_act, n + 1)
                pe.wait_ge(dt_evac_dve, sum(v % 6 < 2 for v in range(n + 1)))

            def dil_turn(n):
                m = n % 6
                g, hh = m // 2, m % 2
                pe.wait_ge(dp_ready, n + 1)
                if n:
                    dil_evacuated(n - 1)
                if n == 0:
                    pe.wait_ge(kv_evac, 2)
                p_ = dp[:, hh, :]
                if g == 0:
                    for j in range(TT):
                        bank, c = ps[2 + j // 2], 256 * (j % 2)
                        a = B_OFF[j] + (P if j else 0)
                        ins = pe.transpose(bank[:, c:c + P], p_[:, a:a + P], ident[:])
                        if j < 3:
                            ins = pe.transpose(bank[:, c + P:c + 256], p_[:, B_OFF[j + 1]:B_OFF[j + 1] + P], ident[:])
                        if j % 2:
                            ins.then_inc(dt_ready, 1)
                else:
                    a = dil_cuts(g)[0][0]
                    for i in range(TT):
                        ins = pe.transpose(ps[2][:, P * i:P * i + P], p_[:, a + P * i:a + P * i + P], ident[:])
                    ins.then_inc(dt_ready, 2)

            def dil_out(n):
                m = n % 6
                g, hh, t = m // 2, m % 2, n // 6
                dil_evacuated(n)
                if n >= 2:
                    pe.wait_ge(do_evac, n - 1)
                rows = slice(HD * hh, HD * hh + HD)
                h = 2 * t + hh
                o = ps[4 + n % 2]
                for i in range(TT):
                    q = slice(P * i, P * i + P)
                    if g == 0 and i:
                        pe.matmul(o[rows, q], vb[:, g, i - 1, HD * h:HD * h + HD], pt[:, n % 2, 256 * (i - 1) + P:256 * i], start=True, stop=False)
                    c = 256 * i if g == 0 else P * i
                    ins = pe.matmul(o[rows, q], vb[:, g, i, HD * h:HD * h + HD], pt[:, n % 2, c:c + P], start=not (g == 0 and i), stop=True)
                ins.then_inc(do_ready, 1)

            def cmp_scores():
                pe.wait_ge(ds_max, 12)
                for i in range(TT):
                    for j in range(4):
                        c = 256 * (i % 2) + 2 * CMP * j
                        ins = pe.matmul(ps[i // 2][:, c:c + 2 * CMP], qa[:, j, P * i:P * i + P], kc[:],
                                        start=True, stop=True)
                ins.then_inc(cs_ready, 1)

            def cmp_turn():
                pe.wait_ge(cp_ready, 1)
                for g in range(2):
                    for i in range(TT):
                        ins = pe.transpose(ps[g][:, P * i:P * i + P],
                                           sc[:, i, 4 * g:4 * g + 4, :].rearrange("p h n -> p (h n)"), ident[:])
                    ins.then_inc(ct_ready, 1)

            def scores(n):
                h, b = n // 2, n % 2
                if n == 0:
                    pe.wait_ge(ct_evac, 2)
                else:
                    pe.wait_ge(s_max, n)
                pe.wait_ge(q_lo, h + 1)
                pe.wait_ge(k_lo, 2 * (h // 4) + b + 1)
                for i in range(TT):
                    bank, c = S_PLACE[i]
                    w = P * (i + 1)
                    for k in range(2):
                        ins = pe.matmul(ps[bank][:, c:c + w], qst[:, h % 2, P * i:P * i + P], kst[:, b, k, 0:w],
                                        start=(k == 0), stop=(k == 1))
                ins.then_inc(s_ready, 1)

            def turn(n):
                pe.wait_ge(p_ready, n + 1)
                if n:
                    pe.wait_ge(t_lo, 3 * n)
                else:
                    pe.wait_ge(do_evac, 12)
                for js in ((0,), (1, 3), (2,)):
                    for j in js:
                        bank, c = K_PLACE[j]
                        for i in range(j, TT):
                            a = Q_OFF[i] + P * j
                            ins = pe.transpose(ps[bank][:, c + P * (i - j):c + P * (i - j) + P],
                                               sp[:, n % 2, a:a + P], ident[:])
                    ins.then_inc(t_ready, 1)

            def out_(n):
                h, b = n // 2, n % 2
                g, j = h // 4, h % 4
                o = ps[6]
                if b == 0:
                    if n == 0:
                        tile_evacuated(max(v for v in TILE_BANK if TILE_BANK[v] == 6))
                    else:
                        pe.wait_ge(y_evac, h)
                    pe.matmul(o[:], vc[CMP * j:CMP * j + CMP, g, :], pc_t[CMP * j:CMP * j + CMP, g, :],
                              start=True, stop=False)
                pe.wait_ge(t_lo, 3 * n + 3)
                pe.wait_ge(v_lo, 2 * g + b + 1)
                for k in range(TT):
                    for c, p_ in ((0, pthi), (HD, ptlo)):
                        ins = pe.matmul(o[:, P * k:], vst[b][:, k, c:c + P], p_[:, K_OFF[k]:K_OFF[k] + P * (TT - k)],
                                        start=False, stop=(b == 1 and k == TT - 1 and c == HD))
                ins.then_inc(o_ready, 1)

            begun = None
            for job, n in SCHEDULE:
                if job == "tile_begin":
                    tile(n, range(KC // 2))
                    begun = n
                elif job == "tile":
                    tile(n, range(KC // 2 if n == begun else 0, KC))
                elif job == "cmp_hidden":
                    compress()
                elif job == "cmp_kv":
                    cmp_kv()
                elif job == "dil_scores":
                    dil_scores(n)
                elif job == "dil_turn":
                    dil_turn(n)
                elif job == "dil_out":
                    dil_out(n)
                elif job == "cmp_scores":
                    cmp_scores()
                elif job == "cmp_turn":
                    cmp_turn()
                elif job == "scores":
                    scores(n)
                elif job == "turn":
                    turn(n)
                elif job == "out":
                    out_(n)

            for f in range(KC):
                u = U_UP + f // 2
                if f == 1:
                    tile_evacuated(len(TILES) - 1)
                if f % 2 == 0:
                    pe.wait_ge(hi_done, u + 1)
                    pe.wait_ge(lo_done, u + 1)
                if f >= 2:
                    pe.wait_ge(m_sum, f - 1)
                w = [slot_view(r, u, 6, 256) for r in (whi, wlo)]
                for k, (lo, hi) in ((1, (4, 6)), (0, (0, 4))):
                    if f == 0 and k:
                        pe.wait_ge(y_lo, 2)
                    for c in range(lo, hi):
                        if f == 0 and c == 3:
                            pe.wait_ge(y_lo, 3)
                        ins = split_product(ps[2 * (f % 2) + k][:], [v[:, c, P * (f % 2):P * (f % 2) + P] for v in w],
                                            (yhi[:, c, :], ylo[:, c, :]), c == lo, c == hi - 1)
                ins.then_inc(ab_ready, 1)

            def to_tokens(act_pairs, w_pairs, tiles, first, last, done, between=None):
                for t in tiles:
                    for half in range(2):
                        for k in range(2):
                            ins = split_product(
                                ps[2 * t + half][:], [v[:, k, P * t:P * t + P] for v in act_pairs],
                                [v[:, k, 512 * half:512 * half + 512] for v in w_pairs],
                                first and k == 0, last and k == 1)
                        if last:
                            ins.then_inc(done, 1)
                    if between and t:
                        between(t - 1)
                return ins

            def w_out_unit(c, tiles, between=None):
                return to_tokens([v[:, 2 * c:2 * c + 2, :] for v in (mhi, mlo)],
                                 [slot_view(r, U_WO + c, 2, D) for r in (whi, wlo)], tiles, c == 0, c == 3,
                                 wo_ready, between)

            def turn_x2(t):
                for half in range(2):
                    pe.wait_ge(x2_sum, 2 * t + half + 1)
                    turn_rows(x2[:, t, :], t, half, 2 * t + half, h_turned)

            for c in range(4):
                pe.wait_ge(m_hi, 2 * c + 2)
                pe.wait_ge(m_lo, 2 * c + 2)
                pe.wait_ge(hi_done, U_WO + c + 1)
                pe.wait_ge(lo_done, U_WO + c + 1)
                if c == 0:
                    w_out_unit(c, (2, 3))
                    pe.wait_ge(m_sum, KC)
                ins = w_out_unit(c, range(2 if c == 0 else TT), turn_x2 if c == 3 else None)
                if c < 3:
                    ins.then_inc(w_used, 1)
            turn_x2(TT - 1)
            pe.wait_ge(h_lo, 2 * TT - 1)

            pe.sem_inc(gu_ready, 1)
            with pe.Fori(0, FT // 2) as i:
                for s in range(2):
                    pe.wait_ge(hi_done, i * 2 + (U_IN + s + 1))
                    pe.wait_ge(lo_done, i * 2 + (U_IN + s + 1))
                    pe.wait_ge(gu_free, i * 2 + (s + 1))
                    for half in range(2):
                        for k in range(KC):
                            if s == 0 and half == 0 and k == 4:
                                pe.wait_ge(h_lo, 2 * TT)
                            w = [slot_view(r, s, KC, 256)[:, k, P * half:P * half + P] for r in (whi, wlo)]
                            ins = split_product(ps[2 * s + half][:], w, (hhi[:, k, :], hlo[:, k, :]), k == 0, k == KC - 1)
                    ins.then_inc(gu_ready, 1)

            def ffn_out(s, tiles, first, last):
                return to_tokens((ahi[:, s], alo[:, s]), [slot_view(r, s, 2, D) for r in (whi, wlo)],
                                 tiles, first, last, fo_ready)

            pe.wait_ge(hi_done, U_OUT + 1)
            pe.wait_ge(lo_done, U_OUT + 1)
            pe.wait_ge(a_lo, 1)
            ffn_out(0, (2, 3), True, False)
            pe.wait_ge(gu_free, 24)
            ffn_out(0, (0, 1), True, False).then_inc(w_used, 1)
            pe.wait_ge(hi_done, U_OUT + 2)
            pe.wait_ge(lo_done, U_OUT + 2)
            pe.wait_ge(a_lo, 2)
            ffn_out(1, range(TT), False, False).then_inc(w_used, 1)
            with pe.Fori(1, FT // 4) as i:
                for s in range(2):
                    pe.wait_ge(hi_done, i * 2 + (U_OUT + s + 1))
                    pe.wait_ge(lo_done, i * 2 + (U_OUT + s + 1))
                    pe.wait_ge(a_lo, i * 2 + (s + 1))
                    ffn_out(s, range(TT), False, False).then_inc(w_used, 1)
            pe.wait_ge(hi_done, N_UNITS)
            pe.wait_ge(lo_done, N_UNITS)
            pe.wait_ge(a_lo, FT // 2)
            ffn_out(0, range(TT), False, True)


def dil_cuts(g):
    if g == 0:
        return [(B_OFF[i], B_OFF[i] + (256 if i else P)) for i in range(TT)]
    base = 896 + 512 * (g - 1)
    return [(base + P * i, base + P * i + P) for i in range(TT)]


BASE = 16512

_INS = ['x', 'norm_mix', 'w_in', 'pe_k', 'pe_v', 'w_ck1', 'w_ck2', 'w_cv1', 'w_cv2', 'w_up_nsa', 'w_up_dil',
        'w_out', 'norm_ffn', 'w_ffn_in', 'w_ffn_out', 'norm_final']


def kernel(**inputs):
    import numpy as _np
    import concourse.bacc as _bacc
    from concourse import mybir as _mybir
    from concourse.bass_utils import run_bass_kernel_spmd as _run

    nc = _bacc.Bacc("TRN2", target_bir_lowering=False, num_devices=1)
    arrays, args = {}, []
    for name in _INS:
        a = _np.ascontiguousarray(inputs[name])
        arrays[f"in_{name}_dram"] = a
        args.append(nc.dram_tensor(f"in_{name}_dram", a.shape, _mybir.dt.from_np(a.dtype), kind="ExternalInput").ap())
    args.append(nc.dram_tensor("out_0_dram", (1, S, D), F32, kind="ExternalOutput").ap())
    args.append([[nc.dram_tensor(f"scratch_{half}_{k}", (S, 4 if k < 2 else 2), F32, kind="Internal").ap()
                  for k in range(4)] for half in range(2)]
                + [[nc.dram_tensor(f"scratch_r{k}", (S,), F32, kind="Internal").ap() for k in range(2)]])
    trunk(nc, *args)
    r = _run(nc, [arrays], core_ids=[0])
    return r.results[0]["out_0_dram"]
```
